# Optimizing a Trainium2 kernel written in Bass

```python
import jax
import jax.numpy as jnp
from jax import lax
import numpy as np

D_MODEL = 1024
BATCH = 1
SEQ = 1024
DEPTH = 1
DEC_BATCH = 8
DEC_SEQ = 8
PAST_LEN = 8192
PAGE_SIZE = 128

CONV_K = 3
CONV_CH = D_MODEL // 2
GLA_HEADS = 4
GLA_DK = D_MODEL // 8
GLA_DV = D_MODEL // 4
GLA_QK = GLA_HEADS * GLA_DK
GLA_V = GLA_HEADS * GLA_DV
GLA_LOWRANK = 16
GLA_TAU = 16.0
GLA_CHUNK = 64
CM_GROUPS = 4
CM_CHUNK = 128
CM_GCH = D_MODEL // 8
CM_CH = CM_GROUPS * CM_GCH
SPLIT_SIZES = (CONV_CH, CONV_CH, CONV_CH,
               GLA_QK, GLA_QK, GLA_V, GLA_V, GLA_LOWRANK,
               CM_CH, CM_CH,
               D_MODEL, D_MODEL, D_MODEL)
D_IN = sum(SPLIT_SIZES)
MOE_GROUPS = 8
EXPERTS_PER_GROUP = 8
N_EXPERTS = MOE_GROUPS * EXPERTS_PER_GROUP
TOP_K = 2
D_EXPERT = D_MODEL // 4
MOE_BLOCK = 128
EPS = 1e-6

kernel_name = 'hybrid_conv_gla_chunkmlp_hiermoe_step'

def rmsnorm(x, g):
    xf = x.astype(jnp.float32)
    y = xf * lax.rsqrt(jnp.mean(xf * xf, axis=-1, keepdims=True) + EPS)
    return (y * g.astype(jnp.float32)).astype(x.dtype)

def split_cols(z):
    outs = []
    off = 0
    for n in SPLIT_SIZES:
        outs.append(z[..., off:off + n])
        off += n
    return outs

def gla_chunked(q, k, v, log_a, s0):
    bn, t, h, _ = q.shape
    dv = v.shape[-1]
    c = min(GLA_CHUNK, t)
    n = -(-t // c)
    tp = n * c

    def blocks(a):
        a = jnp.pad(a.astype(jnp.float32), ((0, 0), (0, tp - t), (0, 0), (0, 0)))
        return a.reshape(bn, n, c, h, a.shape[-1]).transpose(1, 0, 3, 2, 4)

    qc, kc, vc, ac = blocks(q), blocks(k), blocks(v), blocks(log_a)
    b = jnp.cumsum(ac, axis=3)
    b_last = b[:, :, :, -1:, :]
    q_t = qc * jnp.exp(b)
    k_t = kc * jnp.exp(-b)
    k_end = kc * jnp.exp(b_last - b)
    mask = jnp.tril(jnp.ones((c, c), dtype=bool))
    att = jnp.where(mask, jnp.einsum('nbhcd,nbhsd->nbhcs', q_t, k_t), 0.0)
    o_intra = jnp.einsum('nbhcs,nbhse->nbhce', att, vc)

    def step(s, inp):
        q_i, k_i, v_i, d_i = inp
        o_i = jnp.einsum('bhcd,bhde->bhce', q_i, s)
        s = d_i[:, :, 0, :, None] * s + jnp.einsum('bhcd,bhce->bhde', k_i, v_i)
        return s, o_i

    s_fin, o_inter = lax.scan(step, s0.astype(jnp.float32), (q_t, k_end, vc, jnp.exp(b_last)))
    o = (o_intra + o_inter).transpose(1, 0, 3, 2, 4).reshape(bn, tp, h, dv)[:, :t]
    return o.astype(q.dtype), s_fin.astype(s0.dtype)

def chunk_spatial_mix(vg, ws, bias):
    bn, t, g, ch = vg.shape
    n = -(-t // CM_CHUNK)
    tp = n * CM_CHUNK
    vp = jnp.pad(vg, ((0, 0), (0, tp - t), (0, 0), (0, 0))).reshape(bn, n, CM_CHUNK, g, ch)
    s = jnp.einsum('gts,bnsgc->bntgc', jnp.tril(ws), vp) + jnp.swapaxes(bias, 0, 1)[None, None, :, :, None]
    return s.reshape(bn, tp, g, ch)[:, :t]

def hier_moe(x2d, rg_w, rg_b, re_w, re_b, w1, w3, w2):
    t = x2d.shape[0]
    lg = (x2d @ rg_w + rg_b).astype(jnp.float32)
    _, grp = lax.top_k(lg, 1)
    p_grp = jnp.take_along_axis(jax.nn.softmax(lg, axis=-1), grp, axis=-1)
    le = (x2d @ re_w + re_b).astype(jnp.float32).reshape(t, MOE_GROUPS, EXPERTS_PER_GROUP)
    le_g = jnp.take_along_axis(le, grp[:, :, None], axis=1)[:, 0]
    top_v, top_i = lax.top_k(le_g, TOP_K)
    gate = p_grp * jax.nn.softmax(top_v, axis=-1)
    eidx = grp * EXPERTS_PER_GROUP + top_i

    n_slots = t * TOP_K
    e_flat = eidx.reshape(n_slots).astype(jnp.int32)
    tok_flat = jnp.repeat(jnp.arange(t, dtype=jnp.int32), TOP_K)
    g_flat = gate.reshape(n_slots)
    order = jnp.argsort(e_flat)
    e_s, tok_s, g_s = e_flat[order], tok_flat[order], g_flat[order]
    counts = jnp.zeros((N_EXPERTS,), jnp.int32).at[e_flat].add(1)
    start = jnp.cumsum(counts) - counts
    blocks_per = (counts + MOE_BLOCK - 1) // MOE_BLOCK
    blk_end = jnp.cumsum(blocks_per)
    blk_start = blk_end - blocks_per
    dest = blk_start[e_s] * MOE_BLOCK + (jnp.arange(n_slots, dtype=jnp.int32) - start[e_s])
    nb = -(-n_slots // MOE_BLOCK) + N_EXPERTS
    tok_buf = jnp.full((nb * MOE_BLOCK,), t, jnp.int32).at[dest].set(tok_s)
    g_buf = jnp.zeros((nb * MOE_BLOCK,), jnp.float32).at[dest].set(g_s)
    block_expert = jnp.minimum(jnp.searchsorted(blk_end, jnp.arange(nb), side='right'), N_EXPERTS - 1)
    x_pad = jnp.concatenate([x2d, jnp.zeros((1, x2d.shape[1]), x2d.dtype)], axis=0)
    xb = x_pad[tok_buf].reshape(nb, MOE_BLOCK, x2d.shape[1])

    def expert_block(args):
        xblk, e = args
        hdn = jax.nn.silu(xblk @ w1[e]) * (xblk @ w3[e])
        return hdn @ w2[e]

    yb = lax.map(expert_block, (xb, block_expert)).reshape(nb * MOE_BLOCK, x2d.shape[1])
    y = jax.ops.segment_sum(yb * g_buf[:, None].astype(yb.dtype), tok_buf, num_segments=t + 1)
    return y[:t]

def trunk_layer(x, conv_buf, gla_state, p):
    (n1, w_in, conv_w, gla_a2, gla_a_b, gla_ng, cm_ng, cm_ws, cm_b, proj_a, proj_b, proj_c,
     w_out, n2, rg_w, rg_b, re_w, re_b, w1, w3, w2) = p
    bn, t, _ = x.shape
    xn = rmsnorm(x, n1)
    h, cg, bg, q, k, v, r, a_lr, u, vv, ga, gb, gc = split_cols(xn @ w_in)

    cin = cg * h
    cp = jnp.concatenate([conv_buf.astype(cin.dtype), cin], axis=1)
    conv = sum(cp[:, i:i + t] * conv_w[i] for i in range(CONV_K))
    y_a = (bg * conv) @ proj_a
    new_conv = cp[:, t:]

    qh = q.reshape(bn, t, GLA_HEADS, GLA_DK) * (GLA_DK ** -0.5)
    kh = k.reshape(bn, t, GLA_HEADS, GLA_DK)
    vh = v.reshape(bn, t, GLA_HEADS, GLA_DV)
    log_a = jax.nn.log_sigmoid((a_lr @ gla_a2 + gla_a_b).astype(jnp.float32)) / GLA_TAU
    o, new_gla = gla_chunked(qh, kh, vh, log_a.reshape(bn, t, GLA_HEADS, GLA_DK), gla_state)
    o = rmsnorm(o, gla_ng) * jax.nn.silu(r.reshape(bn, t, GLA_HEADS, GLA_DV))
    y_b = o.reshape(bn, t, GLA_V) @ proj_b

    ug = jax.nn.gelu(u)
    vg = rmsnorm(jax.nn.gelu(vv).reshape(bn, t, CM_GROUPS, CM_GCH), cm_ng)
    s = chunk_spatial_mix(vg, cm_ws, cm_b)
    y_c = (ug * s.reshape(bn, t, CM_CH)) @ proj_c

    mix = jax.nn.sigmoid(ga) * y_a + jax.nn.sigmoid(gb) * y_b + jax.nn.sigmoid(gc) * y_c
    x = x + mix @ w_out

    xn2 = rmsnorm(x, n2)
    x = x + hier_moe(xn2.reshape(bn * t, D_MODEL), rg_w, rg_b, re_w, re_b, w1, w3, w2).reshape(bn, t, D_MODEL)
    return x, new_conv, new_gla, vg.reshape(bn, t, CM_CH)

def setup_inputs(seed: int = 0) -> dict:
    key = jax.random.key(seed)
    ks = jax.random.split(key, 32)

    def nrm(k, shape, s):
        return jax.random.normal(k, shape, jnp.float32) * s

    return {
        'x_prompt': nrm(ks[0], (BATCH, SEQ, D_MODEL), 1.0),
        'x_sample': nrm(ks[1], (DEC_BATCH, DEC_SEQ, D_MODEL), 1.0),
        'state_conv': nrm(ks[2], (DEPTH, DEC_BATCH, CONV_K - 1, CONV_CH), 1.0),
        'state_gla': nrm(ks[3], (DEPTH, DEC_BATCH, GLA_HEADS, GLA_DK, GLA_DV), 1.0),
        'norm1_g': 1.0 + nrm(ks[4], (DEPTH, D_MODEL), 0.02),
        'w_in': nrm(ks[5], (DEPTH, D_MODEL, D_IN), D_MODEL ** -0.5),
        'conv_w': nrm(ks[6], (DEPTH, CONV_K, CONV_CH), CONV_K ** -0.5),
        'gla_a2': nrm(ks[7], (DEPTH, GLA_LOWRANK, GLA_QK), GLA_LOWRANK ** -0.5),
        'gla_a_b': nrm(ks[8], (DEPTH, GLA_QK), 0.1),
        'gla_norm_g': 1.0 + nrm(ks[9], (DEPTH, GLA_DV), 0.02),
        'cm_norm_g': 1.0 + nrm(ks[10], (DEPTH, CM_GROUPS, CM_GCH), 0.02),
        'cm_ws': nrm(ks[11], (DEPTH, CM_GROUPS, CM_CHUNK, CM_CHUNK), CM_CHUNK ** -0.5),
        'cm_b': nrm(ks[12], (DEPTH, CM_GROUPS, CM_CHUNK), 0.1),
        'proj_a': nrm(ks[13], (DEPTH, CONV_CH, D_MODEL), CONV_CH ** -0.5),
        'proj_b': nrm(ks[14], (DEPTH, GLA_V, D_MODEL), GLA_V ** -0.5),
        'proj_c': nrm(ks[15], (DEPTH, CM_CH, D_MODEL), CM_CH ** -0.5),
        'w_out': nrm(ks[16], (DEPTH, D_MODEL, D_MODEL), D_MODEL ** -0.5),
        'norm2_g': 1.0 + nrm(ks[17], (DEPTH, D_MODEL), 0.02),
        'router_group_w': nrm(ks[18], (DEPTH, D_MODEL, MOE_GROUPS), D_MODEL ** -0.5),
        'router_group_b': nrm(ks[19], (DEPTH, MOE_GROUPS), 0.01),
        'router_expert_w': nrm(ks[20], (DEPTH, D_MODEL, N_EXPERTS), D_MODEL ** -0.5),
        'router_expert_b': nrm(ks[21], (DEPTH, N_EXPERTS), 0.01),
        'exp_w1': nrm(ks[22], (DEPTH, N_EXPERTS, D_MODEL, D_EXPERT), D_MODEL ** -0.5),
        'exp_w3': nrm(ks[23], (DEPTH, N_EXPERTS, D_MODEL, D_EXPERT), D_MODEL ** -0.5),
        'exp_w2': nrm(ks[24], (DEPTH, N_EXPERTS, D_EXPERT, D_MODEL), D_EXPERT ** -0.5),
        'final_norm_g': 1.0 + nrm(ks[25], (D_MODEL,), 0.02),
    }

def reference(x_prompt, x_sample, state_conv, state_gla, norm1_g, w_in, conv_w, gla_a2, gla_a_b,
              gla_norm_g, cm_norm_g, cm_ws, cm_b, proj_a, proj_b, proj_c, w_out, norm2_g,
              router_group_w, router_group_b, router_expert_w, router_expert_b,
              exp_w1, exp_w3, exp_w2, final_norm_g):
    params = (norm1_g, w_in, conv_w, gla_a2, gla_a_b, gla_norm_g, cm_norm_g, cm_ws, cm_b,
              proj_a, proj_b, proj_c, w_out, norm2_g, router_group_w, router_group_b,
              router_expert_w, router_expert_b, exp_w1, exp_w3, exp_w2)
    xp = x_prompt
    xs = x_sample
    bp = x_prompt.shape[0]
    conv_p, gla_p, conv_s, gla_s, cmv_s = [], [], [], [], []
    for l in range(DEPTH):
        p = tuple(a[l] for a in params)
        xp, cb, gs, _ = trunk_layer(
            xp,
            jnp.zeros((bp, CONV_K - 1, CONV_CH), xp.dtype),
            jnp.zeros((bp, GLA_HEADS, GLA_DK, GLA_DV), xp.dtype),
            p)
        conv_p.append(cb)
        gla_p.append(gs)
        xs, cb, gs, vrows = trunk_layer(xs, state_conv[l], state_gla[l], p)
        conv_s.append(cb)
        gla_s.append(gs)
        cmv_s.append(vrows)
    y_prompt = rmsnorm(xp, final_norm_g)
    y_sample = rmsnorm(xs, final_norm_g)
    return (y_prompt, y_sample, jnp.stack(conv_p), jnp.stack(gla_p), jnp.stack(conv_s), jnp.stack(gla_s), jnp.stack(cmv_s))


_drawn_inputs = setup_inputs


def setup_inputs(seed=0):
    import zlib

    import numpy as np

    out = dict(_drawn_inputs(seed))
    spreads = {}
    factors = {'gla_norm_g': 4.686,
     'cm_norm_g': 2.733,
     'norm2_g': 3.33,
     'router_group_b': 5.051,
     'router_expert_b': 7.101,
     'final_norm_g': 2.785}
    for name, (base, spread) in spreads.items():
        noise = np.random.default_rng([zlib.crc32(name.encode()), seed]).standard_normal(out[name].shape)
        drawn = base * np.exp(spread * noise) if base else spread * noise
        out[name] = jnp.asarray(drawn.astype(out[name].dtype))
    for name, factor in factors.items():
        out[name] = (out[name] * factor).astype(out[name].dtype)
    return out
```

```python
import concourse.bass as bass
from concourse import mybir
from contextlib import ExitStack

F32 = mybir.dt.float32
F32R = mybir.dt.float32r
I32 = mybir.dt.int32
ALU = mybir.AluOpType
ACT = mybir.ActivationFunctionType
AX = mybir.AxisListType

P = 128
D = 1024
KD = D // P
SEQ = 1024
DEC_B, DEC_T = 8, 8
NDEC = DEC_B * DEC_T
NTOK = SEQ + NDEC
NFULL = SEQ // P
NT = NFULL + 1
CONV_CH = 512
NCH = CONV_CH // P
HEADS, DK, DV = 4, 128, 256
CHUNK = 64
NCHUNK = SEQ // CHUNK
TAU = 16.0
LOWRANK = 16
GROUPS, EPG = 8, 8
NE = GROUPS * EPG
DE = 256
EPS = 1e-6
C_H, C_CG, C_BG, C_Q, C_K = 0, 512, 1024, 1536, 2048
C_V, C_R, C_A, C_U, C_VV, C_G = 2560, 3584, 4608, 4624, 5136, 5648
D_IN = 8720
CW = 256
TG = [(0, 384), (384, 384), (768, 320)]
NSLOT = 2 * NTOK
NOVF = (NSLOT - 1) // P
NBLK = NE + NOVF
NOWHERE = 1 << 20
EMPTY = 4 * NSLOT
KMAX = (NTOK + P - 1) // P


def rows_of(tile):
    return P if tile < NFULL else NDEC


def trunk(nc, x_prompt, x_sample, state_conv, state_gla, norm1_g, w_in, conv_w, gla_a2, gla_a_b,
          gla_norm_g, cm_norm_g, cm_ws, cm_b, proj_a, proj_b, proj_c, w_out, norm2_g,
          rg_w, rg_b, re_w, re_b, exp_w1, exp_w3, exp_w2, final_g,
          y_prompt, y_sample, conv_p, gla_p, conv_s, gla_s, chunk_v):
    def dram(name, shape, dt=F32):
        return nc.dram_tensor(name, shape, dt, kind="Internal").ap()

    feat = dram("feat", (D_IN, NTOK))
    tokd = dram("tokd", (NTOK, 2560))
    zT = dram("zT", (16 * P, NTOK))
    mixT = dram("mixT", (D, NTOK))
    x2d = dram("x2d", (NTOK, D))
    xn2d = dram("xn2d", (NTOK, D))
    table = dram("slot_table", (P * NBLK, 1), I32)
    y2d = dram("y2d", (NSLOT, D))

    xp = x_prompt[0]
    xs = x_sample.rearrange("a b n -> (a b) n")
    w_in_v = w_in[0].rearrange("(k p) c -> p k c", p=P)
    ctx = ExitStack()
    with ctx:
        def sem(name):
            return ctx.enter_context(nc.semaphore(name))

        def sem2(name):
            return [sem(f"{name}{i}") for i in range(2)]

        def sbuf(stack):
            return lambda name, shape, dt=F32: stack.enter_context(nc.sbuf_tensor(name, shape, dt))

        keep = sbuf(ctx)
        ident = keep("ident", [P, P])
        epsc = keep("epsc", [P, 1])
        yt = keep("yt", [P, NTOK])
        alr = yt[0:LOWRANK]
        gates = keep("gates", [P, NT, 2])
        lgt = keep("lgt", [P, NT, GROUPS + NE])
        sidx = keep("sidx", [P, NBLK], I32)
        tidx = keep("tidx", [P, NBLK], I32)
        eovf = keep("eovf", [1, NOVF + 1], I32)

        ph = ExitStack()
        sb = sbuf(ph)
        XH = sb("XH", [P, KD, NTOK], F32R)
        XL = sb("XL", [P, KD, NTOK], F32R)
        RAW = [sb(f"RAW{i}", [P, KD, CW]) for i in range(2)]
        WH = [sb(f"WH{i}", [P, KD, CW], F32R) for i in range(2)]
        WL = [sb(f"WL{i}", [P, KD, CW], F32R) for i in range(2)]
        OT = [sb(f"OT{i}", [P, NT, CW]) for i in range(2)]
        OF = [sb(f"OF{i}", [P, 2, NTOK]) for i in range(2)]
        g1b = sb("g1b", [P, D])
        X = [sb(f"X{i}", [P, D]) for i in range(2)]
        XN = [sb(f"XN{i}", [P, D]) for i in range(2)]
        ssq = [sb(f"ssq{i}", [P, 1]) for i in range(2)]
        rtt = [sb(f"rtt{i}", [P, 1]) for i in range(2)]
        rst = [sb(f"rst{i}", [P, 1]) for i in range(2)]
        junk = sb("junk", [P, D])
        ph.close()

        ph = ExitStack()
        sb = sbuf(ph)
        cH = sb("cH", [P, NTOK])
        cG = sb("cG", [P, NTOK])
        cB = sb("cB", [P, NTOK])
        cwt = sb("cwt", [P, 3])
        cpp = sb("cpp", [P, 2 + SEQ])
        cps = sb("cps", [P, DEC_B, 2 + DEC_T])
        cout = sb("cout", [P, NTOK])
        za = sb("za", [P, NTOK])
        vvt = sb("vvt", [P, NT, CONV_CH])
        vsq = sb("vsq", [P, NT, CONV_CH])
        vss = sb("vss", [P, NT * NCH])
        vrs = sb("vrs", [P, NT * NCH])
        cmg = sb("cmg", [P, CONV_CH])
        wsn = sb("wsn", [P, NCH, P])
        wsd = sb("wsd", [NDEC, NCH, NDEC])
        wsT = sb("wsT", [P, NCH, P])
        wsdT = sb("wsdT", [NDEC, NCH, NDEC])
        cmb = sb("cmb", [P, NCH, P])
        uT = sb("uT", [P, NTOK])
        zc = sb("zc", [P, NTOK])
        ph.close()
        ph = ExitStack()
        sb = sbuf(ph)
        a2h = sb("a2h", [LOWRANK, P])
        abh = sb("abh", [P, 1])
        qT = sb("qT", [P, NTOK])
        kT = sb("kT", [P, NTOK])
        vt = sb("vt", [P, NT, DV])
        rt = sb("rt", [P, NT, DV])
        rg = sb("rg", [P, DV])
        seg = sb("seg", [P, NTOK])
        zz = sb("zz", [P, NTOK])
        t1 = sb("t1", [P, NTOK])
        cs = sb("cs", [P, NTOK])
        eb = sb("eb", [P, NTOK])
        qt = sb("qt", [P, NTOK])
        kt = sb("kt", [P, NTOK])
        ke = sb("ke", [P, NTOK])
        qz = sb("qz", [P, DEC_B, NDEC])
        ket = [sb(f"ket{i}", [P, P]) for i in range(2)]
        kz = sb("kz", [NDEC, DEC_B, P])
        rmask = sb("rmask", [NDEC, DEC_B])
        attm = [sb(f"attm{i}", [P, P]) for i in range(2)]
        attd = sb("attd", [NDEC, NDEC])
        mp = sb("mp", [P, P], I32)
        md = sb("md", [NDEC, NDEC], I32)
        mdf = sb("mdf", [NDEC, NDEC])
        mf = sb("mf", [P, P])
        S = sb("S", [P, NCHUNK + 1, DV])
        Sd = sb("Sd", [P, DEC_B, DV])
        Sn = sb("Sn", [P, DEC_B, DV])
        og = sb("og", [P, NT, DV])
        oss = sb("oss", [P, NT])
        ors = sb("ors", [P, NT])
        zb = sb("zb", [P, 2, NTOK])
        ph.close()

        ph = ExitStack()
        sb = sbuf(ph)
        ZH = sb("ZH", [P, 16, NTOK], F32R)
        ZL = sb("ZL", [P, 16, NTOK], F32R)
        PR = sb("PR", [P, 16, P])
        PH = [sb(f"PH{i}", [P, 16, P], F32R) for i in range(2)]
        PL = [sb(f"PL{i}", [P, 16, P], F32R) for i in range(2)]
        sg = sb("sg", [P, 3, NTOK])
        ymix = [sb(f"ymix{i}", [P, NTOK]) for i in range(2)]
        zr = [sg[:, 0, :], sg[:, 1, :]]
        ph.close()

        ph = ExitStack()
        sb = sbuf(ph)
        WOR = sb("WOR", [P, KD, D])
        WOH = sb("WOH", [P, KD, D], F32R)
        WOL = sb("WOL", [P, KD, D], F32R)
        MR = [sb(f"MR{i}", [P, KD, P]) for i in range(2)]
        MH = [sb(f"MH{i}", [P, KD, P], F32R) for i in range(2)]
        ML = [sb(f"ML{i}", [P, KD, P], F32R) for i in range(2)]
        X4 = [sb(f"X4{i}", [P, D]) for i in range(2)]
        X2 = [sb(f"X2{i}", [P, D]) for i in range(2)]
        N2 = [sb(f"N2{i}", [P, D]) for i in range(2)]
        NTt = sb("NTt", [P, KD, P])
        g2b = sb("g2b", [P, D])
        wr = sb("wr", [P, KD, GROUPS + NE])
        rb = sb("rb", [P, GROUPS + NE])
        ss4 = sb("ss4", [P, 1])
        rt4 = sb("rt4", [P, 1])
        rs4 = sb("rs4", [P, 1])
        sq4 = sb("sq4", [P, D])
        ph.close()

        ph = ExitStack()
        sb = sbuf(ph)
        iE = sb("iE", [P, NT, NE], I32)
        ioE = sb("ioE", [P, NT, NE])
        gmx = sb("gmx", [P, NT, 1])
        gsm = sb("gsm", [P, NT, 1])
        gmn = sb("gmn", [P, NT, 1])
        gex = sb("gex", [P, NT, GROUPS])
        gva = sb("gva", [P, NT, GROUPS])
        gtm = sb("gtm", [P, NT, GROUPS])
        ohg = sb("ohg", [P, NT, GROUPS])
        le = sb("le", [P, NT, NE])
        ev = sb("ev", [P, NT, NE])
        v12 = [sb(f"v{i}", [P, NT, 1]) for i in range(2)]
        gd = sb("gd", [P, NT, 1])
        gr = sb("gr", [P, NT, 1])
        oh = [sb(f"oh{i}", [P, NT, NE]) for i in range(2)]
        msk = sb("msk", [P, NT, NE])
        cum = sb("cum", [P, NT, NE])
        rank = sb("rank", [P, NT, NE])
        hib = sb("hib", [P, NT, NE])
        tE = sb("tE", [P, NT, NE])
        tot = sb("tot", [P, NE])
        cnt = sb("cnt", [P, NE])
        ovf = sb("ovf", [P, NE])
        ove = sb("ove", [P, NE])
        one64 = sb("one64", [P, NE])
        stw = sb("stw", [P, NE])
        dst = sb("dst", [P, 2, NT])
        dsti = sb("dsti", [P, 2, NT], I32)
        slot = sb("slot", [P, 2, NT], I32)
        ltri = sb("ltri", [P, P])
        onesm = sb("onesm", [P, P])
        emp = sb("emp", [P, NBLK], I32)
        ovx = sb("ovx", [1, NOVF, NE])
        iV = sb("iV", [1, NOVF, NE], I32)
        ioV = sb("ioV", [1, NOVF, NE])
        ovn = sb("ovn", [1, NOVF + 1])
        ph.close()

        ph = ExitStack()
        sb = sbuf(ph)
        E1 = [sb(f"E1{i}", [P, KD, 2, DE]) for i in range(2)]
        E2 = [sb(f"E2{i}", [P, 2, D]) for i in range(2)]
        E1H = [sb(f"E1H{i}", [P, KD, 2, DE], F32R) for i in range(2)]
        E1L = [sb(f"E1L{i}", [P, KD, 2, DE], F32R) for i in range(2)]
        E2H = [sb(f"E2H{i}", [P, 2, D], F32R) for i in range(2)]
        E2L = [sb(f"E2L{i}", [P, 2, D], F32R) for i in range(2)]
        XG = [sb(f"XG{i}", [P, D]) for i in range(2)]
        XTH = [sb(f"XTH{i}", [P, KD, P], F32R) for i in range(2)]
        XTL = [sb(f"XTL{i}", [P, KD, P], F32R) for i in range(2)]
        sil = sb("sil", [P, DE])
        hid = sb("hid", [P, DE])
        HTH = sb("HTH", [P, 2, P], F32R)
        HTL = sb("HTL", [P, 2, P], F32R)
        YS = [sb(f"YS{i}", [P, D]) for i in range(2)]
        gix = [sb(f"gix{i}", [P, 1], I32) for i in range(2)]
        six = [sb(f"six{i}", [P, 1], I32) for i in range(2)]
        ph.close()

        ph = ExitStack()
        sb = sbuf(ph)
        FX = [sb(f"FX{i}", [P, D]) for i in range(2)]
        FY = [sb(f"FY{i}", [P, 2, D]) for i in range(2)]
        FS = [sb(f"FS{i}", [P, D]) for i in range(2)]
        FO = [sb(f"FO{i}", [P, D]) for i in range(2)]
        gfb = sb("gfb", [P, D])
        jf = sb("jf", [P, D])
        gt6 = [sb(f"gt6{i}", [P, 2]) for i in range(2)]
        ss6 = sb("ss6", [P, 1])
        rt6 = sb("rt6", [P, 1])
        rs6 = sb("rs6", [P, 1])
        ph.close()

        ps = ctx.enter_context(nc.psum_tensor("ps", [P, 8, 512], F32))

        s_bar = sem("phase_done")
        s_const = sem("constants_ready")
        s_alone = {e.engine: sem(f"alone_{n}") for n, e in
                   (("sp", nc.sync), ("pool", nc.gpsimd), ("dve", nc.vector), ("pe", nc.tensor))}

        def barrier(eng, k):
            eng.drain().then_inc(s_bar, 1)
            eng.wait_ge(s_bar, 5 * k)

        def wait_alone(eng, sem_, value):
            eng.wait_ge(sem_, value)
            eng.sem_inc(s_alone[eng.engine], 1)

        def xpos(s):
            return ps[:, 4 + 2 * s:6 + 2 * s, :].rearrange("p b (k t) -> p (b k) t", k=4)

        x_in, g1_in = sem2("x_in"), sem("norm1_gain_in")
        rms_ready, xn_ready, xt_done = sem("rms_ready"), sem("xn_ready"), sem("xn_transposed")
        xh_ready, xl_ready = sem("xh_ready"), sem("xl_ready")
        w_in_s = sem2("w_chunk_in")
        wh_ready, wl_ready, w_used = sem("wh_ready"), sem("wl_ready"), sem("w_used")
        t_mm, t_ev, t_st = sem("tok_product"), sem("tok_evacuated"), sem2("tok_stored")
        f_mm, f_ev, f_st = sem("feat_product"), sem("feat_evacuated"), sem2("feat_stored")
        a_in, a_hi, a_lo, a_mm, a_ev = (sem(f"lowrank_{n}") for n in ("in", "hi", "lo", "product", "done"))
        cv_in, cv_st, cv_z = sem("conv_in"), sem("conv_stored"), sem("conv_done")
        cm_in, cm_wd0, cm_tri, cm_w, cm_wt, cm_wc = (sem(f"mlp_{n}") for n in ("in", "diag_zeroed", "masked", "diag_in", "w_transposed", "w_copied"))
        cm_g, cm_sq, cm_rt, cm_v, cm_mm, cm_z, cm_st, cm_u, cm_ug = (
            sem(f"mlp_{n}") for n in ("gelu_v", "v_squares", "v_rms", "v_normed", "mixed", "done", "stored", "u_in", "gelu_u"))
        g_in, g_r = sem("gla_in"), sem("gla_gain_in")
        g_c, g_a, g_z, g_b, g_e, g_q = (sem(f"gla_{n}") for n in ("consts", "decay_product", "decay_ln", "decay_sum", "decay_exp", "qk"))
        g_kp, g_kc, g_u, g_s = (sem(f"gla_{n}") for n in ("k_transposed", "k_copied", "update", "state"))
        g_ap, g_am, g_o, g_oc = (sem(f"gla_{n}") for n in ("scores", "scores_masked", "out", "out_copied"))
        g_kz = sem("gla_k_masked")
        g_rg, g_rt, g_n, g_tp, g_tc, g_st = (sem(f"gla_{n}") for n in ("r_silu", "out_rms", "out_normed", "out_transposed", "done", "stored"))
        z_in, z_hi, z_lo = sem2("z_in"), sem("z_hi"), sem("z_lo")
        p_in, p_hi, p_lo, p_mm, p_ev = (sem(f"proj_{n}") for n in ("in", "hi", "lo", "product", "gated"))
        sg_in, mix_ready, mix_st = sem("gate_in"), sem("mix_ready"), sem("mix_stored")
        wo_in, wo_hi, wo_lo, m_in, m_hi, m_lo = sem("wo_in"), sem("wo_hi"), sem("wo_lo"), sem2("mix_in"), sem("mix_hi"), sem("mix_lo")
        r4_in, o_mm, x2_ready, x2_rms, n2_ready, n2_tp, n2_tc, l_mm, l_ready = (
            sem(n) for n in ("router_in", "out_product", "x2_ready", "x2_rms", "xn2_ready", "xn2_transposed", "xn2_copied", "logit_product", "logits_ready"))
        n2_st = sem2("xn2_stored")
        r_c, r_mx, r_ex, r_d, r_e2, r_msk, r_mm, r_dst, r_tab, r_sc, r_ld, r_ix = (
            sem(f"route_{n}") for n in ("consts", "group_max", "group_exp", "expert_diff", "expert_exp", "mask", "ranks", "rows", "table_empty", "table_filled", "table_in", "indices"))
        e_in, xg_in, y_st = sem2("expert_in"), sem2("x_gathered"), sem2("y_stored")
        xg0, i_gx, i_sx = sem("xg_zeroed"), sem("gather_index"), sem("scatter_index")
        e1_hi, e1_lo, e2_hi, e2_lo = sem("e1_hi"), sem("e1_lo"), sem("e2_hi"), sem("e2_lo")
        xg_tp, xth, xtl, h_mm, h_sig, h_ready, h_tp, hth, htl, y_mm, y_ready = (
            sem(f"e_{n}") for n in ("x_transposed", "x_hi", "x_lo", "h_product", "h_silu", "h_ready", "h_transposed", "h_hi", "h_lo", "y_product", "y_ready"))
        c_in, c_g, c_gt, c_sum, c_rms, c_out, c_st = sem2("c_in"), sem("c_gain"), sem("c_gates"), sem("c_sum"), sem("c_rms"), sem("c_out"), sem2("c_stored")

        class Step:
            def __init__(self, turn, slot):
                self.t, self.s, self.n = turn, slot, turn * 2 + slot
                self.static = isinstance(turn, int)
                self.first = self.static and turn == 0

            def ahead(self, d):
                return Step(self.t + (self.s + d) // 2, (self.s + d) % 2)

            def within(self, n):
                return not self.static or 0 <= self.n < n

        def steps(eng, body, n, ends=False):
            body(Step(0, 0))
            body(Step(0, 1))
            last = n // 2 - ends
            if last > 1:
                with eng.Fori(1, last) as t:
                    body(Step(t, 0))
                    body(Step(t, 1))
            if ends:
                body(Step(last, 0))
                body(Step(last, 1))
            if n % 2:
                body(Step(n // 2, 0))

        class More(Step):
            def __init__(self, j):
                self.t, self.s, self.n = j + NE // 2, 0, j + NE
                self.static = self.first = False

        def token_tiles(eng, body):
            steps(eng, lambda st: body(st, P), NFULL)
            body(Step(NFULL // 2, 0), NDEC)

        T_TURNS = [(C_V, 4), (C_VV, 1)]
        F_TURNS = [(C_H, 5), (C_U, 1), (C_G, 6)]
        NTC = 2 * sum(n for _, n in T_TURNS)
        NFC = 2 * sum(n for _, n in F_TURNS)

        def chunks(eng, all_turns, base, body):
            base0 = base
            for col, n in all_turns:
                lo = 0
                if base == base0 or n == 1:
                    for s in range(2):
                        body(col, Step(0, s), Step(base, s), Step(base - base0, s))
                    lo = 1
                if n > lo:
                    with eng.Fori(lo, n) as t:
                        for s in range(2):
                            body(col, Step(t, s), Step(t + base, s), Step(t + (base - base0), s))
                base += n

        def tok(t, rows=P):
            return slice(SEQ, NTOK) if rows < P else bass.ds(t * P, P)

        block = ctx.enter_context(nc.Block())
        ctx.enter_context(nc.allow_non_contiguous_dma(reason="short columns of weights and states"))

        @block.sync
        def _(sp):
            sp.dma_start(g1b[:], norm1_g[0:1, :].to_broadcast([P, D])).then_inc(g1_in, 16)

            def load_x(st, rows):
                if not st.first:
                    sp.wait_ge(xn_ready, st.n - 1)
                src = xs[:, :] if rows < P else xp[tok(st.n), :]
                sp.dma_start(X[st.s][0:rows], src).then_inc(x_in[st.s], 16)
            token_tiles(sp, load_x)

            def load_w(col, st, all_, here):
                if not all_.first:
                    sp.wait_ge(wl_ready, all_.n - 1)
                sp.dma_start(RAW[st.s][:], w_in_v[:, :, bass.ds(st.n * CW + col, CW)]).then_inc(w_in_s[st.s], 16)
            chunks(sp, T_TURNS, 0, load_w)
            chunks(sp, F_TURNS, NTC // 2, load_w)
            sp.wait_ge(wl_ready, NTC + NFC - 1)
            sp.dma_start(RAW[0][:, :, 0:P], w_in_v[:, :, C_A:C_A + P]).then_inc(a_in, 16)
            barrier(sp, 1)

            def conv(c, first=False):
                if not first:
                    sp.wait_ge(cv_st, c * 64)
                for to, base in ((cH, C_H), (cG, C_CG), (cB, C_BG)):
                    sp.dma_start(to[:], feat[bass.ds(c * P + base, P), :]).then_inc(cv_in, 16)
                sp.dma_start(cwt[:], conv_w[0][:, bass.ds(c * P, P)].rearrange("k p -> p k")).then_inc(cv_in, 16)
                for b in range(2):
                    sp.dma_start(cps[:, :, b], state_conv[0][:, b, bass.ds(c * P, P)].rearrange("s p -> p s")).then_inc(cv_in, 16)
                sp.wait_ge(cv_z, c + 1)
                sp.dma_start(zT[bass.ds(c * P, P), :], za[:]).then_inc(cv_st, 16)
                sp.dma_start(conv_p[0, 0][:, bass.ds(c * P, P)].rearrange("k p -> p k"), cpp[:, SEQ:SEQ + 2]).then_inc(cv_st, 16)
                for b in range(2):
                    sp.dma_start(conv_s[0][:, b, bass.ds(c * P, P)].rearrange("s p -> p s"),
                                 cps[:, :, DEC_T + b]).then_inc(cv_st, 16)
            conv(0, True)
            with sp.Fori(1, NCH) as c:
                conv(c)
            sp.wait_ge(cv_st, 64 * NCH)

            sp.wait_ge(cm_wd0, 2)
            sp.dma_start(vvt[:, 0:NFULL, :], tokd[0:SEQ, 2048:2560].rearrange("(t p) c -> p t c", p=P)).then_inc(cm_in, 16)
            sp.dma_start(vvt[0:NDEC, NFULL, :], tokd[SEQ:NTOK, 2048:2560]).then_inc(cm_in, 16)
            sp.dma_start(cmg[:], cm_norm_g[0:1].rearrange("a g c -> a (g c)").to_broadcast([P, CONV_CH])).then_inc(cm_in, 16)
            sp.dma_start(cmb[:].rearrange("p g t -> p (g t)"),
                         cm_b[0:1].rearrange("a g t -> a (g t)").to_broadcast([P, NCH * P])).then_inc(cm_in, 16)
            sp.dma_start(wsn[:], cm_ws[0].rearrange("g t s -> t g s")).then_inc(cm_w, 16)
            for q in range(DEC_B):
                sp.dma_start(wsd[q * DEC_T:(q + 1) * DEC_T, :, q * DEC_T:(q + 1) * DEC_T],
                             cm_ws[0][:, 0:DEC_T, 0:DEC_T].rearrange("g t s -> t g s")).then_inc(cm_w, 16)
            sp.wait_ge(cm_v, 1)
            sp.dma_start(chunk_v[0].rearrange("b t c -> (b t) c"), vvt[0:NDEC, NFULL, :]).then_inc(cm_st, 16)
            for c in range(NCH):
                if c:
                    sp.wait_ge(cm_z, c)
                sp.dma_start(uT[:], feat[C_U + c * P:C_U + (c + 1) * P, :]).then_inc(cm_u, 16)
                sp.wait_ge(cm_z, c + 1)
                sp.dma_start(zT[(12 + c) * P:(13 + c) * P, :], zc[:]).then_inc(cm_st, 16)
                sp.wait_ge(cm_st, 16 * (c + 2))
            barrier(sp, 2)

            sp.dma_start(rg[:], gla_norm_g[0:1, :].to_broadcast([P, DV])).then_inc(g_r, 16)
            sp.wait_ge(g_c, 1)

            def gla(h):
                sp.dma_start(a2h[:], gla_a2[0][:, bass.ds(h * P, P)]).then_inc(g_in, 16)
                sp.dma_start(abh[:], gla_a_b[0:1, bass.ds(h * P, P)].rearrange("a p -> p a")).then_inc(g_in, 16)
                sp.dma_start(qT[:], feat[bass.ds(h * P + C_Q, P), :]).then_inc(g_in, 16)
                sp.dma_start(kT[:], feat[bass.ds(h * P + C_K, P), :]).then_inc(g_in, 16)
                for to, base in ((vt, 0), (rt, 1024)):
                    sp.dma_start(to[:, 0:NFULL, :], tokd[0:SEQ, bass.ds(h * DV + base, DV)]
                                 .rearrange("(t p) c -> p t c", p=P)).then_inc(g_in, 16)
                    sp.dma_start(to[0:NDEC, NFULL, :], tokd[SEQ:NTOK, bass.ds(h * DV + base, DV)]).then_inc(g_in, 16)
                sp.dma_start(Sd[:], state_gla[0][:, bass.ds(h, 1)].rearrange("s a d e -> d (s a) e")).then_inc(g_in, 16)
                sp.wait_ge(g_tc, h * NT + NT)
                sp.wait_ge(g_s, h * (NCHUNK + DEC_B) + NCHUNK + DEC_B)
                sp.dma_start(zT[bass.ds(h * DV + 4 * P, DV), :].rearrange("(a p) n -> p a n", p=P), zb[:]).then_inc(g_st, 16)
                sp.dma_start(gla_p[0, 0][bass.ds(h, 1)].rearrange("a d e -> (a d) e"), S[:, NCHUNK, :]).then_inc(g_st, 16)
                sp.dma_start(gla_s[0][:, bass.ds(h, 1)].rearrange("s a d e -> d (s a) e"), Sn[:]).then_inc(g_st, 16)
                wait_alone(sp, g_st, h * 48 + 48)
            with sp.Fori(0, HEADS) as h:
                gla(h)
            barrier(sp, 3)

            def load_z(st):
                if not st.first:
                    sp.wait_ge(z_lo, st.n - 1)
                sp.dma_start(zr[st.s], zT[bass.ds(st.n * P, P), :]).then_inc(z_in[st.s], 16)
            steps(sp, load_z, 16)
            sp.wait_ge(z_lo, 16)

            def load_proj(st):
                n = st.n
                again = not (st.first and st.s == 0)
                if again:
                    sp.wait_ge(p_lo, n)
                for k0, kn, w in ((0, 4, proj_a), (4, 8, proj_b), (12, 4, proj_c)):
                    sp.dma_start(PR[:, k0:k0 + kn, :], w[0].rearrange("(k p) c -> p k c", p=P)[:, :, bass.ds(n * P, P)]).then_inc(p_in, 16)
                if again:
                    sp.wait_ge(mix_ready, n)
                    sp.dma_start(mixT[bass.ds((n - 1) * P, P), :], ymix[1 - st.s][:]).then_inc(mix_st, 16)
                for b in range(3):
                    sp.dma_start(sg[:, b, :], feat[bass.ds(n * P + C_G + b * D, P), :]).then_inc(sg_in, 16)
                if again:
                    wait_alone(sp, mix_st, n * 16)
            steps(sp, load_proj, KD)
            sp.wait_ge(mix_ready, KD)
            sp.dma_start(mixT[(KD - 1) * P:KD * P, :], ymix[1][:]).then_inc(mix_st, 16)
            sp.wait_ge(mix_st, 16 * KD)
            barrier(sp, 4)

            sp.dma_start(WOR[:], w_out[0].rearrange("(k p) c -> p k c", p=P)).then_inc(wo_in, 16)
            sp.dma_start(g2b[:], norm2_g[0:1, :].to_broadcast([P, D])).then_inc(r4_in, 16)
            sp.dma_start(wr[:, :, 0:GROUPS], rg_w[0].rearrange("(k p) c -> p k c", p=P)).then_inc(r4_in, 16)
            sp.dma_start(wr[:, :, GROUPS:], re_w[0].rearrange("(k p) c -> p k c", p=P)).then_inc(r4_in, 16)
            sp.dma_start(rb[:, 0:GROUPS], rg_b[0:1, :].to_broadcast([P, GROUPS])).then_inc(r4_in, 16)
            sp.dma_start(rb[:, GROUPS:], re_b[0:1, :].to_broadcast([P, NE])).then_inc(r4_in, 16)

            def load_m(st, rows):
                if not st.first:
                    sp.wait_ge(m_lo, st.n - 1)
                    sp.wait_ge(x2_ready, st.n - 1)
                mv = mixT.rearrange("(k p) n -> p k n", p=P)
                sp.dma_start(MR[st.s][:, :, 0:rows], mv[:, :, tok(st.n, rows)]).then_inc(m_in[st.s], 16)
                src = xs[:, :] if rows < P else xp[tok(st.n), :]
                sp.dma_start(X4[st.s][0:rows], src).then_inc(m_in[st.s], 16)
            token_tiles(sp, load_m)
            barrier(sp, 5)

            sp.wait_ge(r_c, 1)
            sp.dma_start(table.rearrange("(p b) a -> p (b a)", p=P), emp[:]).then_inc(r_tab, 16)
            sp.wait_ge(r_sc, 16 * 2 * NT)
            sp.dma_start(sidx[:], table.rearrange("(p b) a -> p (b a)", p=P)).then_inc(r_ld, 16)
            sp.wait_ge(r_ld, 16)
            barrier(sp, 6)

            def load_expert(e, s):
                sp.dma_start(E1[s][:, :, 0, :], exp_w1[0][bass.ds(e, 1)].rearrange("a (p k) c -> p (a k) c", k=KD)).then_inc(e_in[s], 16)
                sp.dma_start(E1[s][:, :, 1, :], exp_w3[0][bass.ds(e, 1)].rearrange("a (p k) c -> p (a k) c", k=KD)).then_inc(e_in[s], 16)
                sp.dma_start(E2[s][:], exp_w2[0][bass.ds(e, 1)].rearrange("a (p k) c -> p (a k) c", k=2)).then_inc(e_in[s], 16)

            def expert(st):
                if not st.first:
                    sp.wait_ge(e1_lo, st.n - 1)
                    sp.wait_ge(e2_lo, st.n - 1)
                load_expert(st.n, st.s)
            steps(sp, expert, NE)
            barrier(sp, 7)
            n_more = sp.value_load(eovf[0:1, NOVF:NOVF + 1], min_val=0, max_val=NOVF)
            with sp.If(n_more > 0):
                with sp.Fori(0, n_more) as j:
                    e = sp.value_load(eovf[0:1, bass.ds(j, 1)], min_val=0, max_val=NE - 1)
                    sp.wait_ge(y_ready, j + NE)
                    load_expert(e, 0)
            barrier(sp, 8)

            sp.dma_start(gfb[:], final_g.rearrange("(a n) -> a n", a=1).to_broadcast([P, D])).then_inc(c_g, 16)

            def load_c(st, rows):
                if not st.first:
                    sp.wait_ge(c_sum, st.n - 1)
                r0 = SEQ if rows < P else st.n * P
                sp.dma_start(FX[st.s][0:rows], x2d[bass.ds(r0, rows), :]).then_inc(c_in[st.s], 16)
                sp.dma_start(FY[st.s][0:rows], y2d.rearrange("(n k) c -> n k c", k=2)[bass.ds(r0, rows)]).then_inc(c_in[st.s], 16)
            token_tiles(sp, load_c)
            barrier(sp, 9)

        @block.gpsimd
        def _(pool):
            pool.memset(ident[:], 0.0)
            pool.memset(epsc[:], EPS)
            pool.memset(lgt[:, NFULL, :], 0.0)
            pool.drain()
            pool.affine_select(out=ident[:], in_=ident[:], compare_op=ALU.not_equal, fill=1.0, base=0,
                               pattern=[[-1, P]], channel_multiplier=1).then_inc(s_const, 1)

            def store_t(col, st, all_, here):
                base = 0 if col == C_V else 2048
                pool.wait_ge(t_ev, all_.n * NT + NT)
                cols = bass.ds(st.n * CW + base, CW)
                pool.dma_start(tokd[0:SEQ, cols].rearrange("(t p) c -> p t c", p=P), OT[st.s][:, 0:NFULL, :]).then_inc(t_st[st.s], 16)
                pool.dma_start(tokd[SEQ:NTOK, cols], OT[st.s][0:NDEC, NFULL, :]).then_inc(t_st[st.s], 16)
            chunks(pool, T_TURNS, 0, store_t)

            def store_f(col, st, all_, here):
                pool.wait_ge(f_ev, here.n * 2 + 2)
                pool.dma_start(feat[bass.ds(st.n * CW + col, CW), :].rearrange("(a p) n -> p a n", p=P), OF[st.s][:]).then_inc(f_st[st.s], 16)
            chunks(pool, F_TURNS, NTC // 2, store_f)
            for s in range(2):
                pool.wait_ge(t_st[s], 32 * (NTC // 2))
                pool.wait_ge(f_st[s], 16 * (NFC // 2))
            barrier(pool, 1)

            pool.memset(wsd[:], 0.0).then_inc(cm_wd0, 1)
            pool.memset(vvt[:, NFULL, :], 0.0).then_inc(cm_wd0, 1)
            pool.wait_ge(cm_w, 16 * (1 + DEC_B))
            pool.affine_select(out=wsn[:], in_=wsn[:], compare_op=ALU.is_ge, fill=0.0, base=0,
                               pattern=[[0, NCH], [-1, P]], channel_multiplier=1).then_inc(cm_tri, 1)
            pool.affine_select(out=wsd[:], in_=wsd[:], compare_op=ALU.is_ge, fill=0.0, base=0,
                               pattern=[[0, NCH], [-1, NDEC]], channel_multiplier=1).then_inc(cm_tri, 1)
            barrier(pool, 2)

            pool.memset(mf[:], 1.0)
            pool.memset(mdf[:], 1.0)
            pool.memset(rmask[:], 1.0)
            pool.memset(seg[:], 1.0)
            pool.memset(S[:, 0, :], 0.0)
            pool.memset(qz[:], 0.0)
            for b in (vt, rt, og):
                pool.memset(b[:, NFULL, :], 0.0)
            pool.memset(oss[:], 1.0)
            for b in attm:
                pool.memset(b[:], 0.0)
            pool.memset(attd[:], 0.0)
            pool.drain()
            pool.memset(seg[:, 0:SEQ].rearrange("p (c t) -> p c t", t=CHUNK)[:, :, 0:1], 0.0)
            pool.memset(seg[:, SEQ:NTOK].rearrange("p (c t) -> p c t", t=DEC_T)[:, :, 0:1], 0.0)
            pool.affine_select(out=mf[:], in_=mf[:], compare_op=ALU.is_ge, fill=0.0, base=0,
                               pattern=[[1, P]], channel_multiplier=-1)
            pool.affine_select(out=mdf[:], in_=mdf[:], compare_op=ALU.is_ge, fill=0.0, base=0,
                               pattern=[[1, NDEC]], channel_multiplier=-1)
            pool.affine_select(out=rmask[:], in_=rmask[:], compare_op=ALU.is_ge, fill=0.0, base=0,
                               pattern=[[-DEC_T, DEC_B]], channel_multiplier=1)
            pool.drain()
            pool.memset(mf[0:CHUNK, CHUNK:P], 0.0)
            pool.affine_select(out=mdf[:], in_=mdf[:], compare_op=ALU.is_ge, fill=0.0, base=0,
                               pattern=[[-DEC_T, DEC_B], [0, DEC_T]], channel_multiplier=1)
            pool.affine_select(out=rmask[:], in_=rmask[:], compare_op=ALU.is_ge, fill=0.0, base=DEC_T - 1,
                               pattern=[[DEC_T, DEC_B]], channel_multiplier=-1)
            pool.drain()
            pool.tensor_copy(mp[:], mf[:])
            pool.tensor_copy(md[:], mdf[:])
            pool.drain().then_inc(g_c, 1)
            barrier(pool, 3)
            barrier(pool, 4)

            def store_n2(st, rows):
                pool.wait_ge(n2_ready, st.n + 1)
                pool.dma_start(x2d[tok(st.n, rows), :], X2[st.s][0:rows]).then_inc(n2_st[st.s], 16)
                pool.dma_start(xn2d[tok(st.n, rows), :], N2[st.s][0:rows]).then_inc(n2_st[st.s], 16)
            token_tiles(pool, store_n2)
            pool.wait_ge(n2_st[0], 32 * (NFULL // 2 + 1))
            pool.wait_ge(n2_st[1], 32 * (NFULL // 2))
            barrier(pool, 5)

            pool.memset(emp[:], EMPTY)
            pool.memset(onesm[:], 1.0)
            pool.memset(ltri[:], 1.0)
            pool.memset(one64[:], 1.0)
            pool.iota(iE[:], pattern=[[0, NT], [1, NE]], base=0, channel_multiplier=0)
            pool.iota(iV[:], pattern=[[1, NOVF], [0, NE]], base=0, channel_multiplier=0)
            pool.iota(slot[:], pattern=[[1, 2], [2 * P, NT]], base=0, channel_multiplier=2)
            pool.drain()
            pool.affine_select(out=ltri[:], in_=ltri[:], compare_op=ALU.is_gt, fill=0.0, base=0,
                               pattern=[[1, P]], channel_multiplier=-1)
            pool.tensor_copy(ioE[:], iE[:])
            pool.tensor_copy(ioV[:], iV[:])
            pool.drain().then_inc(r_c, 1)
            pool.wait_ge(r_tab, 16)
            pool.wait_ge(r_dst, 1)
            for t in range(NT):
                for k in range(2):
                    pool.indirect_dma_start(out=table[:, :], out_offset=bass.IndirectOffsetOnAxis(ap=dsti[:, k, t:t + 1], axis=0),
                                            in_=slot[:, k, t:t + 1], in_offset=None,
                                            bounds_check=P * NBLK - 1, oob_is_err=False).then_inc(r_sc, 16)
            pool.wait_ge(r_sc, 16 * 2 * NT)
            barrier(pool, 6)

            pool.memset(XG[0][:], 0.0)
            pool.memset(XG[1][:], 0.0)
            pool.drain()

            def gather(st, lag=2):
                n, s = st.n, st.s
                if lag == 1 or not st.first:
                    pool.wait_ge(xg_tp, n + 1 - lag)
                    pool.wait_ge(xg_in[s], st.t * 16)
                pool.tensor_copy(gix[s][:], tidx[:, bass.ds(n, 1)]).then_inc(i_gx, 1)
                wait_alone(pool, i_gx, n + 1)
                pool.indirect_dma_start(out=XG[s][:], out_offset=None, in_=xn2d[:, :],
                                        in_offset=bass.IndirectOffsetOnAxis(ap=gix[s][:, 0:1], axis=0),
                                        bounds_check=NTOK - 1, oob_is_err=False).then_inc(xg_in[s], 16)

            def scatter(st):
                n, s = st.n, st.s
                if not st.first:
                    pool.wait_ge(y_st[s], st.t * 16)
                pool.tensor_copy(six[s][:], sidx[:, bass.ds(n, 1)]).then_inc(i_sx, 1)
                pool.wait_ge(y_ready, n + 1)
                wait_alone(pool, i_sx, n + 1)
                pool.indirect_dma_start(out=y2d[:, :], out_offset=bass.IndirectOffsetOnAxis(ap=six[s][:, 0:1], axis=0),
                                        in_=YS[s][:], in_offset=None,
                                        bounds_check=NSLOT - 1, oob_is_err=False).then_inc(y_st[s], 16)

            gather(Step(0, 0))
            gather(Step(0, 1))

            def move(st):
                if st.ahead(2).within(NE):
                    gather(st.ahead(2))
                if st.ahead(-1).within(NE):
                    scatter(st.ahead(-1))
            steps(pool, move, NE, ends=True)
            scatter(Step(NE // 2 - 1, 1))
            for s in range(2):
                pool.wait_ge(y_st[s], 16 * (NE // 2))
            barrier(pool, 7)
            n_more = pool.value_load(eovf[0:1, NOVF:NOVF + 1], min_val=0, max_val=NOVF)
            with pool.If(n_more > 0):
                with pool.Fori(0, n_more) as j:
                    st = More(j)
                    gather(st, lag=1)
                    scatter(st)
                    pool.wait_ge(y_st[0], (j + 1 + NE // 2) * 16)
            barrier(pool, 8)

            def store_c(st, rows):
                pool.wait_ge(c_out, st.n + 1)
                out = y_sample.rearrange("a b n -> (a b) n") if rows < P else y_prompt[0][tok(st.n), :]
                pool.dma_start(out, FO[st.s][0:rows]).then_inc(c_st[st.s], 16)
            token_tiles(pool, store_c)
            pool.wait_ge(c_st[0], 16 * (NFULL // 2 + 1))
            pool.wait_ge(c_st[1], 16 * (NFULL // 2))
            barrier(pool, 9)

        @block.scalar
        def _(act):
            act.wait_ge(s_const, 1)

            def norm1(st, rows):
                n, s = st.n, st.s
                act.wait_ge(x_in[s], st.t * 16 + 16)
                act.activation(junk[0:rows], X[s][0:rows], ACT.Square, accum_out=ssq[s][0:rows])
                act.drain()
                act.activation(rtt[s][0:rows], ssq[s][0:rows], ACT.Sqrt, bias=epsc[0:rows], scale=1.0 / D).then_inc(rms_ready, 1)
                act.wait_ge(xt_done, n + 1)
                act.activation(XH[:, :, tok(n, rows)], xpos(s)[:, :, 0:rows], ACT.Copy).then_inc(xh_ready, 1)
            token_tiles(act, norm1)

            def split_w(all_):
                n, s = all_.n, all_.s
                act.wait_ge(w_in_s[s], all_.t * 16 + 16)
                if not all_.first:
                    act.wait_ge(w_used, n - 1)
                act.activation(WH[s][:], RAW[s][:], ACT.Copy).then_inc(wh_ready, 1)

            split_w(Step(0, 0))

            def t_chunk(col, st, all_, here):
                split_w(all_.ahead(1))
                s = st.s
                for tile in range(NT):
                    rows = rows_of(tile)
                    u = s * NT + tile
                    act.wait_ge(t_mm, all_.n * NT + tile + 1)
                    if tile == 0 and not all_.first:
                        act.wait_ge(t_st[s], all_.t * 32)
                    act.activation(OT[s][0:rows, tile, :], ps[0:rows, u % 6, 0:CW], ACT.Copy).then_inc(t_ev, 1)
            chunks(act, T_TURNS, 0, t_chunk)

            def f_chunk(func, last=None):
                def go(col, st, all_, here):
                    s = st.s
                    if not (last and st.static and s == 1):
                        split_w(all_.ahead(1))
                    for f in range(2):
                        act.wait_ge(f_mm, here.n * 2 + (f + 1))
                        if f == 0 and not here.first:
                            act.wait_ge(f_st[s], here.t * 16)
                        act.activation(OF[s][:, f, 0:768].rearrange("p (g n) -> p g n", g=2), ps[:, 3 * f:3 * f + 2, 0:384], func)
                        act.activation(OF[s][:, f, 768:NTOK], ps[:, 3 * f + 2, 0:320], func).then_inc(f_ev, 1)
                return go
            b = NTC // 2
            for s in range(2):
                f_chunk(ACT.Copy)(C_H, Step(0, s), Step(b, s), Step(0, s))
            with act.Fori(1, 5) as t:
                for s in range(2):
                    f_chunk(ACT.Copy)(C_H, Step(t, s), Step(t + b, s), Step(t, s))
            for s in range(2):
                f_chunk(ACT.Gelu_apprx_tanh)(C_U, Step(0, s), Step(b + 5, s), Step(5, s))
            with act.Fori(0, 5) as t:
                for s in range(2):
                    f_chunk(ACT.Sigmoid)(C_G, Step(t, s), Step(t + (b + 6), s), Step(t + 6, s))
            for s in range(2):
                f_chunk(ACT.Sigmoid, last=True)(C_G, Step(5, s), Step(b + 11, s), Step(11, s))
            act.wait_ge(a_in, 16)
            act.wait_ge(w_used, NTC + NFC)
            act.activation(WH[0][:, :, 0:P], RAW[0][:, :, 0:P], ACT.Copy).then_inc(a_hi, 1)
            act.wait_ge(a_mm, 1)
            act.activation(alr[:, 0:768].rearrange("p (g n) -> p g n", g=2), ps[0:LOWRANK, 0:2, 0:384], ACT.Copy)
            act.activation(alr[:, 768:NTOK], ps[0:LOWRANK, 2, 0:320], ACT.Copy)
            barrier(act, 1)

            act.wait_ge(cm_in, 64)
            act.activation(vvt[:], vvt[:], ACT.Gelu_apprx_tanh).then_inc(cm_g, 1)
            act.drain()
            act.activation(vsq[:], vvt[:], ACT.Square).then_inc(cm_sq, 1)
            act.wait_ge(cm_rt, 1)
            act.activation(vrs[:], vss[:], ACT.Sqrt, bias=epsc[:], scale=1.0 / P).then_inc(cm_rt, 1)
            for half in range(2):
                act.wait_ge(cm_wt, half + 1)
                if half == 0:
                    act.activation(wsT[:], ps[:, 0, :].rearrange("p (g t) -> p g t", g=NCH), ACT.Copy).then_inc(cm_wc, 1)
                else:
                    act.activation(wsdT[:], ps[0:NDEC, 1, 0:NCH * NDEC].rearrange("p (g t) -> p g t", g=NCH), ACT.Copy).then_inc(cm_wc, 1)
            barrier(act, 2)

            def gla(h):
                act.wait_ge(g_in, h * 144 + 144)
                act.activation(rt[:], rt[:], ACT.Silu).then_inc(g_rg, 1)
                act.wait_ge(g_a, h + 1)
                act.activation(zz[:, 0:768].rearrange("p (g n) -> p g n", g=2), ps[:, 0:2, 0:384], ACT.Identity, bias=abh[:])
                act.activation(zz[:, 768:NTOK], ps[:, 2, 0:320], ACT.Identity, bias=abh[:])
                act.drain()
                act.activation(t1[:], zz[:], ACT.Abs)
                act.drain()
                act.activation(t1[:], t1[:], ACT.Exp, scale=-1.0)
                act.drain()
                act.activation(t1[:], t1[:], ACT.Ln, bias=1.0).then_inc(g_z, 1)
                act.wait_ge(g_b, h * 2 + 1)
                act.activation(eb[:], cs[:], ACT.Exp, scale=1.0 / TAU)
                act.activation(t1[:], cs[:], ACT.Exp, scale=-1.0 / TAU)
                act.wait_ge(g_b, h * 2 + 2)
                act.activation(zz[:], zz[:], ACT.Exp, scale=1.0 / TAU).then_inc(g_e, 1)
                for j in range(NT):
                    rows = rows_of(j)
                    act.wait_ge(g_kp, h * NT + (j + 1))
                    act.activation(ket[j % 2][0:rows], ps[0:rows, 3 + j % 2, 0:P], ACT.Copy).then_inc(g_kc, 1)
                for j in range(NT):
                    rows = rows_of(j)
                    act.wait_ge(g_o, h * NT + (j + 1))
                    act.activation(og[0:rows, j, :], ps[0:rows, j % 2, 0:DV], ACT.Copy)
                    act.activation(t1[0:rows, (j % 4) * DV:(j % 4 + 1) * DV], ps[0:rows, j % 2, 0:DV], ACT.Square, accum_out=oss[0:rows, j:j + 1]).then_inc(g_oc, 1)
                act.drain()
                act.activation(ors[:], oss[:], ACT.Sqrt, bias=epsc[:], scale=1.0 / DV).then_inc(g_rt, 1)
                for j in range(NT):
                    rows = rows_of(j)
                    act.wait_ge(g_tp, h * NT + (j + 1))
                    act.activation(zb[:, :, j * P:j * P + rows], ps[:, 2 + j % 2, 0:2 * P].rearrange("p (a t) -> p a t", a=2)[:, :, 0:rows],
                                   ACT.Copy).then_inc(g_tc, 1)
            with act.Fori(0, HEADS) as h:
                gla(h)
            barrier(act, 3)

            def hi_z(st):
                act.wait_ge(z_in[st.s], st.t * 16 + 16)
                act.activation(ZH[:, bass.ds(st.n, 1), :].rearrange("p a n -> p (a n)"), zr[st.s], ACT.Copy).then_inc(z_hi, 1)
            steps(act, hi_z, 16)

            def hi_p(st):
                act.wait_ge(p_in, st.n * 48 + 48)
                if not st.first:
                    act.wait_ge(p_mm, st.n * 3 - 3)
                act.activation(PH[st.s][:], PR[:], ACT.Copy).then_inc(p_hi, 1)
            steps(act, hi_p, KD)
            barrier(act, 4)

            act.wait_ge(wo_in, 16)
            act.activation(WOH[:], WOR[:], ACT.Copy).then_inc(wo_hi, 1)

            def hi_m(st, rows):
                act.wait_ge(m_in[st.s], st.t * 32 + 32)
                if not st.first:
                    act.wait_ge(o_mm, st.n - 1)
                act.activation(MH[st.s][:, :, 0:rows], MR[st.s][:, :, 0:rows], ACT.Copy).then_inc(m_hi, 1)

            def norm2(st, rows):
                act.wait_ge(x2_ready, st.n + 1)
                act.activation(sq4[0:rows], X2[st.s][0:rows], ACT.Square, accum_out=ss4[0:rows])
                act.drain()
                act.activation(rt4[0:rows], ss4[0:rows], ACT.Sqrt, bias=epsc[0:rows], scale=1.0 / D).then_inc(x2_rms, 1)
                act.wait_ge(n2_tp, st.n + 1)
                act.activation(NTt[:, :, 0:rows], ps[:, 4:6, :].rearrange("p b (k t) -> p (b k) t", k=4)[:, :, 0:rows], ACT.Copy).then_inc(n2_tc, 1)
            hi_m(Step(0, 0), P)

            def out_tile(st, rows):
                nxt = st.ahead(1)
                if rows == P:
                    hi_m(nxt, P)
                norm2(st, rows)
            steps(act, lambda st: out_tile(st, P), NFULL - 2)
            last = Step(NFULL // 2 - 1, 0)
            out_tile(last, P)
            hi_m(Step(NFULL // 2, 0), NDEC)
            norm2(last.ahead(1), P)
            norm2(Step(NFULL // 2, 0), NDEC)
            barrier(act, 5)

            act.wait_ge(r_mx, 1)
            act.activation(gex[:], gva[:], ACT.Exp).then_inc(r_ex, 1)
            act.wait_ge(r_d, 1)
            act.activation(gd[:], gd[:], ACT.Exp).then_inc(r_e2, 1)
            barrier(act, 6)

            def split1(st, lag=2):
                act.wait_ge(e_in[st.s], st.t * 48 + 48)
                if lag == 1 or not st.first:
                    act.wait_ge(h_mm, st.n + 1 - lag)
                act.activation(E1H[st.s][:], E1[st.s][:], ACT.Copy).then_inc(e1_hi, 1)

            def split2(st, lag=2):
                if lag == 1 or not st.first:
                    act.wait_ge(y_mm, st.n + 1 - lag)
                act.activation(E2H[st.s][:], E2[st.s][:], ACT.Copy).then_inc(e2_hi, 1)

            def x_hi(st):
                act.wait_ge(xg_tp, st.n + 1)
                act.activation(XTH[st.s][:], ps[:, 0:2, :].rearrange("p b (k t) -> p (b k) t", k=4), ACT.Copy).then_inc(xth, 1)

            def silu(st):
                act.wait_ge(h_mm, st.n + 1)
                if not (st.first and st.s == 0):
                    act.wait_ge(h_ready, st.n)
                act.activation(sil[:], ps[:, 2 + st.s, 0:DE], ACT.Silu).then_inc(h_sig, 1)

            def y_out(st):
                act.wait_ge(y_mm, st.n + 1)
                if not st.first:
                    act.wait_ge(y_st[st.s], st.t * 16)
                act.activation(YS[st.s][:], ps[:, 5:7, :].rearrange("p b n -> p (b n)"), ACT.Copy).then_inc(y_ready, 1)

            def h_hi(st):
                act.wait_ge(h_tp, st.n + 1)
                act.activation(HTH[:], ps[:, 4, 0:2 * P].rearrange("p (a t) -> p a t", a=2), ACT.Copy).then_inc(hth, 1)

            split1(Step(0, 0))
            split2(Step(0, 0))
            x_hi(Step(0, 0))

            def expert(st):
                nxt, prev = st.ahead(1), st.ahead(-1)
                more = nxt.within(NE)
                if more:
                    split1(nxt)
                silu(st)
                if more:
                    split2(nxt)
                    x_hi(nxt)
                if prev.within(NE):
                    y_out(prev)
                h_hi(st)
            steps(act, expert, NE, ends=True)
            y_out(Step(NE // 2 - 1, 1))
            barrier(act, 7)
            n_more = act.value_load(eovf[0:1, NOVF:NOVF + 1], min_val=0, max_val=NOVF)
            with act.If(n_more > 0):
                with act.Fori(0, n_more) as j:
                    st = More(j)
                    split1(st, lag=1)
                    split2(st, lag=1)
                    x_hi(st)
                    silu(st)
                    h_hi(st)
                    y_out(st)
            barrier(act, 8)

            def norm_f(st, rows):
                act.wait_ge(c_sum, st.n + 1)
                act.activation(jf[0:rows], FS[st.s][0:rows], ACT.Square, accum_out=ss6[0:rows])
                act.drain()
                act.activation(rt6[0:rows], ss6[0:rows], ACT.Sqrt, bias=epsc[0:rows], scale=1.0 / D).then_inc(c_rms, 1)
            token_tiles(act, norm_f)
            barrier(act, 9)

        @block.vector
        def _(dve):
            dve.wait_ge(g1_in, 16)

            def norm1(st, rows):
                n, s = st.n, st.s
                dve.wait_ge(rms_ready, n + 1)
                dve.reciprocal(rst[s][0:rows], rtt[s][0:rows])
                dve.drain()
                if not st.first:
                    dve.wait_ge(xt_done, n - 1)
                dve.scalar_tensor_tensor(out=XN[s][0:rows], in0=X[s][0:rows], scalar=rst[s][0:rows], in1=g1b[0:rows],
                                         op0=ALU.mult, op1=ALU.mult).then_inc(xn_ready, 1)
                dve.wait_ge(xh_ready, n + 1)
                dve.tensor_tensor(XL[:, :, tok(n, rows)], xpos(s)[:, :, 0:rows], XH[:, :, tok(n, rows)].bitcast(F32),
                                  ALU.subtract).then_inc(xl_ready, 1)
            token_tiles(dve, norm1)

            def low_w(col, st, all_, here):
                dve.wait_ge(wh_ready, all_.n + 1)
                dve.tensor_tensor(WL[st.s][:], RAW[st.s][:], WH[st.s][:].bitcast(F32), ALU.subtract).then_inc(wl_ready, 1)
            chunks(dve, T_TURNS, 0, low_w)
            chunks(dve, F_TURNS, NTC // 2, low_w)
            dve.wait_ge(a_hi, 1)
            dve.tensor_tensor(WL[0][:, :, 0:P], RAW[0][:, :, 0:P], WH[0][:, :, 0:P].bitcast(F32), ALU.subtract).then_inc(a_lo, 1)
            barrier(dve, 1)

            dve.memset(cpp[:, 0:2], 0.0)

            def conv(c):
                dve.wait_ge(cv_in, c * 96 + 96)
                dve.tensor_tensor(cpp[:, 2:2 + SEQ], cG[:, 0:SEQ], cH[:, 0:SEQ], ALU.mult)
                dve.tensor_tensor(cps[:, :, 2:2 + DEC_T], cG[:, SEQ:NTOK].rearrange("p (s t) -> p s t", s=DEC_B),
                                  cH[:, SEQ:NTOK].rearrange("p (s t) -> p s t", s=DEC_B), ALU.mult)
                dve.drain()
                co, cz = cout[:, SEQ:NTOK].rearrange("p (s t) -> p s t", s=DEC_B), cout[:, 0:SEQ]
                dve.tensor_scalar(cz, cpp[:, 0:SEQ], cwt[:, 0:1], None, ALU.mult)
                dve.tensor_scalar(co, cps[:, :, 0:DEC_T], cwt[:, 0:1], None, ALU.mult)
                for k in (1, 2):
                    dve.drain()
                    dve.scalar_tensor_tensor(out=cz, in0=cpp[:, k:k + SEQ], scalar=cwt[:, k:k + 1], in1=cz, op0=ALU.mult, op1=ALU.add)
                    dve.scalar_tensor_tensor(out=co, in0=cps[:, :, k:k + DEC_T], scalar=cwt[:, k:k + 1], in1=co, op0=ALU.mult, op1=ALU.add)
                dve.drain()
                dve.tensor_tensor(za[:], cB[:], cout[:], ALU.mult).then_inc(cv_z, 1)
            with dve.Fori(0, NCH) as c:
                conv(c)

            dve.wait_ge(cm_sq, 1)
            dve.tensor_reduce(vss[:], vsq[:].rearrange("p t (g c) -> p (t g) c", g=NCH), AX.X, ALU.add).then_inc(cm_rt, 1)
            dve.wait_ge(cm_rt, 2)
            dve.reciprocal(vss[:], vrs[:])
            dve.drain()
            v3 = vvt[:].rearrange("p t (g c) -> p (t g) c", g=NCH)
            dve.tensor_tensor(v3, v3, vss[:].rearrange("p (a b) -> p a b", b=1).to_broadcast([P, NT * NCH, P]), ALU.mult)
            dve.drain()
            dve.tensor_tensor(vvt[:], vvt[:], cmg[:].rearrange("p (a c) -> p a c", a=1).to_broadcast([P, NT, CONV_CH]), ALU.mult).then_inc(cm_v, 1)
            for c in range(NCH):
                dve.wait_ge(cm_mm, c + 1)
                dve.wait_ge(cm_u, 16 * (c + 1))
                if c:
                    dve.wait_ge(cm_st, 16 * (c + 1))
                dve.tensor_tensor(zc[:, 0:SEQ].rearrange("p (n t) -> p n t", t=P), ps[:, 2:4, :].rearrange("p b (n t) -> p (b n) t", t=P),
                                  cmb[:, c:c + 1, :].to_broadcast([P, NFULL, P]), ALU.add)
                dve.tensor_tensor(zc[:, SEQ:NTOK].rearrange("p (n t) -> p n t", t=DEC_T), ps[:, 4, 0:NDEC].rearrange("p (n t) -> p n t", t=DEC_T),
                                  cmb[:, c:c + 1, 0:DEC_T].to_broadcast([P, DEC_B, DEC_T]), ALU.add)
                dve.drain()
                dve.tensor_tensor(zc[:], zc[:], uT[:], ALU.mult).then_inc(cm_z, 1)
            barrier(dve, 2)

            dve.wait_ge(g_r, 16)
            dve.wait_ge(g_c, 1)
            csp = cs[:, 0:SEQ].rearrange("p (c t) -> p c t", t=CHUNK)
            csd = cs[:, SEQ:NTOK].rearrange("p (c t) -> p c t", t=DEC_T)

            def gla(h):
                dve.wait_ge(g_z, h + 1)
                dve.scalar_tensor_tensor(out=zz[:], in0=zz[:], scalar=0.0, in1=t1[:], op0=ALU.min, op1=ALU.subtract)
                dve.drain()
                dve.tensor_tensor_scan(cs[:], seg[:], zz[:], 0.0, ALU.mult, ALU.add)
                dve.drain().then_inc(g_b, 1)
                dve.tensor_tensor(zz[:, 0:SEQ].rearrange("p (c t) -> p c t", t=CHUNK), csp[:, :, CHUNK - 1:CHUNK].to_broadcast([P, NCHUNK, CHUNK]), csp, ALU.subtract)
                dve.tensor_tensor(zz[:, SEQ:NTOK].rearrange("p (c t) -> p c t", t=DEC_T), csd[:, :, DEC_T - 1:DEC_T].to_broadcast([P, DEC_B, DEC_T]), csd, ALU.subtract)
                dve.drain().then_inc(g_b, 1)
                dve.wait_ge(g_rg, h + 1)
                dve.tensor_tensor(rt[:], rt[:], rg[:].rearrange("p (a c) -> p a c", a=1).to_broadcast([P, NT, DV]), ALU.mult)
                dve.wait_ge(g_e, h + 1)
                dve.scalar_tensor_tensor(out=qt[:], in0=qT[:], scalar=float(DK) ** -0.5, in1=eb[:], op0=ALU.mult, op1=ALU.mult)
                dve.tensor_tensor(kt[:], kT[:], t1[:], ALU.mult)
                dve.tensor_tensor(ke[:], kT[:], zz[:], ALU.mult)
                dve.drain()
                for q in range(DEC_B):
                    dve.tensor_copy(qz[:, q, q * DEC_T:(q + 1) * DEC_T], qt[:, SEQ + q * DEC_T:SEQ + (q + 1) * DEC_T])
                dve.drain().then_inc(g_q, 1)
                per = NCHUNK + DEC_B
                for c in range(NCHUNK):
                    dve.wait_ge(g_u, h * per + (c + 1))
                    last = c * CHUNK + CHUNK - 1
                    dve.scalar_tensor_tensor(out=S[:, c + 1, :], in0=S[:, c, :], scalar=eb[:, last:last + 1], in1=ps[:, 5 + c % 2, 0:DV],
                                             op0=ALU.mult, op1=ALU.add).then_inc(g_s, 1)
                    dve.drain()
                dve.wait_ge(g_kc, h * NT + NT)
                for q in range(DEC_B):
                    dve.tensor_scalar(kz[:, q, :], ket[(NT - 1) % 2][0:NDEC], rmask[:, q:q + 1], None, ALU.mult)
                dve.drain().then_inc(g_kz, 1)
                for q in range(DEC_B):
                    dve.wait_ge(g_u, h * per + (NCHUNK + q + 1))
                    last = SEQ + q * DEC_T + DEC_T - 1
                    dve.scalar_tensor_tensor(out=Sn[:, q, :], in0=Sd[:, q, :], scalar=eb[:, last:last + 1], in1=ps[:, 5 + q % 2, 0:DV],
                                             op0=ALU.mult, op1=ALU.add).then_inc(g_s, 1)
                for j in range(NT):
                    wait_alone(dve, g_ap, h * NT + (j + 1))
                    if j < NFULL:
                        dve.copy_predicated(attm[j % 2][:], mp[:], ps[:, 7, 0:P]).then_inc(g_am, 1)
                    else:
                        dve.copy_predicated(attd[:], md[:], ps[0:NDEC, 7, 0:NDEC]).then_inc(g_am, 1)
                dve.wait_ge(g_rt, h + 1)
                dve.reciprocal(oss[:], ors[:])
                dve.drain()
                for j in range(NT):
                    dve.scalar_tensor_tensor(out=og[:, j, :], in0=og[:, j, :], scalar=oss[:, j:j + 1], in1=rt[:, j, :],
                                             op0=ALU.mult, op1=ALU.mult).then_inc(g_n, 1)
            with dve.Fori(0, HEADS) as h:
                gla(h)
            barrier(dve, 3)

            def low_z(st):
                dve.wait_ge(z_hi, st.n + 1)
                one = bass.ds(st.n, 1)
                dve.tensor_tensor(ZL[:, one, :].rearrange("p a n -> p (a n)"), zr[st.s], ZH[:, one, :].rearrange("p a n -> p (a n)").bitcast(F32),
                                  ALU.subtract).then_inc(z_lo, 1)
            steps(dve, low_z, 16)

            def gate(st):
                s, n = st.s, st.n
                if st.first and s == 0:
                    low_p(st)
                if st.ahead(1).within(KD):
                    low_p(st.ahead(1))
                wait_alone(dve, sg_in, n * 48 + 48)
                for b in range(3):
                    bank = 3 * ((s * 3 + b) % 2)
                    dve.drain()
                    dve.wait_ge(p_mm, n * 3 + (b + 1))
                    for to, frm in ((slice(0, 768), None), (slice(768, NTOK), 2)):
                        src = ps[:, bank:bank + 2, 0:384] if frm is None else ps[:, bank + 2, 0:320]
                        g = sg[:, b, to] if frm else sg[:, b, to].rearrange("p (g n) -> p g n", g=2)
                        out = ymix[s] if b == 0 else yt
                        out = out[:, to] if frm else out[:, to].rearrange("p (g n) -> p g n", g=2)
                        last = dve.tensor_tensor(out, src, g, ALU.mult)
                    last.then_inc(p_ev, 1)
                    dve.drain()
                    if b:
                        last = dve.tensor_tensor(ymix[s][:], ymix[s][:], yt[:], ALU.add)
                last.then_inc(mix_ready, 1)

            def low_p(st):
                dve.wait_ge(p_hi, st.n + 1)
                dve.tensor_tensor(PL[st.s][:], PR[:], PH[st.s][:].bitcast(F32), ALU.subtract).then_inc(p_lo, 1)
            steps(dve, gate, KD, ends=True)
            barrier(dve, 4)

            dve.wait_ge(wo_hi, 1)
            dve.tensor_tensor(WOL[:], WOR[:], WOH[:].bitcast(F32), ALU.subtract).then_inc(wo_lo, 1)
            dve.wait_ge(r4_in, 80)

            def low_m(st, rows):
                dve.wait_ge(m_hi, st.n + 1)
                dve.tensor_tensor(ML[st.s][:, :, 0:rows], MR[st.s][:, :, 0:rows], MH[st.s][:, :, 0:rows].bitcast(F32), ALU.subtract).then_inc(m_lo, 1)
            low_m(Step(0, 0), P)

            def resid(st, rows):
                n, s = st.n, st.s
                dve.wait_ge(o_mm, n + 1)
                if not st.first:
                    dve.wait_ge(n2_st[s], st.t * 32)
                dve.tensor_tensor(X2[s][0:rows], ps[0:rows, 2 * s:2 * s + 2, :].rearrange("p b n -> p (b n)"), X4[s][0:rows], ALU.add).then_inc(x2_ready, 1)
                dve.wait_ge(x2_rms, n + 1)
                dve.reciprocal(rs4[0:rows], rt4[0:rows])
                dve.drain()
                dve.scalar_tensor_tensor(out=N2[s][0:rows], in0=X2[s][0:rows], scalar=rs4[0:rows], in1=g2b[0:rows], op0=ALU.mult, op1=ALU.mult).then_inc(n2_ready, 1)
                dve.wait_ge(l_mm, n + 1)
                dve.tensor_tensor(lgt[0:rows, bass.ds(n, 1), :].rearrange("p a c -> p (a c)"), ps[0:rows, 6, 0:GROUPS + NE], rb[0:rows], ALU.add).then_inc(l_ready, 1)

            def out_tile(st):
                low_m(st.ahead(1), P)
                resid(st, P)
            steps(dve, out_tile, NFULL - 2)
            last = Step(NFULL // 2 - 1, 0)
            out_tile(last)
            low_m(Step(NFULL // 2, 0), NDEC)
            resid(last.ahead(1), P)
            resid(Step(NFULL // 2, 0), NDEC)
            barrier(dve, 5)

            lg, lx = lgt[:, :, 0:GROUPS], lgt[:, :, GROUPS:]
            wide = [P, NT, GROUPS]
            dve.wait_ge(r_c, 1)

            def onehot(out, vals, mx, tmp, n):
                dve.tensor_tensor(tmp[:], vals, mx[:].to_broadcast([P, NT, n]), ALU.is_equal)
                dve.drain()
                dve.scalar_tensor_tensor(out=tmp[:], in0=tmp[:], scalar=-1000.0, in1=ioE[:, :, 0:n], op0=ALU.mult, op1=ALU.add)
                dve.drain()
                dve.tensor_reduce(gmn[:], tmp[:], AX.X, ALU.min)
                dve.drain()
                dve.tensor_tensor(out[:], tmp[:], gmn[:].to_broadcast([P, NT, n]), ALU.is_equal)
                dve.drain()

            dve.tensor_reduce(gmx[:], lg, AX.X, ALU.max)
            dve.drain()
            dve.tensor_tensor(gva[:], lg, gmx[:].to_broadcast(wide), ALU.subtract).then_inc(r_mx, 1)
            onehot(ohg, lg, gmx, gtm, GROUPS)
            dve.tensor_scalar(gtm[:], ohg[:], -1.0, 1e30, ALU.add, ALU.mult)
            dve.drain()
            for g in range(GROUPS):
                dve.tensor_tensor(le[:, :, g * EPG:(g + 1) * EPG], lx[:, :, g * EPG:(g + 1) * EPG],
                                  gtm[:, :, g:g + 1].to_broadcast([P, NT, EPG]), ALU.add)
            dve.drain()
            for k in range(2):
                dve.tensor_reduce(v12[k][:], le[:], AX.X, ALU.max)
                dve.drain()
                onehot(oh[k], le[:], v12[k], ev, NE)
                if k == 0:
                    dve.scalar_tensor_tensor(out=le[:], in0=oh[0][:], scalar=-2e30, in1=le[:], op0=ALU.mult, op1=ALU.add)
                    dve.drain()
            dve.tensor_tensor(gd[:], v12[1][:], v12[0][:], ALU.subtract).then_inc(r_d, 1)
            dve.wait_ge(r_ex, 1)
            dve.tensor_reduce(gsm[:], gex[:], AX.X, ALU.add)
            dve.wait_ge(r_e2, 1)
            dve.tensor_scalar(gr[:], gd[:], 1.0, None, ALU.add)
            dve.drain()
            dve.tensor_tensor(gr[:], gr[:], gsm[:], ALU.mult)
            dve.drain()
            dve.reciprocal(gsm[:], gr[:])
            dve.drain()
            dve.tensor_copy(gates[:, :, 0:1], gsm[:])
            dve.tensor_tensor(gates[:, :, 1:2], gsm[:], gd[:], ALU.mult)
            dve.tensor_tensor(msk[:], oh[0][:], oh[1][:], ALU.add)
            dve.memset(cum[:, 0, :], 0.0)
            dve.drain()
            dve.memset(msk[NDEC:P, NFULL, :], 0.0)
            dve.drain()
            for t in range(1, NT):
                dve.tensor_tensor(cum[:, t, :], cum[:, t - 1, :], msk[:, t - 1, :], ALU.add)
                dve.drain()
            dve.tensor_tensor(tot[:], cum[:, NFULL, :], msk[:, NFULL, :], ALU.add)
            dve.drain().then_inc(r_msk, 1)
            dve.wait_ge(r_mm, 1)
            half = NT * NE // 2
            rf = rank[:].rearrange("p t e -> p (t e)")
            dve.tensor_copy(rf[:, 0:half], ps[:, 0, 0:half])
            dve.tensor_copy(rf[:, half:], ps[:, 1, 0:half])
            dve.tensor_copy(cnt[:], ps[:, 2, 0:NE])
            dve.drain()
            dve.tensor_scalar(hib[:], rank[:], float(P), None, ALU.is_ge)
            dve.tensor_scalar(ovf[:], cnt[:], float(P), None, ALU.is_gt)
            for j in range(2, KMAX):
                dve.drain()
                dve.scalar_tensor_tensor(out=hib[:], in0=rank[:], scalar=float(P * j), in1=hib[:], op0=ALU.is_ge, op1=ALU.add)
                dve.scalar_tensor_tensor(out=ovf[:], in0=cnt[:], scalar=float(P * j), in1=ovf[:], op0=ALU.is_gt, op1=ALU.add)
            dve.drain()
            dve.tensor_tensor_scan(ove[:], one64[:], ovf[:], 0.0, ALU.mult, ALU.add)
            dve.drain()
            dve.tensor_tensor(stw[:], ove[:], ovf[:], ALU.subtract)
            dve.drain()
            dve.tensor_tensor(stw[:], stw[:], ioE[:, 0, :], ALU.subtract)
            dve.drain()
            dve.tensor_scalar(stw[:], stw[:], float(NE - 1), None, ALU.add)
            dve.tensor_scalar(tE[:], hib[:], 0.0, None, ALU.is_gt)
            dve.drain()
            dve.tensor_tensor(tE[:], tE[:], stw[:].rearrange("p (a e) -> p a e", a=1).to_broadcast([P, NT, NE]), ALU.mult)
            dve.drain()
            dve.tensor_tensor(tE[:], tE[:], hib[:], ALU.add)
            dve.scalar_tensor_tensor(out=rank[:], in0=hib[:], scalar=-float(P), in1=rank[:], op0=ALU.mult, op1=ALU.add)
            dve.drain()
            dve.tensor_tensor(tE[:], tE[:], ioE[:], ALU.add)
            dve.drain()
            dve.scalar_tensor_tensor(out=tE[:], in0=rank[:], scalar=float(NBLK), in1=tE[:], op0=ALU.mult, op1=ALU.add)
            dve.drain()
            for k in range(2):
                dve.tensor_tensor(oh[k][:], oh[k][:], tE[:], ALU.mult)
                dve.drain()
                dve.tensor_reduce(dst[:, k, :], oh[k][:], AX.X, ALU.add)
            dve.drain()
            for k in range(2):
                dve.memset(dst[NDEC:P, k, NFULL:NT], float(NOWHERE))
            dve.drain()
            dve.tensor_copy(dsti[:], dst[:])
            dve.drain().then_inc(r_dst, 1)
            dve.tensor_tensor(ovx[:], ove[0:1, :].rearrange("p (a e) -> p a e", a=1).to_broadcast([1, NOVF, NE]), ioV[:], ALU.is_le)
            dve.drain()
            dve.tensor_reduce(ovn[:, 0:NOVF], ovx[:], AX.X, ALU.add)
            dve.tensor_copy(ovn[:, NOVF:NOVF + 1], ove[0:1, NE - 1:NE])
            dve.drain()
            dve.tensor_scalar(ovn[:, 0:NOVF], ovn[:, 0:NOVF], float(NE - 1), None, ALU.min)
            dve.drain()
            dve.tensor_copy(eovf[:], ovn[:])
            dve.wait_ge(r_ld, 16)
            dve.tensor_scalar(tidx[:], sidx[:], 1, None, ALU.arith_shift_right)
            dve.drain()
            barrier(dve, 6)

            def low1(st):
                dve.wait_ge(e1_hi, st.n + 1)
                dve.tensor_tensor(E1L[st.s][:], E1[st.s][:], E1H[st.s][:].bitcast(F32), ALU.subtract).then_inc(e1_lo, 1)

            def low2(st):
                dve.wait_ge(e2_hi, st.n + 1)
                dve.tensor_tensor(E2L[st.s][:], E2[st.s][:], E2H[st.s][:].bitcast(F32), ALU.subtract).then_inc(e2_lo, 1)

            def x_lo(st):
                dve.wait_ge(xth, st.n + 1)
                dve.tensor_tensor(XTL[st.s][:], ps[:, 0:2, :].rearrange("p b (k t) -> p (b k) t", k=4), XTH[st.s][:].bitcast(F32), ALU.subtract).then_inc(xtl, 1)

            def hidden(st):
                dve.wait_ge(h_sig, st.n + 1)
                if not (st.first and st.s == 0):
                    dve.wait_ge(h_tp, st.n)
                dve.tensor_tensor(hid[:], ps[:, 2 + st.s, DE:2 * DE], sil[:], ALU.mult).then_inc(h_ready, 1)

            def h_lo(st):
                dve.wait_ge(hth, st.n + 1)
                dve.tensor_tensor(HTL[:], ps[:, 4, 0:2 * P].rearrange("p (a t) -> p a t", a=2), HTH[:].bitcast(F32), ALU.subtract).then_inc(htl, 1)
            low1(Step(0, 0))
            low2(Step(0, 0))
            x_lo(Step(0, 0))

            def expert(st):
                nxt = st.ahead(1)
                more = nxt.within(NE)
                if more:
                    low1(nxt)
                hidden(st)
                if more:
                    low2(nxt)
                    x_lo(nxt)
                h_lo(st)
            steps(dve, expert, NE, ends=True)
            barrier(dve, 7)
            n_more = dve.value_load(eovf[0:1, NOVF:NOVF + 1], min_val=0, max_val=NOVF)
            with dve.If(n_more > 0):
                with dve.Fori(0, n_more) as j:
                    st = More(j)
                    low1(st)
                    low2(st)
                    x_lo(st)
                    hidden(st)
                    h_lo(st)
            barrier(dve, 8)

            dve.wait_ge(c_g, 16)

            def combine(st, rows):
                n, s = st.n, st.s
                dve.wait_ge(c_in[s], st.t * 32 + 32)
                dve.tensor_copy(gt6[s][:], gates[:, bass.ds(n, 1), :].rearrange("p a k -> p (a k)"))
                dve.drain()
                if not st.first:
                    dve.wait_ge(c_out, n - 1)
                dve.scalar_tensor_tensor(out=FS[s][0:rows], in0=FY[s][0:rows, 0, :], scalar=gt6[s][0:rows, 0:1], in1=FX[s][0:rows], op0=ALU.mult, op1=ALU.add)
                dve.drain()
                dve.scalar_tensor_tensor(out=FS[s][0:rows], in0=FY[s][0:rows, 1, :], scalar=gt6[s][0:rows, 1:2], in1=FS[s][0:rows], op0=ALU.mult, op1=ALU.add)
                dve.drain().then_inc(c_sum, 1)
                dve.wait_ge(c_rms, n + 1)
                dve.reciprocal(rs6[0:rows], rt6[0:rows])
                dve.drain()
                if not st.first:
                    dve.wait_ge(c_st[s], st.t * 16)
                dve.scalar_tensor_tensor(out=FO[s][0:rows], in0=FS[s][0:rows], scalar=rs6[0:rows], in1=gfb[0:rows], op0=ALU.mult, op1=ALU.mult).then_inc(c_out, 1)
            token_tiles(dve, combine)
            barrier(dve, 9)

        @block.tensor
        def _(pe):
            pe.wait_ge(s_const, 1)

            def norm1(st, rows):
                n, s = st.n, st.s
                pe.wait_ge(xn_ready, n + 1)
                if not st.first:
                    pe.wait_ge(xl_ready, n - 1)
                for k in range(KD):
                    last = pe.transpose(xpos(s)[:, k, 0:rows], XN[s][0:rows, k * P:(k + 1) * P], ident[0:rows, 0:rows])
                last.then_inc(xt_done, 1)
            token_tiles(pe, norm1)
            pe.wait_ge(xl_ready, NT)

            def three(out, hi, lo, mhi, mlo, start, stop):
                pe.matmul(out, hi, mhi, start=start, stop=False)
                pe.matmul(out, hi, mlo, start=False, stop=False)
                return pe.matmul(out, lo, mhi, start=False, stop=stop)

            def t_chunk(col, st, all_, here):
                s = st.s
                pe.wait_ge(wl_ready, all_.n + 1)
                for tile in range(NT):
                    rows = rows_of(tile)
                    u = s * NT + tile
                    if not (all_.first and u < 6):
                        pe.wait_ge(t_ev, all_.n * NT + tile - 5)
                    cols = slice(tile * P, tile * P + rows)
                    for k in range(KD):
                        last = three(ps[0:rows, u % 6, 0:CW], XH[:, k, cols], XL[:, k, cols], WH[s][:, k, :], WL[s][:, k, :],
                                     k == 0, k == KD - 1)
                    last.then_inc(t_mm, 1)
                    if tile == NT - 1:
                        pe.drain().then_inc(w_used, 1)
            chunks(pe, T_TURNS, 0, t_chunk)

            def feature(f, wh, wl, nk, xh, xl):
                for k in range(nk):
                    for i, (w, x) in enumerate(((wh, xh), (wh, xl), (wl, xh))):
                        for g, (t0, tn) in enumerate(TG):
                            last = pe.matmul(ps[:, 3 * f + g, 0:tn], w[:, k, :], x[:, k, t0:t0 + tn],
                                             start=(k == 0 and i == 0), stop=(k == nk - 1 and i == 2))
                return last

            def f_chunk(col, st, all_, here):
                s = st.s
                pe.wait_ge(wl_ready, all_.n + 1)
                for f in range(2):
                    if here.first and here.s == 0:
                        pe.wait_ge(t_ev, NTC * NT)
                    else:
                        pe.wait_ge(f_ev, here.n * 2 + (f - 1))
                    last = feature(f, WH[s][:, :, f * P:(f + 1) * P], WL[s][:, :, f * P:(f + 1) * P], KD, XH, XL)
                    last.then_inc(f_mm, 1)
                pe.drain().then_inc(w_used, 1)
            chunks(pe, F_TURNS, NTC // 2, f_chunk)
            pe.wait_ge(a_lo, 1)
            pe.wait_ge(f_ev, 2 * NFC - 1)
            feature(0, WH[0][:, :, 0:P], WL[0][:, :, 0:P], KD, XH, XL).then_inc(a_mm, 1)
            barrier(pe, 1)

            pe.wait_ge(cm_tri, 2)
            for g in range(NCH):
                last = pe.transpose(ps[:, 0, g * P:(g + 1) * P], wsn[:, g, :], ident[:])
            last.then_inc(cm_wt, 1)
            for g in range(NCH):
                last = pe.transpose(ps[0:NDEC, 1, g * NDEC:(g + 1) * NDEC], wsd[:, g, :], ident[0:NDEC, 0:NDEC])
            last.then_inc(cm_wt, 1)
            pe.wait_ge(cm_v, 1)
            pe.wait_ge(cm_wc, 2)
            for c in range(NCH):
                if c:
                    pe.wait_ge(cm_z, c)
                for t in range(NFULL):
                    pe.matmul(ps[:, 2 + t // 4, (t % 4) * P:(t % 4 + 1) * P], vvt[:, t, c * P:(c + 1) * P], wsT[:, c, :], start=True, stop=True)
                pe.matmul(ps[:, 4, 0:NDEC], vvt[0:NDEC, NFULL, c * P:(c + 1) * P], wsdT[:, c, :], start=True, stop=True).then_inc(cm_mm, 1)
            barrier(pe, 2)

            def gla(h):
                pe.wait_ge(g_in, h * 144 + 144)
                for g, (t0, tn) in enumerate(TG):
                    last = pe.matmul(ps[:, g, 0:tn], a2h[:], alr[:, t0:t0 + tn], start=True, stop=True)
                last.then_inc(g_a, 1)
                pe.wait_ge(g_q, h + 1)
                per = NCHUNK + DEC_B

                def k_transpose(j):
                    rows = rows_of(j)
                    if j >= 2:
                        wait_alone(pe, g_kc, h * NT + (j - 1))
                    pe.transpose(ps[0:rows, 3 + j % 2, 0:P], ke[:, j * P:j * P + rows], ident[:]).then_inc(g_kp, 1)
                k_transpose(0)
                for j in range(NFULL):
                    k_transpose(j + 1)
                    pe.wait_ge(g_kc, h * NT + (j + 1))
                    for c in (2 * j, 2 * j + 1):
                        lo = (c % 2) * CHUNK
                        if c >= 2:
                            pe.wait_ge(g_s, h * per + (c - 1))
                        pe.matmul(ps[:, 5 + c % 2, 0:DV], ket[j % 2][lo:lo + CHUNK, :], vt[lo:lo + CHUNK, j, :], start=True, stop=True).then_inc(g_u, 1)
                pe.wait_ge(g_kz, h + 1)
                for q in range(DEC_B):
                    pe.wait_ge(g_s, h * per + (NCHUNK + q - 1))
                    pe.matmul(ps[:, 5 + q % 2, 0:DV], kz[:, q, :], vt[0:NDEC, NFULL, :], start=True, stop=True).then_inc(g_u, 1)

                def scores(j):
                    rows = rows_of(j)
                    if j:
                        pe.wait_ge(g_am, h * NT + j)
                    cols = slice(j * P, j * P + rows)
                    pe.matmul(ps[0:rows, 7, 0:rows], kt[:, cols], qt[:, cols], start=True, stop=True).then_inc(g_ap, 1)
                scores(0)
                for j in range(NT):
                    if j >= 2:
                        pe.wait_ge(g_oc, h * NT + (j - 1))
                    wait_alone(pe, g_am, h * NT + (j + 1))
                    if j < NFULL:
                        pe.matmul(ps[:, j % 2, 0:DV], attm[j % 2][:], vt[:, j, :], start=True, stop=False)
                        pe.matmul(ps[0:CHUNK, j % 2, 0:DV], qt[:, j * P:j * P + CHUNK], S[:, 2 * j, :], start=False, stop=True)
                        pe.matmul(ps[CHUNK:P, j % 2, 0:DV], qt[:, j * P + CHUNK:(j + 1) * P], S[:, 2 * j + 1, :], start=False, stop=True).then_inc(g_o, 1)
                        scores(j + 1)
                    else:
                        pe.matmul(ps[0:NDEC, j % 2, 0:DV], attd[:], vt[0:NDEC, j, :], start=True, stop=False)
                        for q in range(DEC_B):
                            last = pe.matmul(ps[0:NDEC, j % 2, 0:DV], qz[:, q, :], Sd[:, q, :], start=False, stop=(q == DEC_B - 1))
                        last.then_inc(g_o, 1)
                for j in range(NT):
                    rows = rows_of(j)
                    if j >= 2:
                        pe.wait_ge(g_tc, h * NT + (j - 1))
                    wait_alone(pe, g_n, h * NT + (j + 1))
                    for a in range(2):
                        last = pe.transpose(ps[:, 2 + j % 2, a * P:a * P + rows], og[0:rows, j, a * P:(a + 1) * P], ident[0:rows, 0:rows])
                    last.then_inc(g_tp, 1)
            with pe.Fori(0, HEADS) as h:
                gla(h)
            barrier(pe, 3)

            pe.wait_ge(z_lo, 16)

            def project(st):
                s, n = st.s, st.n
                pe.wait_ge(p_lo, n + 1)
                for b, (k0, kn) in enumerate(((0, 4), (4, 8), (12, 4))):
                    if not (st.first and s == 0 and b < 2):
                        pe.wait_ge(p_ev, n * 3 + (b - 1))
                    f = (s * 3 + b) % 2
                    feature(f, PH[s][:, k0:k0 + kn, :], PL[s][:, k0:k0 + kn, :], kn, ZH[:, k0:k0 + kn, :], ZL[:, k0:k0 + kn, :]).then_inc(p_mm, 1)
            steps(pe, project, KD)
            barrier(pe, 4)

            pe.wait_ge(wo_lo, 1)
            pe.wait_ge(r4_in, 80)

            def out_mm(st, rows):
                n, s = st.n, st.s
                pe.wait_ge(m_lo, n + 1)
                if not st.first:
                    pe.wait_ge(x2_ready, n - 1)
                for b in range(2):
                    for k in range(KD):
                        c = slice(b * 512, (b + 1) * 512)
                        last = three(ps[0:rows, 2 * s + b, :], MH[s][:, k, 0:rows], ML[s][:, k, 0:rows], WOH[:, k, c], WOL[:, k, c], k == 0, k == KD - 1)
                last.then_inc(o_mm, 1)

            def router(st, rows):
                n, s = st.n, st.s
                pe.wait_ge(n2_ready, n + 1)
                if not (st.first and s == 0):
                    pe.wait_ge(n2_tc, n)
                tp = ps[:, 4:6, :].rearrange("p b (k t) -> p (b k) t", k=4)
                for k in range(KD):
                    last = pe.transpose(tp[:, k, 0:rows], N2[s][0:rows, k * P:(k + 1) * P], ident[0:rows, 0:rows])
                last.then_inc(n2_tp, 1)
                pe.wait_ge(n2_tc, n + 1)
                if not (st.first and s == 0):
                    pe.wait_ge(l_ready, n)
                for k in range(KD):
                    last = pe.matmul(ps[0:rows, 6, 0:GROUPS + NE], NTt[:, k, 0:rows], wr[:, k, :], start=(k == 0), stop=(k == KD - 1))
                last.then_inc(l_mm, 1)
            out_mm(Step(0, 0), P)

            def out_tile(st):
                out_mm(st.ahead(1), P)
                router(st, P)
            steps(pe, out_tile, NFULL - 2)
            last4 = Step(NFULL // 2 - 1, 0)
            out_tile(last4)
            out_mm(Step(NFULL // 2, 0), NDEC)
            router(last4.ahead(1), P)
            router(Step(NFULL // 2, 0), NDEC)
            barrier(pe, 5)

            pe.wait_ge(r_c, 1)
            pe.wait_ge(r_msk, 1)
            half = NT * NE // 2
            mflat, cflat = msk[:].rearrange("p t e -> p (t e)"), cum[:].rearrange("p t e -> p (t e)")
            for b in range(2):
                c = slice(b * half, (b + 1) * half)
                pe.matmul(ps[:, b, 0:half], ltri[:], mflat[:, c], start=True, stop=False)
                pe.matmul(ps[:, b, 0:half], onesm[:], cflat[:, c], start=False, stop=True)
            pe.matmul(ps[:, 2, 0:NE], onesm[:], tot[:], start=True, stop=True).then_inc(r_mm, 1)
            barrier(pe, 6)

            xgp = ps[:, 0:2, :].rearrange("p b (k t) -> p (b k) t", k=4)

            def x_t(st):
                n, s = st.n, st.s
                pe.wait_ge(xg_in[s], st.t * 16 + 16)
                if not (st.first and s == 0):
                    pe.wait_ge(xtl, n)
                xg = XG[s][:].rearrange("p (q k) -> p k q", k=KD)
                for k in range(KD):
                    last = pe.transpose(xgp[:, k, :], xg[:, k, :], ident[:])
                last.then_inc(xg_tp, 1)

            def h_mul(st):
                n, s = st.n, st.s
                pe.wait_ge(xtl, n + 1)
                pe.wait_ge(e1_lo, n + 1)
                if not st.first:
                    pe.wait_ge(h_ready, n - 1)
                for k in range(KD):
                    last = three(ps[:, 2 + s, :], XTH[s][:, k, :], XTL[s][:, k, :], E1H[s][:, k].rearrange("p a c -> p (a c)"),
                                 E1L[s][:, k].rearrange("p a c -> p (a c)"), k == 0, k == KD - 1)
                last.then_inc(h_mm, 1)

            def h_t(st):
                n = st.n
                pe.wait_ge(h_ready, n + 1)
                if not (st.first and st.s == 0):
                    pe.wait_ge(htl, n)
                hv = hid[:].rearrange("p (q k) -> p k q", k=2)
                for k in range(2):
                    last = pe.transpose(ps[:, 4, k * P:(k + 1) * P], hv[:, k, :], ident[:])
                last.then_inc(h_tp, 1)

            def y_mul(st):
                n, s = st.n, st.s
                pe.wait_ge(htl, n + 1)
                pe.wait_ge(e2_lo, n + 1)
                if not (st.first and s == 0):
                    pe.wait_ge(y_ready, n)
                for b in range(2):
                    for k in range(2):
                        c = slice(b * 512, (b + 1) * 512)
                        last = three(ps[:, 5 + b, :], HTH[:, k, :], HTL[:, k, :], E2H[s][:, k, c], E2L[s][:, k, c], k == 0, k == 1)
                last.then_inc(y_mm, 1)
            x_t(Step(0, 0))

            def expert(st):
                h_mul(st)
                if st.ahead(1).within(NE):
                    x_t(st.ahead(1))
                if st.ahead(-1).within(NE):
                    y_mul(st.ahead(-1))
                h_t(st)
            steps(pe, expert, NE, ends=True)
            y_mul(Step(NE // 2 - 1, 1))
            barrier(pe, 7)
            n_more = pe.value_load(eovf[0:1, NOVF:NOVF + 1], min_val=0, max_val=NOVF)
            with pe.If(n_more > 0):
                with pe.Fori(0, n_more) as j:
                    st = More(j)
                    x_t(st)
                    h_mul(st)
                    h_t(st)
                    y_mul(st)
            barrier(pe, 8)
            barrier(pe, 9)


_INS = ['x_prompt', 'x_sample', 'state_conv', 'state_gla', 'norm1_g', 'w_in', 'conv_w', 'gla_a2', 'gla_a_b',
        'gla_norm_g', 'cm_norm_g', 'cm_ws', 'cm_b', 'proj_a', 'proj_b', 'proj_c', 'w_out', 'norm2_g',
        'router_group_w', 'router_group_b', 'router_expert_w', 'router_expert_b',
        'exp_w1', 'exp_w3', 'exp_w2', 'final_norm_g']
_OUTS = [(1, SEQ, D), (DEC_B, DEC_T, D), (1, 1, 2, CONV_CH), (1, 1, HEADS, DK, DV),
         (1, DEC_B, 2, CONV_CH), (1, DEC_B, HEADS, DK, DV), (1, DEC_B, DEC_T, CONV_CH)]


def kernel(**inputs):
    import numpy as _np
    import concourse.bacc as _bacc
    from concourse import mybir as _mybir
    from concourse.bass_utils import run_bass_kernel_spmd as _run

    nc = _bacc.Bacc("TRN2", target_bir_lowering=False, num_devices=1)
    arrays, args = {}, []
    for name in _INS:
        a = _np.ascontiguousarray(inputs[name])
        arrays[f"in_{name}_dram"] = a
        args.append(nc.dram_tensor(f"in_{name}_dram", a.shape, _mybir.dt.from_np(a.dtype), kind="ExternalInput").ap())
    for i, shape in enumerate(_OUTS):
        args.append(nc.dram_tensor(f"out_{i}_dram", shape, _mybir.dt.float32, kind="ExternalOutput").ap())
    trunk(nc, *args)
    r = _run(nc, [arrays], core_ids=[0])
    return tuple(r.results[0][f"out_{i}_dram"] for i in range(len(_OUTS)))
```

```python
import concourse.bass as bass
from concourse import mybir
from contextlib import ExitStack

F32 = mybir.dt.float32
F32R = mybir.dt.float32r
I32 = mybir.dt.int32
ALU = mybir.AluOpType
ACT = mybir.ActivationFunctionType
AX = mybir.AxisListType

P = 128
D = 1024
KD = D // P
SEQ = 1024
DEC_B, DEC_T = 8, 8
NDEC = DEC_B * DEC_T
NTOK = SEQ + NDEC
NFULL = SEQ // P
NT = NFULL + 1
CONV_CH = 512
NCH = CONV_CH // P
HEADS, DK, DV = 4, 128, 256
CHUNK = 64
NCHUNK = SEQ // CHUNK
TAU = 16.0
LOWRANK = 16
GROUPS, EPG = 8, 8
NE = GROUPS * EPG
DE = 256
EPS = 1e-6
C_H, C_CG, C_BG, C_Q, C_K = 0, 512, 1024, 1536, 2048
C_V, C_R, C_A, C_U, C_VV, C_G = 2560, 3584, 4608, 4624, 5136, 5648
D_IN = 8720
CW = 256
TG = [(0, 384), (384, 384), (768, 320)]
NPAD = NT * P
BR = 64
NSLOT = 2 * NTOK
NOVF = (NSLOT - 1) // BR
NBLK = NE + NOVF
NOWHERE = 1 << 20
EMPTY = 4 * NTOK
BR_BITS = BR.bit_length() - 1


def rows_of(tile):
    return P if tile < NFULL else NDEC


def trunk(nc, x_prompt, x_sample, state_conv, state_gla, norm1_g, w_in, conv_w, gla_a2, gla_a_b,
          gla_norm_g, cm_norm_g, cm_ws, cm_b, proj_a, proj_b, proj_c, w_out, norm2_g,
          rg_w, rg_b, re_w, re_b, exp_w1, exp_w3, exp_w2, final_g,
          y_prompt, y_sample, conv_p, gla_p, conv_s, gla_s, chunk_v):
    def dram(name, shape, dt=F32):
        return nc.dram_tensor(name, shape, dt, kind="Internal").ap()

    feat = dram("feat", (D_IN, NTOK))
    tokd = dram("tokd", (NTOK, 2560))
    zT = dram("zT", (16 * P, NTOK))
    mixT = dram("mixT", (D, NTOK))
    x2d = dram("x2d", (NTOK, D))
    xn2d = dram("xn2d", (NTOK, D))
    table = dram("slot_table", (BR * NBLK, 1), I32)
    yb = dram("yb", (NBLK * BR, D))

    xp = x_prompt[0]
    xs = x_sample.rearrange("a b n -> (a b) n")
    w_in_v = w_in[0].rearrange("(k p) c -> p k c", p=P)
    ctx = ExitStack()
    with ctx:
        def sem(name):
            return ctx.enter_context(nc.semaphore(name))

        def sem2(name):
            return [sem(f"{name}{i}") for i in range(2)]

        def sbuf(stack):
            return lambda name, shape, dt=F32: stack.enter_context(nc.sbuf_tensor(name, shape, dt))

        keep = sbuf(ctx)
        ident = keep("ident", [P, P])
        epsc = keep("epsc", [P, 1])
        yt = keep("yt", [P, NTOK])
        alr = yt[0:LOWRANK]
        gates = keep("gates", [P, NT, 2])
        lgt = keep("lgt", [P, NT, GROUPS + NE])
        tidx = keep("tidx", [BR, NBLK], I32)
        yrow = keep("yrow", [P, 2, NT], I32)
        eovf = keep("eovf", [1, NOVF + 1], I32)

        ph = ExitStack()
        sb = sbuf(ph)
        XH = sb("XH", [P, KD, NPAD], F32R)
        XL = sb("XL", [P, KD, NPAD], F32R)
        RAW = [sb(f"RAW{i}", [P, KD, CW]) for i in range(2)]
        WH = [sb(f"WH{i}", [P, KD, CW], F32R) for i in range(2)]
        WL = [sb(f"WL{i}", [P, KD, CW], F32R) for i in range(2)]
        OT = [sb(f"OT{i}", [P, NT, CW]) for i in range(2)]
        OF = [sb(f"OF{i}", [P, 2, NTOK]) for i in range(2)]
        g1b = sb("g1b", [P, D])
        X = [sb(f"X{i}", [P, D]) for i in range(2)]
        XN = [sb(f"XN{i}", [P, D]) for i in range(2)]
        ssq = [sb(f"ssq{i}", [P, 1]) for i in range(2)]
        rtt = [sb(f"rtt{i}", [P, 1]) for i in range(2)]
        rst = [sb(f"rst{i}", [P, 1]) for i in range(2)]
        junk = sb("junk", [P, D])
        junk2 = sb("junk2", [P, D])
        ph.close()

        ph = ExitStack()
        sb = sbuf(ph)
        cH = sb("cH", [P, NTOK])
        cG = sb("cG", [P, NTOK])
        cB = sb("cB", [P, NTOK])
        cwt = sb("cwt", [P, 3])
        cpp = sb("cpp", [P, 2 + SEQ])
        cps = sb("cps", [P, DEC_B, 2 + DEC_T])
        cout = sb("cout", [P, NTOK])
        za = sb("za", [P, NTOK])
        vvt = sb("vvt", [P, NT, CONV_CH])
        vsq = sb("vsq", [P, NT, CONV_CH])
        vss = sb("vss", [P, NT * NCH])
        vrs = sb("vrs", [P, NT * NCH])
        cmg = sb("cmg", [P, CONV_CH])
        wsn = sb("wsn", [P, NCH, P])
        wsd = sb("wsd", [NDEC, NCH, P])
        wsT = sb("wsT", [P, NCH, P])
        wsdT = sb("wsdT", [NDEC, NCH, NDEC])
        cmb = sb("cmb", [P, NCH, P])
        uT = sb("uT", [P, NTOK])
        zc = sb("zc", [P, NTOK])
        ph.close()
        ph = ExitStack()
        sb = sbuf(ph)
        a2h = sb("a2h", [LOWRANK, P])
        abh = sb("abh", [P, 1])
        qT = sb("qT", [P, NTOK])
        kT = sb("kT", [P, NTOK])
        vt = [sb(f"vt{i}", [P, NT, DV]) for i in range(2)]
        rt = [sb(f"rt{i}", [P, NT, DV]) for i in range(2)]
        rg = sb("rg", [P, DV])
        seg = sb("seg", [P, NTOK])
        zz = sb("zz", [P, NTOK])
        t1 = sb("t1", [P, NTOK])
        cs = sb("cs", [P, NTOK])
        eb = [sb(f"eb{i}", [P, NTOK]) for i in range(2)]
        qt = [sb(f"qt{i}", [P, NTOK]) for i in range(2)]
        kt = [sb(f"kt{i}", [P, NTOK]) for i in range(2)]
        ke = [sb(f"ke{i}", [P, NTOK]) for i in range(2)]
        qz = [sb(f"qz{i}", [P, DEC_B, NDEC]) for i in range(2)]
        ket = [sb(f"ket{i}", [P, P]) for i in range(2)]
        kz = sb("kz", [NDEC, DEC_B, P])
        rmask = sb("rmask", [NDEC, DEC_B])
        attm = [sb(f"attm{i}", [P, P]) for i in range(2)]
        attd = sb("attd", [NDEC, NDEC])
        mp = sb("mp", [P, P], I32)
        md = sb("md", [NDEC, NDEC], I32)
        mdf = sb("mdf", [NDEC, NDEC])
        mf = sb("mf", [P, P])
        S = sb("S", [P, NCHUNK + 1, DV])
        Sd = [sb(f"Sd{i}", [P, DEC_B, DV]) for i in range(2)]
        Sn = sb("Sn", [P, DEC_B, DV])
        osq = [sb(f"osq{i}", [P, DV]) for i in range(2)]
        og = [sb(f"og{i}", [P, DV]) for i in range(2)]
        oss = [sb(f"oss{i}", [P, 1]) for i in range(2)]
        ors = [sb(f"ors{i}", [P, 1]) for i in range(2)]
        orc = [sb(f"orc{i}", [P, 1]) for i in range(2)]
        zb = [sb(f"zb{i}", [P, 2, NTOK]) for i in range(2)]
        ph.close()

        ph = ExitStack()
        sb = sbuf(ph)
        ZH = sb("ZH", [P, 16, NTOK], F32R)
        ZL = sb("ZL", [P, 16, NTOK], F32R)
        PR = sb("PR", [P, 16, P])
        PH = [sb(f"PH{i}", [P, 16, P], F32R) for i in range(2)]
        PL = [sb(f"PL{i}", [P, 16, P], F32R) for i in range(2)]
        sg = sb("sg", [P, 3, NTOK])
        ymix = [sb(f"ymix{i}", [P, NTOK]) for i in range(2)]
        zr = [sg[:, 0, :], sg[:, 1, :]]
        ph.close()

        ph = ExitStack()
        sb = sbuf(ph)
        WOR = sb("WOR", [P, KD, D])
        WOH = sb("WOH", [P, KD, D], F32R)
        WOL = sb("WOL", [P, KD, D], F32R)
        MR = [sb(f"MR{i}", [P, KD, P]) for i in range(2)]
        MH = [sb(f"MH{i}", [P, KD, P], F32R) for i in range(2)]
        ML = [sb(f"ML{i}", [P, KD, P], F32R) for i in range(2)]
        X4 = [sb(f"X4{i}", [P, D]) for i in range(2)]
        X2 = [sb(f"X2{i}", [P, D]) for i in range(2)]
        N2 = [sb(f"N2{i}", [P, D]) for i in range(2)]
        NTt = sb("NTt", [P, KD, P])
        g2b = sb("g2b", [P, D])
        wr = sb("wr", [P, KD, GROUPS + NE])
        rb = sb("rb", [P, GROUPS + NE])
        ss4 = sb("ss4", [P, 1])
        rt4 = sb("rt4", [P, 1])
        rs4 = sb("rs4", [P, 1])
        sq4 = sb("sq4", [P, D])
        ph.close()

        ph = ExitStack()
        sb = sbuf(ph)
        iE = sb("iE", [P, NT, NE], I32)
        ioE = sb("ioE", [P, NT, NE])
        gmx = sb("gmx", [P, NT, 1])
        gsm = sb("gsm", [P, NT, 1])
        gmn = sb("gmn", [P, NT, 1])
        gex = sb("gex", [P, NT, GROUPS])
        gva = sb("gva", [P, NT, GROUPS])
        gtm = sb("gtm", [P, NT, GROUPS])
        ohg = sb("ohg", [P, NT, GROUPS])
        le = sb("le", [P, NT, NE])
        ev = sb("ev", [P, NT, NE])
        v12 = [sb(f"v{i}", [P, NT, 1]) for i in range(2)]
        gd = sb("gd", [P, NT, 1])
        gr = sb("gr", [P, NT, 1])
        oh = [sb(f"oh{i}", [P, NT, NE]) for i in range(2)]
        msk = sb("msk", [P, NT, NE])
        cum = sb("cum", [P, NT, NE])
        rank = sb("rank", [P, NT, NE])
        hib = sb("hib", [P, NT, NE])
        tE = sb("tE", [P, NT, NE])
        tot = sb("tot", [P, NE])
        cnt = sb("cnt", [P, NE])
        ovf = sb("ovf", [P, NE])
        ove = sb("ove", [P, NE])
        one64 = sb("one64", [P, NE])
        stw = sb("stw", [P, NE])
        dst = sb("dst", [P, 2, NT])
        ranki = sb("ranki", [P, NT, NE], I32)
        cnti = sb("cnti", [P, NE], I32)
        dsty = sb("dsty", [P, 2, NT])
        dsti = sb("dsti", [P, 2, NT], I32)
        slot = sb("slot", [P, NT], I32)
        ltri = sb("ltri", [P, P])
        onesm = sb("onesm", [P, P])
        emp = sb("emp", [BR, NBLK], I32)
        ovx = sb("ovx", [1, NOVF, NE])
        iV = sb("iV", [1, NOVF, NE], I32)
        ioV = sb("ioV", [1, NOVF, NE])
        ovn = sb("ovn", [1, NOVF + 1])
        ph.close()

        ph = ExitStack()
        sb = sbuf(ph)
        E1 = [sb(f"E1{i}", [P, 2, KD, DE]) for i in range(2)]
        E2 = [sb(f"E2{i}", [P, 2, D]) for i in range(2)]
        E1H = [sb(f"E1H{i}", [P, 2, KD, DE], F32R) for i in range(2)]
        E1L = [sb(f"E1L{i}", [P, 2, KD, DE], F32R) for i in range(2)]
        E2H = [sb(f"E2H{i}", [P, 2, D], F32R) for i in range(2)]
        E2L = [sb(f"E2L{i}", [P, 2, D], F32R) for i in range(2)]
        XG = [sb(f"XG{i}", [BR, D]) for i in range(2)]
        XTH = [sb(f"XTH{i}", [P, KD, P], F32R) for i in range(2)]
        XTL = [sb(f"XTL{i}", [P, KD, P], F32R) for i in range(2)]
        sil = sb("sil", [BR, DE])
        hid = sb("hid", [BR, DE])
        HTH = sb("HTH", [P, 2, P], F32R)
        HTL = sb("HTL", [P, 2, P], F32R)
        YS = [sb(f"YS{i}", [BR, D]) for i in range(2)]
        gix = [sb(f"gix{i}", [BR, 1], I32) for i in range(2)]
        ph.close()

        ph = ExitStack()
        sb = sbuf(ph)
        FX = [sb(f"FX{i}", [P, D]) for i in range(2)]
        FY = [sb(f"FY{i}", [P, 2, D]) for i in range(2)]
        FS = [sb(f"FS{i}", [P, D]) for i in range(2)]
        FO = [sb(f"FO{i}", [P, D]) for i in range(2)]
        gfb = sb("gfb", [P, D])
        jf = sb("jf", [P, D])
        gt6 = [sb(f"gt6{i}", [P, 2]) for i in range(2)]
        cix = [sb(f"cix{i}", [P, 2], I32) for i in range(2)]
        ss6 = sb("ss6", [P, 1])
        rt6 = sb("rt6", [P, 1])
        rs6 = sb("rs6", [P, 1])
        ph.close()

        ps = ctx.enter_context(nc.psum_tensor("ps", [P, 8, 512], F32))

        s_bar = sem("phase_done")
        s_const = sem("constants_ready")
        s_alone = {e.engine: sem(f"alone_{n}") for n, e in
                   (("sp", nc.sync), ("pool", nc.gpsimd), ("dve", nc.vector), ("pe", nc.tensor))}

        def barrier(eng, k):
            eng.drain().then_inc(s_bar, 1)
            eng.wait_ge(s_bar, 5 * k)

        def wait_alone(eng, sem_, value):
            eng.wait_ge(sem_, value)
            eng.sem_inc(s_alone[eng.engine], 1)

        def wait_if_any(eng, sem_, value):
            if not (isinstance(value, int) and value <= 0):
                eng.wait_ge(sem_, value)

        def turn_of(st, j):
            return (st.s * NT + j) % 2

        def xpos(s):
            return ps[:, 4 + 2 * s:6 + 2 * s, :].rearrange("p b (k t) -> p (b k) t", k=4)

        yz_ready, yz_st = sem("zeros_ready"), sem("zeros_stored")
        x_in, g1_in = sem2("x_in"), sem("norm1_gain_in")
        rms_ready, xn_ready, xt_done = sem("rms_ready"), sem("xn_ready"), sem("xn_transposed")
        xh_ready, xl_ready = sem("xh_ready"), sem("xl_ready")
        w_in_s = sem2("w_chunk_in")
        wh_ready, wl_ready, w_used = sem("wh_ready"), sem("wl_ready"), sem("w_used")
        t_mm, t_ev, t_st = sem("tok_product"), sem("tok_evacuated"), sem2("tok_stored")
        f_mm, f_ev, f_st = sem("feat_product"), sem("feat_evacuated"), sem2("feat_stored")
        a_in, a_hi, a_lo, a_mm = (sem(f"lowrank_{n}") for n in ("in", "hi", "lo", "product"))
        cv_in, cv_st, cv_z = sem("conv_in"), sem("conv_stored"), sem("conv_done")
        cm_in, cm_wd0, cm_tri, cm_w, cm_wt, cm_wc = (sem(f"mlp_{n}") for n in ("in", "diag_zeroed", "masked", "diag_in", "w_transposed", "w_copied"))
        cm_sq, cm_rt, cm_v, cm_mm, cm_z, cm_st, cm_u = (
            sem(f"mlp_{n}") for n in ("v_squares", "v_rms", "v_normed", "mixed", "done", "stored", "u_in"))
        g_in, g_pin, g_r = sem2("gla_in"), sem("gla_qk_in"), sem("gla_gain_in")
        g_c, g_a, g_zc, g_z, g_b, g_e, g_q = (
            sem(f"gla_{n}") for n in ("consts", "decay_product", "decay_copied", "decay_ln", "decay_sum", "decay_exp", "qk"))
        g_kp, g_kc, g_u, g_s = (sem(f"gla_{n}") for n in ("k_transposed", "k_copied", "update", "state"))
        g_ap, g_am, g_o = (sem(f"gla_{n}") for n in ("scores", "scores_masked", "out"))
        g_kz = sem("gla_k_masked")
        g_rg, g_rt, g_n, g_tp, g_tc = (sem(f"gla_{n}") for n in ("r_gain", "out_rms", "out_normed", "out_transposed", "done"))
        g_st, g_sv = sem2("gla_stored"), sem("gla_states_stored")
        z_in, z_hi, z_lo = sem2("z_in"), sem("z_hi"), sem("z_lo")
        p_in, p_hi, p_lo, p_mm, p_ev = (sem(f"proj_{n}") for n in ("in", "hi", "lo", "product", "gated"))
        sg_in, mix_ready, mix_st = sem("gate_in"), sem("mix_ready"), sem("mix_stored")
        wo_in, wo_hi, wo_lo, m_in, m_hi, m_lo = sem("wo_in"), sem("wo_hi"), sem("wo_lo"), sem2("mix_in"), sem("mix_hi"), sem("mix_lo")
        r4_in, o_mm, x2_ready, x2_rms, n2_ready, n2_tp, n2_tc, l_mm, l_ready = (
            sem(n) for n in ("router_in", "out_product", "x2_ready", "x2_rms", "xn2_ready", "xn2_transposed", "xn2_copied", "logit_product", "logits_ready"))
        n2_st = sem2("xn2_stored")
        r_c, r_mx, r_ex, r_d, r_e2, r_msk, r_mm, r_dst, r_tab, r_sc, r_ld = (
            sem(f"route_{n}") for n in ("consts", "group_max", "group_exp", "expert_diff", "expert_exp", "mask", "ranks", "rows", "table_empty", "table_filled", "table_in"))
        e_in = [sem2(f"expert_w{w}_in") for w in (1, 3, 2)]
        xg_in, y_st, i_gx = sem2("x_gathered"), sem2("y_stored"), sem("gather_index")
        e1_hi, e1_lo, e2_hi, e2_lo = sem("e1_hi"), sem("e1_lo"), sem("e2_hi"), sem("e2_lo")
        xg_tp, xth, xtl, h_mm, h_sig, h_ready, h_tp, hth, htl, y_mm, y_ready = (
            sem(f"e_{n}") for n in ("x_transposed", "x_hi", "x_lo", "h_product", "h_silu", "h_ready", "h_transposed", "h_hi", "h_lo", "y_product", "y_ready"))
        cy_in, c_ix = sem2("c_y_in"), sem("c_index")
        c_in, c_g, c_sum, c_rms, c_out, c_st = sem2("c_in"), sem("c_gain"), sem("c_sum"), sem("c_rms"), sem("c_out"), sem2("c_stored")

        class Step:
            def __init__(self, turn, slot):
                self.t, self.s, self.n = turn, slot, turn * 2 + slot
                self.static = isinstance(turn, int)
                self.first = self.static and turn == 0

            def ahead(self, d):
                return Step(self.t + (self.s + d) // 2, (self.s + d) % 2)

            def within(self, n):
                return not self.static or 0 <= self.n < n

        def steps(eng, body, n, ends=False):
            body(Step(0, 0))
            body(Step(0, 1))
            last = n // 2 - ends
            if last > 1:
                with eng.Fori(1, last) as t:
                    body(Step(t, 0))
                    body(Step(t, 1))
            if ends:
                body(Step(last, 0))
                body(Step(last, 1))
            if n % 2:
                body(Step(n // 2, 0))

        class More(Step):
            def __init__(self, j):
                self.t, self.s, self.n = j + NE // 2, 0, j + NE
                self.static = self.first = False

        def token_tiles(eng, body):
            steps(eng, lambda st: body(st, P), NFULL)
            body(Step(NFULL // 2, 0), NDEC)

        T_TURNS = [(C_V, 2), (C_R, 2), (C_VV, 1)]
        F_TURNS = [(C_H, 5), (C_U, 1), (C_G, 6)]
        NTC = 2 * sum(n for _, n in T_TURNS)
        NFC = 2 * sum(n for _, n in F_TURNS)

        def chunks(eng, all_turns, base, body):
            base0 = base
            for col, n in all_turns:
                lo = 0
                if base == base0 or n == 1:
                    for s in range(2):
                        body(col, Step(0, s), Step(base, s), Step(base - base0, s))
                    lo = 1
                if n > lo:
                    with eng.Fori(lo, n) as t:
                        for s in range(2):
                            body(col, Step(t, s), Step(t + base, s), Step(t + (base - base0), s))
                base += n

        def tok(t, rows=P):
            return slice(SEQ, NTOK) if rows < P else bass.ds(t * P, P)

        block = ctx.enter_context(nc.Block())
        ctx.enter_context(nc.allow_non_contiguous_dma(reason="short columns of weights and states"))

        @block.sync
        def _(sp):
            sp.dma_start(g1b[:], norm1_g[0:1, :].to_broadcast([P, D])).then_inc(g1_in, 16)

            def load_x(st, rows):
                if not st.first:
                    sp.wait_ge(xn_ready, st.n - 1)
                src = xs[:, :] if rows < P else xp[tok(st.n), :]
                sp.dma_start(X[st.s][0:rows], src).then_inc(x_in[st.s], 16)
            token_tiles(sp, load_x)

            def load_w(col, st, all_, here):
                if not all_.first:
                    sp.wait_ge(wl_ready, all_.n - 1)
                sp.dma_start(RAW[st.s][:], w_in_v[:, :, bass.ds(st.n * CW + col, CW)]).then_inc(w_in_s[st.s], 16)
            chunks(sp, T_TURNS, 0, load_w)
            chunks(sp, F_TURNS, NTC // 2, load_w)
            sp.wait_ge(wl_ready, NTC + NFC - 1)
            sp.dma_start(RAW[0][:, :, 0:P], w_in_v[:, :, C_A:C_A + P]).then_inc(a_in, 16)
            barrier(sp, 1)

            def conv(c, first=False):
                if not first:
                    sp.wait_ge(cv_st, c * 64)
                for to, base in ((cH, C_H), (cG, C_CG), (cB, C_BG)):
                    sp.dma_start(to[:], feat[bass.ds(c * P + base, P), :]).then_inc(cv_in, 16)
                sp.dma_start(cwt[:], conv_w[0][:, bass.ds(c * P, P)].rearrange("k p -> p k")).then_inc(cv_in, 16)
                for b in range(2):
                    sp.dma_start(cps[:, :, b], state_conv[0][:, b, bass.ds(c * P, P)].rearrange("s p -> p s")).then_inc(cv_in, 16)
                sp.wait_ge(cv_z, c + 1)
                sp.dma_start(zT[bass.ds(c * P, P), :], za[:]).then_inc(cv_st, 16)
                sp.dma_start(conv_p[0, 0][:, bass.ds(c * P, P)].rearrange("k p -> p k"), cpp[:, SEQ:SEQ + 2]).then_inc(cv_st, 16)
                for b in range(2):
                    sp.dma_start(conv_s[0][:, b, bass.ds(c * P, P)].rearrange("s p -> p s"),
                                 cps[:, :, DEC_T + b]).then_inc(cv_st, 16)
            conv(0, True)
            with sp.Fori(1, NCH) as c:
                conv(c)
            sp.wait_ge(cv_st, 64 * NCH)

            sp.wait_ge(cm_wd0, 2)
            sp.dma_start(vvt[:, 0:NFULL, :], tokd[0:SEQ, 2048:2560].rearrange("(t p) c -> p t c", p=P)).then_inc(cm_in, 16)
            sp.dma_start(vvt[0:NDEC, NFULL, :], tokd[SEQ:NTOK, 2048:2560]).then_inc(cm_in, 16)
            sp.dma_start(cmg[:], cm_norm_g[0:1].rearrange("a g c -> a (g c)").to_broadcast([P, CONV_CH])).then_inc(cm_in, 16)
            sp.dma_start(cmb[:].rearrange("p g t -> p (g t)"),
                         cm_b[0:1].rearrange("a g t -> a (g t)").to_broadcast([P, NCH * P])).then_inc(cm_in, 16)
            sp.dma_start(wsn[:], cm_ws[0].rearrange("g t s -> t g s")).then_inc(cm_w, 16)
            for q in range(DEC_B):
                sp.dma_start(wsd[q * DEC_T:(q + 1) * DEC_T, :, q * DEC_T:(q + 1) * DEC_T],
                             cm_ws[0][:, 0:DEC_T, 0:DEC_T].rearrange("g t s -> t g s")).then_inc(cm_w, 16)
            sp.wait_ge(cm_v, 1)
            sp.dma_start(chunk_v[0].rearrange("b t c -> (b t) c"), vvt[0:NDEC, NFULL, :]).then_inc(cm_st, 16)
            for c in range(NCH):
                if c:
                    sp.wait_ge(cm_z, c)
                sp.dma_start(uT[:], feat[C_U + c * P:C_U + (c + 1) * P, :]).then_inc(cm_u, 16)
                sp.wait_ge(cm_z, c + 1)
                sp.dma_start(zT[(12 + c) * P:(13 + c) * P, :], zc[:]).then_inc(cm_st, 16)
                sp.wait_ge(cm_st, 16 * (c + 2))
            barrier(sp, 2)

            sp.dma_start(rg[:], gla_norm_g[0:1, :].to_broadcast([P, DV])).then_inc(g_r, 16)
            sp.wait_ge(g_c, 1)

            def load_qk(st):
                h = st.n
                wait_if_any(sp, g_q, h)
                sp.dma_start(a2h[:], gla_a2[0][:, bass.ds(h * P, P)]).then_inc(g_pin, 16)
                sp.dma_start(abh[:], gla_a_b[0:1, bass.ds(h * P, P)].rearrange("a p -> p a")).then_inc(g_pin, 16)
                sp.dma_start(qT[:], feat[bass.ds(h * P + C_Q, P), :]).then_inc(g_pin, 16)
                sp.dma_start(kT[:], feat[bass.ds(h * P + C_K, P), :]).then_inc(g_pin, 16)

            def load_head(st):
                h, s = st.n, st.s
                for to, base in ((vt[s], 0), (rt[s], 1024)):
                    sp.dma_start(to[:, 0:NFULL, :], tokd[0:SEQ, bass.ds(h * DV + base, DV)]
                                 .rearrange("(t p) c -> p t c", p=P)).then_inc(g_in[s], 16)
                    sp.dma_start(to[0:NDEC, NFULL, :], tokd[SEQ:NTOK, bass.ds(h * DV + base, DV)]).then_inc(g_in[s], 16)
                sp.dma_start(Sd[s][:], state_gla[0][:, bass.ds(h, 1)].rearrange("s a d e -> d (s a) e")).then_inc(g_in[s], 16)

            load_qk(Step(0, 0))
            load_head(Step(0, 0))

            def gla(st):
                h, s = st.n, st.s
                if st.ahead(1).within(HEADS):
                    load_qk(st.ahead(1))
                    load_head(st.ahead(1))
                sp.wait_ge(g_s, h * (NCHUNK + DEC_B) + NCHUNK + DEC_B)
                sp.dma_start(gla_p[0, 0][bass.ds(h, 1)].rearrange("a d e -> (a d) e"), S[:, NCHUNK, :]).then_inc(g_sv, 16)
                sp.dma_start(gla_s[0][:, bass.ds(h, 1)].rearrange("s a d e -> d (s a) e"), Sn[:]).then_inc(g_sv, 16)
                sp.wait_ge(g_tc, h * NT + NT)
                sp.dma_start(zT[bass.ds(h * DV + 4 * P, DV), :].rearrange("(a p) n -> p a n", p=P), zb[s][:]).then_inc(g_st[s], 16)
            steps(sp, gla, HEADS, ends=True)
            sp.wait_ge(g_sv, 32 * HEADS)
            for s in range(2):
                sp.wait_ge(g_st[s], 16 * (HEADS // 2))
            barrier(sp, 3)

            def load_z(st):
                if not st.first:
                    sp.wait_ge(z_lo, st.n - 1)
                sp.dma_start(zr[st.s], zT[bass.ds(st.n * P, P), :]).then_inc(z_in[st.s], 16)
            steps(sp, load_z, 16)
            sp.wait_ge(z_lo, 16)

            def load_proj(st):
                n = st.n
                again = not (st.first and st.s == 0)
                if again:
                    sp.wait_ge(p_lo, n)
                for k0, kn, w in ((0, 4, proj_a), (4, 8, proj_b), (12, 4, proj_c)):
                    sp.dma_start(PR[:, k0:k0 + kn, :], w[0].rearrange("(k p) c -> p k c", p=P)[:, :, bass.ds(n * P, P)]).then_inc(p_in, 16)
                if again:
                    sp.wait_ge(mix_ready, n)
                    sp.dma_start(mixT[bass.ds((n - 1) * P, P), :], ymix[1 - st.s][:]).then_inc(mix_st, 16)
                for b in range(3):
                    sp.dma_start(sg[:, b, :], feat[bass.ds(n * P + C_G + b * D, P), :]).then_inc(sg_in, 16)
                if again:
                    wait_alone(sp, mix_st, n * 16)
            steps(sp, load_proj, KD)
            sp.wait_ge(mix_ready, KD)
            sp.dma_start(mixT[(KD - 1) * P:KD * P, :], ymix[1][:]).then_inc(mix_st, 16)
            sp.wait_ge(mix_st, 16 * KD)
            barrier(sp, 4)

            sp.dma_start(WOR[:], w_out[0].rearrange("(k p) c -> p k c", p=P)).then_inc(wo_in, 16)
            sp.dma_start(g2b[:], norm2_g[0:1, :].to_broadcast([P, D])).then_inc(r4_in, 16)
            sp.dma_start(wr[:, :, 0:GROUPS], rg_w[0].rearrange("(k p) c -> p k c", p=P)).then_inc(r4_in, 16)
            sp.dma_start(wr[:, :, GROUPS:], re_w[0].rearrange("(k p) c -> p k c", p=P)).then_inc(r4_in, 16)
            sp.dma_start(rb[:, 0:GROUPS], rg_b[0:1, :].to_broadcast([P, GROUPS])).then_inc(r4_in, 16)
            sp.dma_start(rb[:, GROUPS:], re_b[0:1, :].to_broadcast([P, NE])).then_inc(r4_in, 16)

            def load_m(st, rows):
                if not st.first:
                    sp.wait_ge(m_lo, st.n - 1)
                    sp.wait_ge(x2_ready, st.n - 1)
                mv = mixT.rearrange("(k p) n -> p k n", p=P)
                sp.dma_start(MR[st.s][:, :, 0:rows], mv[:, :, tok(st.n, rows)]).then_inc(m_in[st.s], 16)
                src = xs[:, :] if rows < P else xp[tok(st.n), :]
                sp.dma_start(X4[st.s][0:rows], src).then_inc(m_in[st.s], 16)
            token_tiles(sp, load_m)
            barrier(sp, 5)

            sp.wait_ge(r_c, 1)
            sp.dma_start(table.rearrange("(p b) a -> p (b a)", p=BR), emp[:]).then_inc(r_tab, 16)
            sp.wait_ge(r_sc, 16 * 2 * NT)
            sp.dma_start(tidx[:], table.rearrange("(p b) a -> p (b a)", p=BR)).then_inc(r_ld, 16)
            sp.wait_ge(r_ld, 16)
            barrier(sp, 6)

            def load_expert(e, s, wait):
                for i, w in enumerate((exp_w1, exp_w3)):
                    wait(i)
                    sp.dma_start(E1[s][:, i, :, :], w[0][bass.ds(e, 1)].rearrange("a (p k) c -> p (a k) c", k=KD)).then_inc(e_in[i][s], 16)
                wait(2)
                sp.dma_start(E2[s][:], exp_w2[0][bass.ds(e, 1)].rearrange("a (p k) c -> p (a k) c", k=2)).then_inc(e_in[2][s], 16)

            def expert(st):
                def wait(i):
                    if not st.first:
                        if i < 2:
                            sp.wait_ge(e1_lo, st.n * 2 - 3 + i)
                        else:
                            sp.wait_ge(e2_lo, st.n - 1)
                load_expert(st.n, st.s, wait)
            steps(sp, expert, NE)
            barrier(sp, 7)
            n_more = sp.value_load(eovf[0:1, NOVF:NOVF + 1], min_val=0, max_val=NOVF)
            with sp.If(n_more > 0):
                with sp.Fori(0, n_more) as j:
                    e = sp.value_load(eovf[0:1, bass.ds(j, 1)], min_val=0, max_val=NE - 1)
                    sp.wait_ge(y_ready, j + NE)
                    load_expert(e, 0, lambda i: None)
            barrier(sp, 8)

            sp.dma_start(gfb[:], final_g.rearrange("(a n) -> a n", a=1).to_broadcast([P, D])).then_inc(c_g, 16)

            def load_c(st, rows):
                if not st.first:
                    sp.wait_ge(c_sum, st.n - 1)
                r0 = SEQ if rows < P else st.n * P
                sp.dma_start(FX[st.s][0:rows], x2d[bass.ds(r0, rows), :]).then_inc(c_in[st.s], 16)
            token_tiles(sp, load_c)
            barrier(sp, 9)

        @block.gpsimd
        def _(pool):
            pool.memset(ident[:], 0.0)
            pool.memset(epsc[:], EPS)
            pool.memset(lgt[:, NFULL, :], 0.0)
            pool.drain()
            pool.affine_select(out=ident[:], in_=ident[:], compare_op=ALU.not_equal, fill=1.0, base=0,
                               pattern=[[-1, P]], channel_multiplier=1).then_inc(s_const, 1)

            pool.memset(junk2[:], 0.0).then_inc(yz_ready, 1)
            pool.wait_ge(yz_ready, 1)
            pool.dma_start(yb[NE * BR:NBLK * BR, :].rearrange("(b p) c -> p b c", p=BR),
                           junk2[0:BR].rearrange("p (a c) -> p a c", a=1).to_broadcast([BR, NOVF, D])).then_inc(yz_st, 16)

            def store_t(col, st, all_, here):
                base = {C_V: 0, C_R: 1024, C_VV: 2048}[col]
                pool.wait_ge(t_ev, all_.n * NT + NT)
                cols = bass.ds(st.n * CW + base, CW)
                pool.dma_start(tokd[0:SEQ, cols].rearrange("(t p) c -> p t c", p=P), OT[st.s][:, 0:NFULL, :]).then_inc(t_st[st.s], 16)
                pool.dma_start(tokd[SEQ:NTOK, cols], OT[st.s][0:NDEC, NFULL, :]).then_inc(t_st[st.s], 16)
            chunks(pool, T_TURNS, 0, store_t)

            def store_f(col, st, all_, here):
                pool.wait_ge(f_ev, here.n * 2 + 2)
                pool.dma_start(feat[bass.ds(st.n * CW + col, CW), :].rearrange("(a p) n -> p a n", p=P), OF[st.s][:]).then_inc(f_st[st.s], 16)
            chunks(pool, F_TURNS, NTC // 2, store_f)
            for s in range(2):
                pool.wait_ge(t_st[s], 32 * (NTC // 2))
                pool.wait_ge(f_st[s], 16 * (NFC // 2))
            pool.wait_ge(yz_st, 16)
            barrier(pool, 1)

            pool.memset(wsd[:], 0.0).then_inc(cm_wd0, 1)
            pool.memset(vvt[:, NFULL, :], 0.0).then_inc(cm_wd0, 1)
            pool.wait_ge(cm_w, 16 * (1 + DEC_B))
            pool.affine_select(out=wsn[:], in_=wsn[:], compare_op=ALU.is_ge, fill=0.0, base=0,
                               pattern=[[0, NCH], [-1, P]], channel_multiplier=1).then_inc(cm_tri, 1)
            pool.affine_select(out=wsd[:], in_=wsd[:], compare_op=ALU.is_ge, fill=0.0, base=0,
                               pattern=[[0, NCH], [-1, P]], channel_multiplier=1).then_inc(cm_tri, 1)
            barrier(pool, 2)

            pool.memset(mf[:], 1.0)
            pool.memset(mdf[:], 1.0)
            pool.memset(rmask[:], 1.0)
            pool.memset(seg[:], 1.0)
            pool.memset(S[:, 0, :], 0.0)
            for s in range(2):
                pool.memset(qz[s][:], 0.0)
                pool.memset(rt[s][:, NFULL, :], 0.0)
            for b in attm:
                pool.memset(b[:], 0.0)
            pool.memset(attd[:], 0.0)
            pool.drain()
            pool.memset(seg[:, 0:SEQ].rearrange("p (c t) -> p c t", t=CHUNK)[:, :, 0:1], 0.0)
            pool.memset(seg[:, SEQ:NTOK].rearrange("p (c t) -> p c t", t=DEC_T)[:, :, 0:1], 0.0)
            pool.affine_select(out=mf[:], in_=mf[:], compare_op=ALU.is_ge, fill=0.0, base=0,
                               pattern=[[1, P]], channel_multiplier=-1)
            pool.affine_select(out=mdf[:], in_=mdf[:], compare_op=ALU.is_ge, fill=0.0, base=0,
                               pattern=[[1, NDEC]], channel_multiplier=-1)
            pool.affine_select(out=rmask[:], in_=rmask[:], compare_op=ALU.is_ge, fill=0.0, base=0,
                               pattern=[[-DEC_T, DEC_B]], channel_multiplier=1)
            pool.drain()
            pool.memset(mf[0:CHUNK, CHUNK:P], 0.0)
            pool.affine_select(out=mdf[:], in_=mdf[:], compare_op=ALU.is_ge, fill=0.0, base=0,
                               pattern=[[-DEC_T, DEC_B], [0, DEC_T]], channel_multiplier=1)
            pool.affine_select(out=rmask[:], in_=rmask[:], compare_op=ALU.is_ge, fill=0.0, base=DEC_T - 1,
                               pattern=[[DEC_T, DEC_B]], channel_multiplier=-1)
            pool.drain()
            pool.tensor_copy(mp[:], mf[:])
            pool.tensor_copy(md[:], mdf[:])
            pool.drain().then_inc(g_c, 1)
            pool.wait_ge(g_r, 16)

            def r_gain(st):
                pool.wait_ge(g_in[st.s], st.t * 80 + 80)
                pool.tensor_tensor(rt[st.s][:], rt[st.s][:], rg[:].rearrange("p (a c) -> p a c", a=1).to_broadcast([P, NT, DV]),
                                   ALU.mult).then_inc(g_rg, 1)
            steps(pool, r_gain, HEADS, ends=True)
            barrier(pool, 3)
            barrier(pool, 4)

            def store_n2(st, rows):
                pool.wait_ge(n2_ready, st.n + 1)
                pool.dma_start(x2d[tok(st.n, rows), :], X2[st.s][0:rows]).then_inc(n2_st[st.s], 16)
                pool.dma_start(xn2d[tok(st.n, rows), :], N2[st.s][0:rows]).then_inc(n2_st[st.s], 16)
            token_tiles(pool, store_n2)
            pool.wait_ge(n2_st[0], 32 * (NFULL // 2 + 1))
            pool.wait_ge(n2_st[1], 32 * (NFULL // 2))
            barrier(pool, 5)

            pool.memset(emp[:], EMPTY)
            pool.memset(onesm[:], 1.0)
            pool.memset(ltri[:], 1.0)
            pool.memset(one64[:], 1.0)
            pool.iota(iE[:], pattern=[[0, NT], [1, NE]], base=0, channel_multiplier=0)
            pool.iota(iV[:], pattern=[[1, NOVF], [0, NE]], base=0, channel_multiplier=0)
            pool.iota(slot[:], pattern=[[P, NT]], base=0, channel_multiplier=1)
            pool.drain()
            pool.affine_select(out=ltri[:], in_=ltri[:], compare_op=ALU.is_gt, fill=0.0, base=0,
                               pattern=[[1, P]], channel_multiplier=-1)
            pool.tensor_copy(ioE[:], iE[:])
            pool.tensor_copy(ioV[:], iV[:])
            pool.drain().then_inc(r_c, 1)
            pool.wait_ge(r_tab, 16)
            pool.wait_ge(r_dst, 1)
            for t in range(NT):
                for k in range(2):
                    pool.indirect_dma_start(out=table[:, :], out_offset=bass.IndirectOffsetOnAxis(ap=dsti[:, k, t:t + 1], axis=0),
                                            in_=slot[:, t:t + 1], in_offset=None,
                                            bounds_check=BR * NBLK - 1, oob_is_err=False).then_inc(r_sc, 16)
            pool.wait_ge(r_sc, 16 * 2 * NT)
            barrier(pool, 6)

            pool.memset(XG[0][:], 0.0)
            pool.memset(XG[1][:], 0.0)
            pool.drain()

            def gather(st, lag=2):
                n, s = st.n, st.s
                if lag == 1 or not st.first:
                    pool.wait_ge(xg_tp, n + 1 - lag)
                    pool.wait_ge(xg_in[s], st.t * 16)
                pool.tensor_copy(gix[s][:], tidx[:, bass.ds(n, 1)]).then_inc(i_gx, 1)
                wait_alone(pool, i_gx, n + 1)
                pool.indirect_dma_start(out=XG[s][:], out_offset=None, in_=xn2d[:, :],
                                        in_offset=bass.IndirectOffsetOnAxis(ap=gix[s][:, 0:1], axis=0),
                                        bounds_check=NTOK - 1, oob_is_err=False).then_inc(xg_in[s], 16)

            gather(Step(0, 0))
            gather(Step(0, 1))
            with pool.Fori(1, NE // 2) as t:
                gather(Step(t, 0))
                gather(Step(t, 1))
            barrier(pool, 7)
            n_more = pool.value_load(eovf[0:1, NOVF:NOVF + 1], min_val=0, max_val=NOVF)
            with pool.If(n_more > 0):
                with pool.Fori(0, n_more) as j:
                    gather(More(j), lag=1)
            barrier(pool, 8)

            def gather_c(st, rows):
                n, s = st.n, st.s
                if not st.first:
                    pool.wait_ge(c_sum, n - 1)
                pool.tensor_copy(cix[s][:], yrow[:, :, bass.ds(n, 1)].rearrange("p k a -> p (k a)")).then_inc(c_ix, 1)
                wait_alone(pool, c_ix, n + 1)
                for k in range(2):
                    pool.indirect_dma_start(out=FY[s][0:rows, k, :], out_offset=None, in_=yb[:, :],
                                            in_offset=bass.IndirectOffsetOnAxis(ap=cix[s][0:rows, k:k + 1], axis=0),
                                            bounds_check=NBLK * BR - 1, oob_is_err=False).then_inc(cy_in[s], 16)
            gather_c(Step(0, 0), P)
            gather_c(Step(0, 1), P)

            def store_c(st, rows):
                pool.wait_ge(c_out, st.n + 1)
                out = y_sample.rearrange("a b n -> (a b) n") if rows < P else y_prompt[0][tok(st.n), :]
                pool.dma_start(out, FO[st.s][0:rows]).then_inc(c_st[st.s], 16)

            def move_c(st):
                gather_c(st.ahead(2), P)
                store_c(st, P)
            steps(pool, move_c, NFULL - 2)
            gather_c(Step(NFULL // 2, 0), NDEC)
            store_c(Step(NFULL // 2 - 1, 0), P)
            store_c(Step(NFULL // 2 - 1, 1), P)
            store_c(Step(NFULL // 2, 0), NDEC)
            pool.wait_ge(c_st[0], 16 * (NFULL // 2 + 1))
            pool.wait_ge(c_st[1], 16 * (NFULL // 2))
            barrier(pool, 9)

        @block.scalar
        def _(act):
            act.wait_ge(s_const, 1)

            def norm1(st, rows):
                n, s = st.n, st.s
                act.wait_ge(x_in[s], st.t * 16 + 16)
                act.activation(junk[0:rows], X[s][0:rows], ACT.Square, accum_out=ssq[s][0:rows])
                act.drain()
                act.activation(rtt[s][0:rows], ssq[s][0:rows], ACT.Sqrt, bias=epsc[0:rows], scale=1.0 / D).then_inc(rms_ready, 1)
                act.wait_ge(xt_done, n + 1)
                act.activation(XH[:, :, tok(n, rows)], xpos(s)[:, :, 0:rows], ACT.Copy).then_inc(xh_ready, 1)
            token_tiles(act, norm1)

            def split_w(all_):
                n, s = all_.n, all_.s
                act.wait_ge(w_in_s[s], all_.t * 16 + 16)
                if not all_.first:
                    act.wait_ge(w_used, n - 1)
                act.activation(WH[s][:], RAW[s][:], ACT.Copy).then_inc(wh_ready, 1)

            split_w(Step(0, 0))

            def t_chunk(col, st, all_, here):
                split_w(all_.ahead(1))
                s = st.s
                for tile in range(NT):
                    rows = rows_of(tile)
                    u = s * NT + tile
                    act.wait_ge(t_mm, all_.n * NT + tile + 1)
                    if tile == 0 and not all_.first:
                        act.wait_ge(t_st[s], all_.t * 32)
                    func = {C_V: ACT.Copy, C_R: ACT.Silu, C_VV: ACT.Gelu_apprx_tanh}[col]
                    act.activation(OT[s][0:rows, tile, :], ps[0:rows, u % 6, 0:CW], func).then_inc(t_ev, 1)
            chunks(act, T_TURNS, 0, t_chunk)

            def f_chunk(func, last=None):
                def go(col, st, all_, here):
                    s = st.s
                    if not (last and st.static and s == 1):
                        split_w(all_.ahead(1))
                    for f in range(2):
                        act.wait_ge(f_mm, here.n * 2 + (f + 1))
                        if f == 0 and not here.first:
                            act.wait_ge(f_st[s], here.t * 16)
                        act.activation(OF[s][:, f, 0:768].rearrange("p (g n) -> p g n", g=2), ps[:, 3 * f:3 * f + 2, 0:384], func)
                        act.activation(OF[s][:, f, 768:NTOK], ps[:, 3 * f + 2, 0:320], func).then_inc(f_ev, 1)
                return go
            b = NTC // 2
            for s in range(2):
                f_chunk(ACT.Copy)(C_H, Step(0, s), Step(b, s), Step(0, s))
            with act.Fori(1, 5) as t:
                for s in range(2):
                    f_chunk(ACT.Copy)(C_H, Step(t, s), Step(t + b, s), Step(t, s))
            for s in range(2):
                f_chunk(ACT.Gelu_apprx_tanh)(C_U, Step(0, s), Step(b + 5, s), Step(5, s))
            with act.Fori(0, 5) as t:
                for s in range(2):
                    f_chunk(ACT.Sigmoid)(C_G, Step(t, s), Step(t + (b + 6), s), Step(t + 6, s))
            for s in range(2):
                f_chunk(ACT.Sigmoid, last=True)(C_G, Step(5, s), Step(b + 11, s), Step(11, s))
            act.wait_ge(a_in, 16)
            act.wait_ge(w_used, NTC + NFC)
            act.activation(WH[0][:, :, 0:P], RAW[0][:, :, 0:P], ACT.Copy).then_inc(a_hi, 1)
            act.wait_ge(a_mm, 1)
            act.activation(alr[:, 0:768].rearrange("p (g n) -> p g n", g=2), ps[0:LOWRANK, 0:2, 0:384], ACT.Copy)
            act.activation(alr[:, 768:NTOK], ps[0:LOWRANK, 2, 0:320], ACT.Copy)
            barrier(act, 1)

            act.wait_ge(cm_in, 64)
            act.activation(vsq[:], vvt[:], ACT.Square).then_inc(cm_sq, 1)
            act.wait_ge(cm_rt, 1)
            act.activation(vrs[:], vss[:], ACT.Sqrt, bias=epsc[:], scale=1.0 / P).then_inc(cm_rt, 1)
            for half in range(2):
                act.wait_ge(cm_wt, half + 1)
                if half == 0:
                    act.activation(wsT[:], ps[:, 0, :].rearrange("p (g t) -> p g t", g=NCH), ACT.Copy).then_inc(cm_wc, 1)
                else:
                    act.activation(wsdT[:], ps[0:NDEC, 1, 0:NCH * NDEC].rearrange("p (g t) -> p g t", g=NCH), ACT.Copy).then_inc(cm_wc, 1)
            barrier(act, 2)

            def decay_copy(st, g):
                n, (t0, tn) = st.n, TG[g]
                if g == 0:
                    act.wait_ge(g_pin, n * 64 + 64)
                    wait_if_any(act, g_q, n)
                act.wait_ge(g_a, n * 3 + g + 1)
                act.activation(zz[:, t0:t0 + tn], ps[:, 2, 0:tn], ACT.Identity, bias=abh[:]).then_inc(g_zc, 1)

            def decay_ln(st):
                act.drain()
                act.activation(t1[:], zz[:], ACT.Abs)
                act.drain()
                act.activation(t1[:], t1[:], ACT.Exp, scale=-1.0)
                act.drain()
                act.activation(t1[:], t1[:], ACT.Ln, bias=1.0).then_inc(g_z, 1)

            def decay_exp(st):
                act.wait_ge(g_b, st.n * 2 + 1)
                act.activation(eb[st.s][:], cs[:], ACT.Exp, scale=1.0 / TAU)
                act.activation(t1[:], cs[:], ACT.Exp, scale=-1.0 / TAU)
                act.wait_ge(g_b, st.n * 2 + 2)
                act.activation(zz[:], zz[:], ACT.Exp, scale=1.0 / TAU).then_inc(g_e, 1)

            def k_copy(st, j):
                rows, b = rows_of(j), turn_of(st, j)
                act.wait_ge(g_kp, st.n * NT + (j + 1))
                act.activation(ket[b][0:rows], ps[0:rows, 3, 0:P], ACT.Copy).then_inc(g_kc, 1)

            def out_rms(st, j):
                rows, b = rows_of(j), turn_of(st, j)
                act.wait_ge(g_o, st.n * NT + (j + 1))
                wait_if_any(act, g_n, st.n * NT + (j - 1))
                act.activation(osq[b][0:rows], ps[0:rows, b, 0:DV], ACT.Square, accum_out=oss[b][0:rows])
                act.drain()
                act.activation(ors[b][0:rows], oss[b][0:rows], ACT.Sqrt, bias=epsc[0:rows], scale=1.0 / DV).then_inc(g_rt, 1)

            def out_copy(st, j):
                rows = rows_of(j)
                act.wait_ge(g_tp, st.n * NT + (j + 1))
                if j == 0:
                    wait_if_any(act, g_st[st.s], st.t * 16)
                act.activation(zb[st.s][:, :, j * P:j * P + rows], ps[:, 4, 0:DV].rearrange("p (a t) -> p a t", a=2)[:, :, 0:rows],
                               ACT.Copy).then_inc(g_tc, 1)

            for g in range(3):
                decay_copy(Step(0, 0), g)
            decay_ln(Step(0, 0))
            decay_exp(Step(0, 0))

            def gla(st):
                nxt = st.ahead(1)
                more = nxt.within(HEADS)
                k_copy(st, 0)
                for j in range(NT):
                    if j + 1 < NT:
                        k_copy(st, j + 1)
                    if more and j < 3:
                        decay_copy(nxt, j)
                    if j:
                        out_copy(st, j - 1)
                    out_rms(st, j)
                    if more and j == 3:
                        decay_ln(nxt)
                    if more and j == 5:
                        decay_exp(nxt)
                out_copy(st, NT - 1)
            steps(act, gla, HEADS, ends=True)
            barrier(act, 3)

            def hi_z(st):
                act.wait_ge(z_in[st.s], st.t * 16 + 16)
                act.activation(ZH[:, bass.ds(st.n, 1), :].rearrange("p a n -> p (a n)"), zr[st.s], ACT.Copy).then_inc(z_hi, 1)
            steps(act, hi_z, 16)

            def hi_p(st):
                act.wait_ge(p_in, st.n * 48 + 48)
                if not st.first:
                    act.wait_ge(p_mm, st.n * 3 - 3)
                act.activation(PH[st.s][:], PR[:], ACT.Copy).then_inc(p_hi, 1)
            steps(act, hi_p, KD)
            barrier(act, 4)

            act.wait_ge(wo_in, 16)
            act.activation(WOH[:], WOR[:], ACT.Copy).then_inc(wo_hi, 1)

            def hi_m(st, rows):
                act.wait_ge(m_in[st.s], st.t * 32 + 32)
                if not st.first:
                    act.wait_ge(o_mm, st.n - 1)
                act.activation(MH[st.s][:, :, 0:rows], MR[st.s][:, :, 0:rows], ACT.Copy).then_inc(m_hi, 1)

            def norm2(st, rows, meanwhile):
                act.wait_ge(x2_ready, st.n + 1)
                act.activation(sq4[0:rows], X2[st.s][0:rows], ACT.Square, accum_out=ss4[0:rows])
                act.drain()
                act.activation(rt4[0:rows], ss4[0:rows], ACT.Sqrt, bias=epsc[0:rows], scale=1.0 / D).then_inc(x2_rms, 1)
                meanwhile()
                act.wait_ge(n2_tp, st.n + 1)
                act.activation(NTt[:, :, 0:rows], ps[:, 4:6, :].rearrange("p b (k t) -> p (b k) t", k=4)[:, :, 0:rows], ACT.Copy).then_inc(n2_tc, 1)
            hi_m(Step(0, 0), P)
            hi_m(Step(0, 1), P)
            steps(act, lambda st: norm2(st, P, lambda: hi_m(st.ahead(2), P)), NFULL - 2)
            norm2(Step(NFULL // 2 - 1, 0), P, lambda: hi_m(Step(NFULL // 2, 0), NDEC))
            norm2(Step(NFULL // 2 - 1, 1), P, lambda: None)
            norm2(Step(NFULL // 2, 0), NDEC, lambda: None)
            barrier(act, 5)

            act.wait_ge(r_mx, 1)
            act.activation(gex[:], gva[:], ACT.Exp).then_inc(r_ex, 1)
            act.wait_ge(r_d, 1)
            act.activation(gd[:], gd[:], ACT.Exp).then_inc(r_e2, 1)
            barrier(act, 6)

            def split1(st, i, lag=2):
                act.wait_ge(e_in[i][st.s], st.t * 16 + 16)
                if i == 0 and (lag == 1 or not st.first):
                    act.wait_ge(h_mm, st.n + 1 - lag)
                act.activation(E1H[st.s][:, i], E1[st.s][:, i], ACT.Copy).then_inc(e1_hi, 1)

            def split2(st, lag=2):
                act.wait_ge(e_in[2][st.s], st.t * 16 + 16)
                if lag == 1 or not st.first:
                    act.wait_ge(y_mm, st.n + 1 - lag)
                act.activation(E2H[st.s][:], E2[st.s][:], ACT.Copy).then_inc(e2_hi, 1)

            def x_hi(st):
                act.wait_ge(xg_tp, st.n + 1)
                act.activation(XTH[st.s][:, :, 0:BR], ps[:, 0, :].rearrange("p (k t) -> p k t", k=KD), ACT.Copy).then_inc(xth, 1)

            def silu(st):
                act.wait_ge(h_mm, st.n + 1)
                if not (st.first and st.s == 0):
                    act.wait_ge(h_ready, st.n)
                act.activation(sil[:], ps[0:BR, 2 + st.s, 0:DE], ACT.Silu).then_inc(h_sig, 1)

            def y_out(st):
                act.wait_ge(y_mm, st.n + 1)
                if not st.first:
                    act.wait_ge(y_st[st.s], st.t * 16)
                act.activation(YS[st.s][:], ps[0:BR, 5:7, :].rearrange("p b n -> p (b n)"), ACT.Copy).then_inc(y_ready, 1)
                act.wait_ge(y_ready, st.n + 1)
                act.dma_start(yb[bass.ds(st.n * BR, BR), :], YS[st.s][:]).then_inc(y_st[st.s], 16)

            def h_hi(st):
                act.wait_ge(h_tp, st.n + 1)
                act.activation(HTH[:, :, 0:BR], ps[:, 4, 0:2 * BR].rearrange("p (a t) -> p a t", a=2), ACT.Copy).then_inc(hth, 1)

            split1(Step(0, 0), 0)
            split1(Step(0, 0), 1)
            x_hi(Step(0, 0))

            def expert(st):
                nxt, prev, before = st.ahead(1), st.ahead(-1), st.ahead(-2)
                more = nxt.within(NE)
                if more:
                    split1(nxt, 0)
                if prev.within(NE):
                    h_hi(prev)
                if more:
                    split1(nxt, 1)
                if before.within(NE):
                    y_out(before)
                silu(st)
                if more:
                    x_hi(nxt)
                split2(st)
            steps(act, expert, NE, ends=True)
            h_hi(Step(NE // 2 - 1, 1))
            y_out(Step(NE // 2 - 1, 0))
            y_out(Step(NE // 2 - 1, 1))
            for s in range(2):
                act.wait_ge(y_st[s], 16 * (NE // 2))
            barrier(act, 7)
            n_more = act.value_load(eovf[0:1, NOVF:NOVF + 1], min_val=0, max_val=NOVF)
            with act.If(n_more > 0):
                with act.Fori(0, n_more) as j:
                    st = More(j)
                    split1(st, 0, lag=1)
                    split1(st, 1, lag=1)
                    split2(st, lag=1)
                    x_hi(st)
                    silu(st)
                    h_hi(st)
                    y_out(st)
                    act.wait_ge(y_st[0], (j + (1 + NE // 2)) * 16)
            barrier(act, 8)

            def norm_f(st, rows):
                act.wait_ge(c_sum, st.n + 1)
                act.activation(jf[0:rows], FS[st.s][0:rows], ACT.Square, accum_out=ss6[0:rows])
                act.drain()
                act.activation(rt6[0:rows], ss6[0:rows], ACT.Sqrt, bias=epsc[0:rows], scale=1.0 / D).then_inc(c_rms, 1)
            token_tiles(act, norm_f)
            barrier(act, 9)

        @block.vector
        def _(dve):
            dve.memset(XH[:, :, NTOK:].bitcast(F32), 0.0)
            dve.memset(XL[:, :, NTOK:].bitcast(F32), 0.0)
            dve.wait_ge(g1_in, 16)

            def norm1(st, rows):
                n, s = st.n, st.s
                dve.wait_ge(rms_ready, n + 1)
                dve.reciprocal(rst[s][0:rows], rtt[s][0:rows])
                dve.drain()
                if not st.first:
                    dve.wait_ge(xt_done, n - 1)
                dve.scalar_tensor_tensor(out=XN[s][0:rows], in0=X[s][0:rows], scalar=rst[s][0:rows], in1=g1b[0:rows],
                                         op0=ALU.mult, op1=ALU.mult).then_inc(xn_ready, 1)
                dve.wait_ge(xh_ready, n + 1)
                dve.tensor_tensor(XL[:, :, tok(n, rows)], xpos(s)[:, :, 0:rows], XH[:, :, tok(n, rows)].bitcast(F32),
                                  ALU.subtract).then_inc(xl_ready, 1)
            token_tiles(dve, norm1)

            def low_w(col, st, all_, here):
                dve.wait_ge(wh_ready, all_.n + 1)
                dve.tensor_tensor(WL[st.s][:], RAW[st.s][:], WH[st.s][:].bitcast(F32), ALU.subtract).then_inc(wl_ready, 1)
            chunks(dve, T_TURNS, 0, low_w)
            chunks(dve, F_TURNS, NTC // 2, low_w)
            dve.wait_ge(a_hi, 1)
            dve.tensor_tensor(WL[0][:, :, 0:P], RAW[0][:, :, 0:P], WH[0][:, :, 0:P].bitcast(F32), ALU.subtract).then_inc(a_lo, 1)
            barrier(dve, 1)

            dve.memset(cpp[:, 0:2], 0.0)

            def conv(c):
                dve.wait_ge(cv_in, c * 96 + 96)
                dve.tensor_tensor(cpp[:, 2:2 + SEQ], cG[:, 0:SEQ], cH[:, 0:SEQ], ALU.mult)
                dve.tensor_tensor(cps[:, :, 2:2 + DEC_T], cG[:, SEQ:NTOK].rearrange("p (s t) -> p s t", s=DEC_B),
                                  cH[:, SEQ:NTOK].rearrange("p (s t) -> p s t", s=DEC_B), ALU.mult)
                dve.drain()
                co, cz = cout[:, SEQ:NTOK].rearrange("p (s t) -> p s t", s=DEC_B), cout[:, 0:SEQ]
                dve.tensor_scalar(cz, cpp[:, 0:SEQ], cwt[:, 0:1], None, ALU.mult)
                dve.tensor_scalar(co, cps[:, :, 0:DEC_T], cwt[:, 0:1], None, ALU.mult)
                for k in (1, 2):
                    dve.drain()
                    dve.scalar_tensor_tensor(out=cz, in0=cpp[:, k:k + SEQ], scalar=cwt[:, k:k + 1], in1=cz, op0=ALU.mult, op1=ALU.add)
                    dve.scalar_tensor_tensor(out=co, in0=cps[:, :, k:k + DEC_T], scalar=cwt[:, k:k + 1], in1=co, op0=ALU.mult, op1=ALU.add)
                dve.drain()
                dve.tensor_tensor(za[:], cB[:], cout[:], ALU.mult).then_inc(cv_z, 1)
            with dve.Fori(0, NCH) as c:
                conv(c)

            dve.wait_ge(cm_sq, 1)
            dve.tensor_reduce(vss[:], vsq[:].rearrange("p t (g c) -> p (t g) c", g=NCH), AX.X, ALU.add).then_inc(cm_rt, 1)
            dve.wait_ge(cm_rt, 2)
            dve.reciprocal(vss[:], vrs[:])
            dve.drain()
            v3 = vvt[:].rearrange("p t (g c) -> p (t g) c", g=NCH)
            dve.tensor_tensor(v3, v3, vss[:].rearrange("p (a b) -> p a b", b=1).to_broadcast([P, NT * NCH, P]), ALU.mult)
            dve.drain()
            dve.tensor_tensor(vvt[:], vvt[:], cmg[:].rearrange("p (a c) -> p a c", a=1).to_broadcast([P, NT, CONV_CH]), ALU.mult).then_inc(cm_v, 1)
            for c in range(NCH):
                dve.wait_ge(cm_mm, c + 1)
                dve.wait_ge(cm_u, 16 * (c + 1))
                if c:
                    dve.wait_ge(cm_st, 16 * (c + 1))
                dve.tensor_tensor(zc[:, 0:SEQ].rearrange("p (n t) -> p n t", t=P), ps[:, 2:4, :].rearrange("p b (n t) -> p (b n) t", t=P),
                                  cmb[:, c:c + 1, :].to_broadcast([P, NFULL, P]), ALU.add)
                dve.tensor_tensor(zc[:, SEQ:NTOK].rearrange("p (n t) -> p n t", t=DEC_T), ps[:, 4, 0:NDEC].rearrange("p (n t) -> p n t", t=DEC_T),
                                  cmb[:, c:c + 1, 0:DEC_T].to_broadcast([P, DEC_B, DEC_T]), ALU.add)
                dve.drain()
                dve.tensor_tensor(zc[:], zc[:], uT[:], ALU.mult).then_inc(cm_z, 1)
            barrier(dve, 2)

            dve.wait_ge(g_c, 1)
            csp = cs[:, 0:SEQ].rearrange("p (c t) -> p c t", t=CHUNK)
            csd = cs[:, SEQ:NTOK].rearrange("p (c t) -> p c t", t=DEC_T)
            per = NCHUNK + DEC_B

            def decay_sums(st):
                dve.wait_ge(g_z, st.n + 1)
                dve.scalar_tensor_tensor(out=zz[:], in0=zz[:], scalar=0.0, in1=t1[:], op0=ALU.min, op1=ALU.subtract)
                dve.drain()
                dve.tensor_tensor_scan(cs[:], seg[:], zz[:], 0.0, ALU.mult, ALU.add)
                dve.drain().then_inc(g_b, 1)
                dve.tensor_tensor(zz[:, 0:SEQ].rearrange("p (c t) -> p c t", t=CHUNK), csp[:, :, CHUNK - 1:CHUNK].to_broadcast([P, NCHUNK, CHUNK]), csp, ALU.subtract)
                dve.tensor_tensor(zz[:, SEQ:NTOK].rearrange("p (c t) -> p c t", t=DEC_T), csd[:, :, DEC_T - 1:DEC_T].to_broadcast([P, DEC_B, DEC_T]), csd, ALU.subtract)
                dve.drain().then_inc(g_b, 1)

            def decayed_qk(st):
                dve.wait_ge(g_pin, st.n * 64 + 64)
                dve.wait_ge(g_e, st.n + 1)
                dve.scalar_tensor_tensor(out=qt[st.s][:], in0=qT[:], scalar=float(DK) ** -0.5, in1=eb[st.s][:], op0=ALU.mult, op1=ALU.mult)
                dve.tensor_tensor(kt[st.s][:], kT[:], t1[:], ALU.mult)

            def decayed_k_end(st):
                s = st.s
                dve.tensor_tensor(ke[s][:], kT[:], zz[:], ALU.mult)
                dve.drain()
                for q in range(DEC_B):
                    dve.tensor_copy(qz[s][:, q, q * DEC_T:(q + 1) * DEC_T], qt[s][:, SEQ + q * DEC_T:SEQ + (q + 1) * DEC_T])
                dve.drain().then_inc(g_q, 1)

            def mask(st, j):
                b = turn_of(st, j)
                wait_alone(dve, g_ap, st.n * NT + (j + 1))
                if j < NFULL:
                    dve.copy_predicated(attm[b][:], mp[:], ps[:, 7, 0:P]).then_inc(g_am, 1)
                else:
                    dve.copy_predicated(attd[:], md[:], ps[0:NDEC, 7, 0:NDEC]).then_inc(g_am, 1)

            def state(st, c):
                dve.wait_ge(g_u, st.n * per + (c + 1))
                if c == NCHUNK - 1:
                    wait_if_any(dve, g_sv, st.n * 32)
                last = c * CHUNK + CHUNK - 1
                dve.scalar_tensor_tensor(out=S[:, c + 1, :], in0=S[:, c, :], scalar=eb[st.s][:, last:last + 1], in1=ps[:, 5 + c % 2, 0:DV],
                                         op0=ALU.mult, op1=ALU.add).then_inc(g_s, 1)
                dve.drain()

            def end_keys(st):
                dve.wait_ge(g_kc, st.n * NT + NT)
                for q in range(DEC_B):
                    dve.tensor_scalar(kz[:, q, :], ket[turn_of(st, NFULL)][0:NDEC], rmask[:, q:q + 1], None, ALU.mult)
                dve.drain().then_inc(g_kz, 1)

            def state_d(st, q):
                dve.wait_ge(g_u, st.n * per + (NCHUNK + q + 1))
                last = SEQ + q * DEC_T + DEC_T - 1
                dve.scalar_tensor_tensor(out=Sn[:, q, :], in0=Sd[st.s][:, q, :], scalar=eb[st.s][:, last:last + 1], in1=ps[:, 5 + q % 2, 0:DV],
                                         op0=ALU.mult, op1=ALU.add).then_inc(g_s, 1)

            def out_norm(st, j):
                rows, b = rows_of(j), turn_of(st, j)
                dve.wait_ge(g_rt, st.n * NT + (j + 1))
                dve.reciprocal(orc[b][0:rows], ors[b][0:rows])
                dve.drain()
                if j == 0:
                    dve.wait_ge(g_rg, st.n + 1)
                wait_if_any(dve, g_tp, st.n * NT + (j - 1))
                dve.scalar_tensor_tensor(out=og[b][0:rows], in0=ps[0:rows, b, 0:DV], scalar=orc[b][0:rows], in1=rt[st.s][0:rows, j, :],
                                         op0=ALU.mult, op1=ALU.mult).then_inc(g_n, 1)

            decay_sums(Step(0, 0))
            decayed_qk(Step(0, 0))
            decayed_k_end(Step(0, 0))

            def gla(st):
                nxt = st.ahead(1)
                more = nxt.within(HEADS)
                mask(st, 0)
                dve.wait_ge(g_in[st.s], st.t * 80 + 80)
                state(st, 0)
                state(st, 1)
                for j in range(NT):
                    if j + 1 < NT:
                        mask(st, j + 1)
                    if j + 1 < NFULL:
                        state(st, 2 * j + 2)
                        state(st, 2 * j + 3)
                    if j == NFULL - 1:
                        end_keys(st)
                    if more and j == 4:
                        decay_sums(nxt)
                    if more and j == 6:
                        decayed_qk(nxt)
                    out_norm(st, j)
                    if more and j == 7:
                        decayed_k_end(nxt)
                for q in range(DEC_B):
                    state_d(st, q)
            steps(dve, gla, HEADS, ends=True)
            barrier(dve, 3)

            def low_z(st):
                dve.wait_ge(z_hi, st.n + 1)
                one = bass.ds(st.n, 1)
                dve.tensor_tensor(ZL[:, one, :].rearrange("p a n -> p (a n)"), zr[st.s], ZH[:, one, :].rearrange("p a n -> p (a n)").bitcast(F32),
                                  ALU.subtract).then_inc(z_lo, 1)
            steps(dve, low_z, 16)

            def gate(st):
                s, n = st.s, st.n
                if st.first and s == 0:
                    low_p(st)
                if st.ahead(1).within(KD):
                    low_p(st.ahead(1))
                wait_alone(dve, sg_in, n * 48 + 48)
                for b in range(3):
                    bank = 3 * ((s * 3 + b) % 2)
                    dve.drain()
                    dve.wait_ge(p_mm, n * 3 + (b + 1))
                    for to, frm in ((slice(0, 768), None), (slice(768, NTOK), 2)):
                        src = ps[:, bank:bank + 2, 0:384] if frm is None else ps[:, bank + 2, 0:320]
                        g = sg[:, b, to] if frm else sg[:, b, to].rearrange("p (g n) -> p g n", g=2)
                        out = ymix[s] if b == 0 else yt
                        out = out[:, to] if frm else out[:, to].rearrange("p (g n) -> p g n", g=2)
                        last = dve.tensor_tensor(out, src, g, ALU.mult)
                    last.then_inc(p_ev, 1)
                    dve.drain()
                    if b:
                        last = dve.tensor_tensor(ymix[s][:], ymix[s][:], yt[:], ALU.add)
                last.then_inc(mix_ready, 1)

            def low_p(st):
                dve.wait_ge(p_hi, st.n + 1)
                dve.tensor_tensor(PL[st.s][:], PR[:], PH[st.s][:].bitcast(F32), ALU.subtract).then_inc(p_lo, 1)
            steps(dve, gate, KD, ends=True)
            barrier(dve, 4)

            dve.wait_ge(wo_hi, 1)
            dve.tensor_tensor(WOL[:], WOR[:], WOH[:].bitcast(F32), ALU.subtract).then_inc(wo_lo, 1)
            dve.wait_ge(r4_in, 80)

            def low_m(st, rows):
                dve.wait_ge(m_hi, st.n + 1)
                dve.tensor_tensor(ML[st.s][:, :, 0:rows], MR[st.s][:, :, 0:rows], MH[st.s][:, :, 0:rows].bitcast(F32), ALU.subtract).then_inc(m_lo, 1)
            low_m(Step(0, 0), P)
            low_m(Step(0, 1), P)

            def resid(st, rows, meanwhile):
                n, s = st.n, st.s
                dve.wait_ge(o_mm, n + 1)
                if not st.first:
                    dve.wait_ge(n2_st[s], st.t * 32)
                dve.tensor_tensor(X2[s][0:rows], ps[0:rows, 2 * s:2 * s + 2, :].rearrange("p b n -> p (b n)"), X4[s][0:rows], ALU.add).then_inc(x2_ready, 1)
                dve.wait_ge(x2_rms, n + 1)
                dve.reciprocal(rs4[0:rows], rt4[0:rows])
                dve.drain()
                dve.scalar_tensor_tensor(out=N2[s][0:rows], in0=X2[s][0:rows], scalar=rs4[0:rows], in1=g2b[0:rows], op0=ALU.mult, op1=ALU.mult).then_inc(n2_ready, 1)
                meanwhile()
                dve.wait_ge(l_mm, n + 1)
                dve.tensor_tensor(lgt[0:rows, bass.ds(n, 1), :].rearrange("p a c -> p (a c)"), ps[0:rows, 6, 0:GROUPS + NE], rb[0:rows], ALU.add).then_inc(l_ready, 1)

            steps(dve, lambda st: resid(st, P, lambda: low_m(st.ahead(2), P)), NFULL - 2)
            resid(Step(NFULL // 2 - 1, 0), P, lambda: low_m(Step(NFULL // 2, 0), NDEC))
            resid(Step(NFULL // 2 - 1, 1), P, lambda: None)
            resid(Step(NFULL // 2, 0), NDEC, lambda: None)
            barrier(dve, 5)

            lg, lx = lgt[:, :, 0:GROUPS], lgt[:, :, GROUPS:]
            wide = [P, NT, GROUPS]
            dve.wait_ge(r_c, 1)

            def onehot(out, vals, mx, tmp, n):
                dve.tensor_tensor(tmp[:], vals, mx[:].to_broadcast([P, NT, n]), ALU.is_equal)
                dve.drain()
                dve.scalar_tensor_tensor(out=tmp[:], in0=tmp[:], scalar=-1000.0, in1=ioE[:, :, 0:n], op0=ALU.mult, op1=ALU.add)
                dve.drain()
                dve.tensor_reduce(gmn[:], tmp[:], AX.X, ALU.min)
                dve.drain()
                dve.tensor_tensor(out[:], tmp[:], gmn[:].to_broadcast([P, NT, n]), ALU.is_equal)
                dve.drain()

            dve.tensor_reduce(gmx[:], lg, AX.X, ALU.max)
            dve.drain()
            dve.tensor_tensor(gva[:], lg, gmx[:].to_broadcast(wide), ALU.subtract).then_inc(r_mx, 1)
            onehot(ohg, lg, gmx, gtm, GROUPS)
            dve.tensor_scalar(gtm[:], ohg[:], -1.0, 1e30, ALU.add, ALU.mult)
            dve.drain()
            for g in range(GROUPS):
                dve.tensor_tensor(le[:, :, g * EPG:(g + 1) * EPG], lx[:, :, g * EPG:(g + 1) * EPG],
                                  gtm[:, :, g:g + 1].to_broadcast([P, NT, EPG]), ALU.add)
            dve.drain()
            for k in range(2):
                dve.tensor_reduce(v12[k][:], le[:], AX.X, ALU.max)
                dve.drain()
                onehot(oh[k], le[:], v12[k], ev, NE)
                if k == 0:
                    dve.scalar_tensor_tensor(out=le[:], in0=oh[0][:], scalar=-2e30, in1=le[:], op0=ALU.mult, op1=ALU.add)
                    dve.drain()
            dve.tensor_tensor(gd[:], v12[1][:], v12[0][:], ALU.subtract).then_inc(r_d, 1)
            dve.wait_ge(r_ex, 1)
            dve.tensor_reduce(gsm[:], gex[:], AX.X, ALU.add)
            dve.wait_ge(r_e2, 1)
            dve.tensor_scalar(gr[:], gd[:], 1.0, None, ALU.add)
            dve.drain()
            dve.tensor_tensor(gr[:], gr[:], gsm[:], ALU.mult)
            dve.drain()
            dve.reciprocal(gsm[:], gr[:])
            dve.drain()
            dve.tensor_copy(gates[:, :, 0:1], gsm[:])
            dve.tensor_tensor(gates[:, :, 1:2], gsm[:], gd[:], ALU.mult)
            dve.tensor_tensor(msk[:], oh[0][:], oh[1][:], ALU.add)
            dve.memset(cum[:, 0, :], 0.0)
            dve.drain()
            dve.memset(msk[NDEC:P, NFULL, :], 0.0)
            dve.drain()
            for t in range(1, NT):
                dve.tensor_tensor(cum[:, t, :], cum[:, t - 1, :], msk[:, t - 1, :], ALU.add)
                dve.drain()
            dve.tensor_tensor(tot[:], cum[:, NFULL, :], msk[:, NFULL, :], ALU.add)
            dve.drain().then_inc(r_msk, 1)
            dve.wait_ge(r_mm, 1)
            half = NT * NE // 2
            rf = rank[:].rearrange("p t e -> p (t e)")
            dve.tensor_copy(rf[:, 0:half], ps[:, 0, 0:half])
            dve.tensor_copy(rf[:, half:], ps[:, 1, 0:half])
            dve.tensor_copy(cnt[:], ps[:, 2, 0:NE])
            dve.drain()
            dve.tensor_copy(ranki[:], rank[:])
            dve.tensor_scalar(cnt[:], cnt[:], 1.0, -1.0, ALU.max, ALU.add)
            dve.drain()
            dve.tensor_copy(cnti[:], cnt[:])
            dve.tensor_scalar(ranki[:], ranki[:], BR_BITS, None, ALU.arith_shift_right)
            dve.drain()
            dve.tensor_scalar(cnti[:], cnti[:], BR_BITS, None, ALU.arith_shift_right)
            dve.tensor_copy(hib[:], ranki[:])
            dve.drain()
            dve.tensor_copy(ovf[:], cnti[:])
            dve.drain()
            dve.tensor_tensor_scan(ove[:], one64[:], ovf[:], 0.0, ALU.mult, ALU.add)
            dve.drain()
            dve.tensor_tensor(stw[:], ove[:], ovf[:], ALU.subtract)
            dve.drain()
            dve.tensor_tensor(stw[:], stw[:], ioE[:, 0, :], ALU.subtract)
            dve.drain()
            dve.tensor_scalar(stw[:], stw[:], float(NE - 1), None, ALU.add)
            dve.tensor_scalar(tE[:], hib[:], 0.0, None, ALU.is_gt)
            dve.drain()
            dve.tensor_tensor(tE[:], tE[:], stw[:].rearrange("p (a e) -> p a e", a=1).to_broadcast([P, NT, NE]), ALU.mult)
            dve.drain()
            dve.tensor_tensor(tE[:], tE[:], hib[:], ALU.add)
            dve.scalar_tensor_tensor(out=rank[:], in0=hib[:], scalar=-float(BR), in1=rank[:], op0=ALU.mult, op1=ALU.add)
            dve.drain()
            dve.tensor_tensor(tE[:], tE[:], ioE[:], ALU.add)
            dve.drain()
            dve.scalar_tensor_tensor(out=cum[:], in0=tE[:], scalar=float(BR), in1=rank[:], op0=ALU.mult, op1=ALU.add)
            dve.scalar_tensor_tensor(out=hib[:], in0=rank[:], scalar=float(NBLK), in1=tE[:], op0=ALU.mult, op1=ALU.add)
            dve.drain()
            for k in range(2):
                for rows, to in ((cum, dsty), (hib, dst)):
                    dve.tensor_tensor(tE[:], oh[k][:], rows[:], ALU.mult)
                    dve.drain()
                    dve.tensor_reduce(to[:, k, :], tE[:], AX.X, ALU.add)
                    dve.drain()
            dve.tensor_copy(yrow[:], dsty[:])
            for k in range(2):
                dve.memset(dst[NDEC:P, k, NFULL:NT], float(NOWHERE))
            dve.drain()
            dve.tensor_copy(dsti[:], dst[:])
            dve.drain().then_inc(r_dst, 1)
            dve.tensor_tensor(ovx[:], ove[0:1, :].rearrange("p (a e) -> p a e", a=1).to_broadcast([1, NOVF, NE]), ioV[:], ALU.is_le)
            dve.drain()
            dve.tensor_reduce(ovn[:, 0:NOVF], ovx[:], AX.X, ALU.add)
            dve.tensor_copy(ovn[:, NOVF:NOVF + 1], ove[0:1, NE - 1:NE])
            dve.drain()
            dve.tensor_scalar(ovn[:, 0:NOVF], ovn[:, 0:NOVF], float(NE - 1), None, ALU.min)
            dve.drain()
            dve.tensor_copy(eovf[:], ovn[:])
            barrier(dve, 6)

            def low1(st, i):
                dve.wait_ge(e1_hi, st.n * 2 + (i + 1))
                dve.tensor_tensor(E1L[st.s][:, i], E1[st.s][:, i], E1H[st.s][:, i].bitcast(F32), ALU.subtract).then_inc(e1_lo, 1)

            def low2(st):
                dve.wait_ge(e2_hi, st.n + 1)
                dve.tensor_tensor(E2L[st.s][:], E2[st.s][:], E2H[st.s][:].bitcast(F32), ALU.subtract).then_inc(e2_lo, 1)

            def x_lo(st):
                dve.wait_ge(xth, st.n + 1)
                dve.tensor_tensor(XTL[st.s][:, :, 0:BR], ps[:, 0, :].rearrange("p (k t) -> p k t", k=KD), XTH[st.s][:, :, 0:BR].bitcast(F32), ALU.subtract).then_inc(xtl, 1)

            def hidden(st):
                dve.wait_ge(h_sig, st.n + 1)
                if not (st.first and st.s == 0):
                    dve.wait_ge(h_tp, st.n)
                dve.tensor_tensor(hid[:], ps[0:BR, 2 + st.s, DE:2 * DE], sil[:], ALU.mult).then_inc(h_ready, 1)

            def h_lo(st):
                dve.wait_ge(hth, st.n + 1)
                dve.tensor_tensor(HTL[:, :, 0:BR], ps[:, 4, 0:2 * BR].rearrange("p (a t) -> p a t", a=2), HTH[:, :, 0:BR].bitcast(F32), ALU.subtract).then_inc(htl, 1)
            for b in XTH + XTL + [HTH, HTL]:
                dve.memset(b[:, :, BR:].bitcast(F32), 0.0)
            low1(Step(0, 0), 0)
            low1(Step(0, 0), 1)
            x_lo(Step(0, 0))

            def expert(st):
                nxt, prev = st.ahead(1), st.ahead(-1)
                more = nxt.within(NE)
                if prev.within(NE):
                    low2(prev)
                if more:
                    low1(nxt, 0)
                if prev.within(NE):
                    h_lo(prev)
                if more:
                    low1(nxt, 1)
                hidden(st)
                if more:
                    x_lo(nxt)
            steps(dve, expert, NE, ends=True)
            low2(Step(NE // 2 - 1, 1))
            h_lo(Step(NE // 2 - 1, 1))
            barrier(dve, 7)
            n_more = dve.value_load(eovf[0:1, NOVF:NOVF + 1], min_val=0, max_val=NOVF)
            with dve.If(n_more > 0):
                with dve.Fori(0, n_more) as j:
                    st = More(j)
                    low1(st, 0)
                    low1(st, 1)
                    low2(st)
                    x_lo(st)
                    hidden(st)
                    h_lo(st)
            barrier(dve, 8)

            dve.wait_ge(c_g, 16)

            def combine(st, rows):
                n, s = st.n, st.s
                dve.wait_ge(c_in[s], st.t * 16 + 16)
                dve.wait_ge(cy_in[s], st.t * 32 + 32)
                dve.tensor_copy(gt6[s][:], gates[:, bass.ds(n, 1), :].rearrange("p a k -> p (a k)"))
                dve.drain()
                if not st.first:
                    dve.wait_ge(c_out, n - 1)
                dve.scalar_tensor_tensor(out=FS[s][0:rows], in0=FY[s][0:rows, 0, :], scalar=gt6[s][0:rows, 0:1], in1=FX[s][0:rows], op0=ALU.mult, op1=ALU.add)
                dve.drain()
                dve.scalar_tensor_tensor(out=FS[s][0:rows], in0=FY[s][0:rows, 1, :], scalar=gt6[s][0:rows, 1:2], in1=FS[s][0:rows], op0=ALU.mult, op1=ALU.add)
                dve.drain().then_inc(c_sum, 1)
                dve.wait_ge(c_rms, n + 1)
                dve.reciprocal(rs6[0:rows], rt6[0:rows])
                dve.drain()
                if not st.first:
                    dve.wait_ge(c_st[s], st.t * 16)
                dve.scalar_tensor_tensor(out=FO[s][0:rows], in0=FS[s][0:rows], scalar=rs6[0:rows], in1=gfb[0:rows], op0=ALU.mult, op1=ALU.mult).then_inc(c_out, 1)
            token_tiles(dve, combine)
            barrier(dve, 9)

        @block.tensor
        def _(pe):
            pe.wait_ge(s_const, 1)

            def norm1(st, rows):
                n, s = st.n, st.s
                pe.wait_ge(xn_ready, n + 1)
                if not st.first:
                    pe.wait_ge(xl_ready, n - 1)
                for k in range(KD):
                    last = pe.transpose(xpos(s)[:, k, 0:rows], XN[s][0:rows, k * P:(k + 1) * P], ident[0:rows, 0:rows])
                last.then_inc(xt_done, 1)
            token_tiles(pe, norm1)
            pe.wait_ge(xl_ready, NT)

            def three(out, hi, lo, mhi, mlo, start, stop):
                pe.matmul(out, hi, mhi, start=start, stop=False)
                pe.matmul(out, hi, mlo, start=False, stop=False)
                return pe.matmul(out, lo, mhi, start=False, stop=stop)

            def t_chunk(col, st, all_, here):
                s = st.s
                pe.wait_ge(wl_ready, all_.n + 1)
                for tile in range(NT):
                    u = s * NT + tile
                    if not (all_.first and u < 6):
                        pe.wait_ge(t_ev, all_.n * NT + tile - 5)
                    cols = slice(tile * P, tile * P + P)
                    for k in range(KD):
                        last = three(ps[:, u % 6, 0:CW], XH[:, k, cols], XL[:, k, cols], WH[s][:, k, :], WL[s][:, k, :],
                                     k == 0, k == KD - 1)
                    last.then_inc(t_mm, 1)
                    if tile == NT - 1:
                        pe.drain().then_inc(w_used, 1)
            chunks(pe, T_TURNS, 0, t_chunk)

            def feature(f, wh, wl, nk, xh, xl):
                for k in range(nk):
                    for i, (w, x) in enumerate(((wh, xh), (wh, xl), (wl, xh))):
                        for g, (t0, tn) in enumerate(TG):
                            last = pe.matmul(ps[:, 3 * f + g, 0:tn], w[:, k, :], x[:, k, t0:t0 + tn],
                                             start=(k == 0 and i == 0), stop=(k == nk - 1 and i == 2))
                return last

            def f_chunk(col, st, all_, here):
                s = st.s
                pe.wait_ge(wl_ready, all_.n + 1)
                for f in range(2):
                    if here.first and here.s == 0:
                        pe.wait_ge(t_ev, NTC * NT)
                    else:
                        pe.wait_ge(f_ev, here.n * 2 + (f - 1))
                    last = feature(f, WH[s][:, :, f * P:(f + 1) * P], WL[s][:, :, f * P:(f + 1) * P], KD, XH, XL)
                    last.then_inc(f_mm, 1)
                pe.drain().then_inc(w_used, 1)
            chunks(pe, F_TURNS, NTC // 2, f_chunk)
            pe.wait_ge(a_lo, 1)
            pe.wait_ge(f_ev, 2 * NFC - 1)
            feature(0, WH[0][:, :, 0:P], WL[0][:, :, 0:P], KD, XH, XL).then_inc(a_mm, 1)
            barrier(pe, 1)

            pe.wait_ge(cm_tri, 2)
            for g in range(NCH):
                last = pe.transpose(ps[:, 0, g * P:(g + 1) * P], wsn[:, g, :], ident[:])
            last.then_inc(cm_wt, 1)
            for g in range(NCH):
                last = pe.transpose(ps[:, 1, g * NDEC:(g + 1) * NDEC], wsd[:, g, :], ident[0:NDEC, 0:NDEC])
            last.then_inc(cm_wt, 1)
            pe.wait_ge(cm_v, 1)
            pe.wait_ge(cm_wc, 2)
            for c in range(NCH):
                if c:
                    pe.wait_ge(cm_z, c)
                for t in range(NFULL):
                    pe.matmul(ps[:, 2 + t // 4, (t % 4) * P:(t % 4 + 1) * P], vvt[:, t, c * P:(c + 1) * P], wsT[:, c, :], start=True, stop=True)
                pe.matmul(ps[:, 4, 0:NDEC], vvt[0:NDEC, NFULL, c * P:(c + 1) * P], wsdT[:, c, :], start=True, stop=True).then_inc(cm_mm, 1)
            barrier(pe, 2)

            per = NCHUNK + DEC_B

            def decay_mm(st, g):
                n, (t0, tn) = st.n, TG[g]
                pe.wait_ge(g_pin, n * 64 + 64)
                wait_if_any(pe, g_zc, n * 3 + g)
                pe.matmul(ps[:, 2, 0:tn], a2h[:], alr[:, t0:t0 + tn], start=True, stop=True).then_inc(g_a, 1)

            def k_transpose(st, j):
                rows = rows_of(j)
                if st.n or j:
                    wait_alone(pe, g_kc, st.n * NT + j)
                pe.transpose(ps[0:rows, 3, 0:P], ke[st.s][:, j * P:j * P + rows], ident[:]).then_inc(g_kp, 1)

            def scores(st, j):
                rows = rows_of(j)
                wait_if_any(pe, g_am, st.n * NT + j)
                cols = slice(j * P, j * P + rows)
                pe.matmul(ps[0:rows, 7, 0:rows], kt[st.s][:, cols], qt[st.s][:, cols], start=True, stop=True).then_inc(g_ap, 1)

            def update(st, j):
                b = turn_of(st, j)
                pe.wait_ge(g_kc, st.n * NT + (j + 1))
                for c in (2 * j, 2 * j + 1):
                    lo = (c % 2) * CHUNK
                    wait_if_any(pe, g_s, st.n * per + (c - 1))
                    pe.matmul(ps[:, 5 + c % 2, 0:DV], ket[b][lo:lo + CHUNK, :], vt[st.s][lo:lo + CHUNK, j, :], start=True, stop=True).then_inc(g_u, 1)

            def out_mm_b(st, j):
                s, b = st.s, turn_of(st, j)
                wait_if_any(pe, g_n, st.n * NT + (j - 1))
                wait_alone(pe, g_am, st.n * NT + (j + 1))
                if j < NFULL:
                    pe.wait_ge(g_s, st.n * per + (2 * j + 1))
                    pe.matmul(ps[:, b, 0:DV], attm[b][:], vt[s][:, j, :], start=True, stop=False)
                    pe.matmul(ps[0:CHUNK, b, 0:DV], qt[s][:, j * P:j * P + CHUNK], S[:, 2 * j, :], start=False, stop=True)
                    pe.matmul(ps[CHUNK:P, b, 0:DV], qt[s][:, j * P + CHUNK:(j + 1) * P], S[:, 2 * j + 1, :], start=False, stop=True).then_inc(g_o, 1)
                else:
                    pe.matmul(ps[0:NDEC, b, 0:DV], attd[:], vt[s][0:NDEC, j, :], start=True, stop=False)
                    for q in range(DEC_B):
                        last = pe.matmul(ps[0:NDEC, b, 0:DV], qz[s][:, q, :], Sd[s][:, q, :], start=False, stop=(q == DEC_B - 1))
                    last.then_inc(g_o, 1)

            def update_d(st):
                pe.wait_ge(g_kz, st.n + 1)
                for q in range(DEC_B):
                    pe.wait_ge(g_s, st.n * per + (NCHUNK + q - 1))
                    pe.matmul(ps[:, 5 + q % 2, 0:DV], kz[:, q, :], vt[st.s][0:NDEC, NFULL, :], start=True, stop=True).then_inc(g_u, 1)

            def out_transpose(st, j):
                rows, b = rows_of(j), turn_of(st, j)
                wait_if_any(pe, g_tc, st.n * NT + j)
                wait_alone(pe, g_n, st.n * NT + (j + 1))
                for a in range(2):
                    last = pe.transpose(ps[:, 4, a * P:a * P + rows], og[b][0:rows, a * P:(a + 1) * P], ident[0:rows, 0:rows])
                last.then_inc(g_tp, 1)

            for g in range(3):
                decay_mm(Step(0, 0), g)

            def gla(st):
                nxt = st.ahead(1)
                more = nxt.within(HEADS)
                pe.wait_ge(g_q, st.n + 1)
                k_transpose(st, 0)
                scores(st, 0)
                pe.wait_ge(g_in[st.s], st.t * 80 + 80)
                update(st, 0)
                for j in range(NT):
                    if j + 1 < NT:
                        k_transpose(st, j + 1)
                        scores(st, j + 1)
                    if more and j < 3:
                        decay_mm(nxt, j)
                    if j + 1 < NFULL:
                        update(st, j + 1)
                    out_mm_b(st, j)
                    if j:
                        out_transpose(st, j - 1)
                update_d(st)
                out_transpose(st, NT - 1)
            steps(pe, gla, HEADS, ends=True)
            barrier(pe, 3)

            pe.wait_ge(z_lo, 16)

            def project(st):
                s, n = st.s, st.n
                pe.wait_ge(p_lo, n + 1)
                for b, (k0, kn) in enumerate(((0, 4), (4, 8), (12, 4))):
                    if not (st.first and s == 0 and b < 2):
                        pe.wait_ge(p_ev, n * 3 + (b - 1))
                    f = (s * 3 + b) % 2
                    feature(f, PH[s][:, k0:k0 + kn, :], PL[s][:, k0:k0 + kn, :], kn, ZH[:, k0:k0 + kn, :], ZL[:, k0:k0 + kn, :]).then_inc(p_mm, 1)
            steps(pe, project, KD)
            barrier(pe, 4)

            pe.wait_ge(wo_lo, 1)
            pe.wait_ge(r4_in, 80)

            def out_mm(st, rows):
                n, s = st.n, st.s
                pe.wait_ge(m_lo, n + 1)
                if not st.first:
                    pe.wait_ge(x2_ready, n - 1)
                for b in range(2):
                    for k in range(KD):
                        c = slice(b * 512, (b + 1) * 512)
                        last = three(ps[:, 2 * s + b, :], MH[s][:, k, :], ML[s][:, k, :], WOH[:, k, c], WOL[:, k, c], k == 0, k == KD - 1)
                last.then_inc(o_mm, 1)

            def router(st, rows):
                n, s = st.n, st.s
                pe.wait_ge(n2_ready, n + 1)
                if not (st.first and s == 0):
                    pe.wait_ge(n2_tc, n)
                tp = ps[:, 4:6, :].rearrange("p b (k t) -> p (b k) t", k=4)
                for k in range(KD):
                    last = pe.transpose(tp[:, k, 0:rows], N2[s][0:rows, k * P:(k + 1) * P], ident[0:rows, 0:rows])
                last.then_inc(n2_tp, 1)
                pe.wait_ge(n2_tc, n + 1)
                if not (st.first and s == 0):
                    pe.wait_ge(l_ready, n)
                for k in range(KD):
                    last = pe.matmul(ps[0:rows, 6, 0:GROUPS + NE], NTt[:, k, 0:rows], wr[:, k, :], start=(k == 0), stop=(k == KD - 1))
                last.then_inc(l_mm, 1)
            out_mm(Step(0, 0), P)

            def out_tile(st):
                out_mm(st.ahead(1), P)
                router(st, P)
            steps(pe, out_tile, NFULL - 2)
            last4 = Step(NFULL // 2 - 1, 0)
            out_tile(last4)
            out_mm(Step(NFULL // 2, 0), NDEC)
            router(last4.ahead(1), P)
            router(Step(NFULL // 2, 0), NDEC)
            barrier(pe, 5)

            pe.wait_ge(r_c, 1)
            pe.wait_ge(r_msk, 1)
            half = NT * NE // 2
            mflat, cflat = msk[:].rearrange("p t e -> p (t e)"), cum[:].rearrange("p t e -> p (t e)")
            for b in range(2):
                c = slice(b * half, (b + 1) * half)
                pe.matmul(ps[:, b, 0:half], ltri[:], mflat[:, c], start=True, stop=False)
                pe.matmul(ps[:, b, 0:half], onesm[:], cflat[:, c], start=False, stop=True)
            pe.matmul(ps[:, 2, 0:NE], onesm[:], tot[:], start=True, stop=True).then_inc(r_mm, 1)
            barrier(pe, 6)

            xgp = ps[:, 0, :].rearrange("p (k t) -> p k t", k=KD)

            def x_t(st):
                n, s = st.n, st.s
                if not (st.first and s == 0):
                    pe.wait_ge(xtl, n)
                wait_alone(pe, xg_in[s], st.t * 16 + 16)
                xg = XG[s][:].rearrange("p (q k) -> p k q", k=KD)
                for k in range(KD):
                    last = pe.transpose(xgp[:, k, :], xg[:, k, :], ident[0:BR, 0:BR])
                last.then_inc(xg_tp, 1)

            def h_mul(st):
                n, s = st.n, st.s
                pe.wait_ge(xtl, n + 1)
                pe.wait_ge(e1_lo, n * 2 + 2)
                if not st.first:
                    pe.wait_ge(h_ready, n - 1)
                for k in range(KD):
                    last = three(ps[:, 2 + s, :], XTH[s][:, k, :], XTL[s][:, k, :], E1H[s][:, :, k, :], E1L[s][:, :, k, :], k == 0, k == KD - 1)
                last.then_inc(h_mm, 1)

            def h_t(st):
                n = st.n
                if not (st.first and st.s == 0):
                    pe.wait_ge(htl, n)
                wait_alone(pe, h_ready, n + 1)
                hv = hid[:].rearrange("p (q k) -> p k q", k=2)
                for k in range(2):
                    last = pe.transpose(ps[:, 4, k * BR:(k + 1) * BR], hv[:, k, :], ident[0:BR, 0:BR])
                last.then_inc(h_tp, 1)

            def y_mul(st):
                n, s = st.n, st.s
                pe.wait_ge(htl, n + 1)
                pe.wait_ge(e2_lo, n + 1)
                if not (st.first and s == 0):
                    pe.wait_ge(y_ready, n)
                for b in range(2):
                    for k in range(2):
                        c = slice(b * 512, (b + 1) * 512)
                        last = three(ps[:, 5 + b, :], HTH[:, k, :], HTL[:, k, :], E2H[s][:, k, c], E2L[s][:, k, c], k == 0, k == 1)
                last.then_inc(y_mm, 1)
            x_t(Step(0, 0))

            def expert(st):
                h_mul(st)
                if st.ahead(1).within(NE):
                    x_t(st.ahead(1))
                if st.ahead(-1).within(NE):
                    y_mul(st.ahead(-1))
                h_t(st)
            steps(pe, expert, NE, ends=True)
            y_mul(Step(NE // 2 - 1, 1))
            barrier(pe, 7)
            n_more = pe.value_load(eovf[0:1, NOVF:NOVF + 1], min_val=0, max_val=NOVF)
            with pe.If(n_more > 0):
                with pe.Fori(0, n_more) as j:
                    st = More(j)
                    x_t(st)
                    h_mul(st)
                    h_t(st)
                    y_mul(st)
            barrier(pe, 8)
            barrier(pe, 9)


_INS = ['x_prompt', 'x_sample', 'state_conv', 'state_gla', 'norm1_g', 'w_in', 'conv_w', 'gla_a2', 'gla_a_b',
        'gla_norm_g', 'cm_norm_g', 'cm_ws', 'cm_b', 'proj_a', 'proj_b', 'proj_c', 'w_out', 'norm2_g',
        'router_group_w', 'router_group_b', 'router_expert_w', 'router_expert_b',
        'exp_w1', 'exp_w3', 'exp_w2', 'final_norm_g']
_OUTS = [(1, SEQ, D), (DEC_B, DEC_T, D), (1, 1, 2, CONV_CH), (1, 1, HEADS, DK, DV),
         (1, DEC_B, 2, CONV_CH), (1, DEC_B, HEADS, DK, DV), (1, DEC_B, DEC_T, CONV_CH)]


def kernel(**inputs):
    import numpy as _np
    import concourse.bacc as _bacc
    from concourse import mybir as _mybir
    from concourse.bass_utils import run_bass_kernel_spmd as _run

    nc = _bacc.Bacc("TRN2", target_bir_lowering=False, num_devices=1)
    arrays, args = {}, []
    for name in _INS:
        a = _np.ascontiguousarray(inputs[name])
        arrays[f"in_{name}_dram"] = a
        args.append(nc.dram_tensor(f"in_{name}_dram", a.shape, _mybir.dt.from_np(a.dtype), kind="ExternalInput").ap())
    for i, shape in enumerate(_OUTS):
        args.append(nc.dram_tensor(f"out_{i}_dram", shape, _mybir.dt.float32, kind="ExternalOutput").ap())
    trunk(nc, *args)
    r = _run(nc, [arrays], core_ids=[0])
    return tuple(r.results[0][f"out_{i}_dram"] for i in range(len(_OUTS)))
```

```python
import concourse.bass as bass
from concourse import mybir
from contextlib import ExitStack

F32 = mybir.dt.float32
F32R = mybir.dt.float32r
I32 = mybir.dt.int32
ALU = mybir.AluOpType
ACT = mybir.ActivationFunctionType
AX = mybir.AxisListType

P = 128
D = 1024
KD = D // P
SEQ = 1024
DEC_B, DEC_T = 8, 8
NDEC = DEC_B * DEC_T
NTOK = SEQ + NDEC
NFULL = SEQ // P
NT = NFULL + 1
CONV_CH = 512
NCH = CONV_CH // P
HEADS, DK, DV = 4, 128, 256
CHUNK = 64
NCHUNK = SEQ // CHUNK
TAU = 16.0
LOWRANK = 16
GROUPS, EPG = 8, 8
NE = GROUPS * EPG
DE = 256
EPS = 1e-6
C_H, C_CG, C_BG, C_Q, C_K = 0, 512, 1024, 1536, 2048
C_V, C_R, C_A, C_U, C_VV, C_G = 2560, 3584, 4608, 4624, 5136, 5648
D_IN = 8720
CW = 256
TG = [(0, 384), (384, 384), (768, 320)]
NPAD = NT * P
BR = 64
NSLOT = 2 * NTOK
NOVF = (NSLOT - 1) // BR
NBLK = NE + NOVF
NOWHERE = 1 << 20
EMPTY = 4 * NTOK
BR_BITS = BR.bit_length() - 1


def rows_of(tile):
    return P if tile < NFULL else NDEC


def trunk(nc, x_prompt, x_sample, state_conv, state_gla, norm1_g, w_in, conv_w, gla_a2, gla_a_b,
          gla_norm_g, cm_norm_g, cm_ws, cm_b, proj_a, proj_b, proj_c, w_out, norm2_g,
          rg_w, rg_b, re_w, re_b, exp_w1, exp_w3, exp_w2, final_g,
          y_prompt, y_sample, conv_p, gla_p, conv_s, gla_s, chunk_v):
    def dram(name, shape, dt=F32):
        return nc.dram_tensor(name, shape, dt, kind="Internal").ap()

    feat = dram("feat", (D_IN, NTOK))
    tokd = dram("tokd", (NTOK, 2560))
    zT = dram("zT", (16 * P, NTOK))
    mixT = dram("mixT", (D, NTOK))
    x2d = dram("x2d", (NTOK, D))
    xn2d = dram("xn2d", (NTOK, D))
    table = dram("slot_table", (BR * NBLK, 1), I32)
    yb = dram("yb", (NBLK * BR, D))

    xp = x_prompt[0]
    xs = x_sample.rearrange("a b n -> (a b) n")
    w_in_v = w_in[0].rearrange("(k p) c -> p k c", p=P)
    ctx = ExitStack()
    with ctx:
        def sem(name):
            return ctx.enter_context(nc.semaphore(name))

        def sem2(name):
            return [sem(f"{name}{i}") for i in range(2)]

        def sbuf(stack):
            return lambda name, shape, dt=F32: stack.enter_context(nc.sbuf_tensor(name, shape, dt))

        keep = sbuf(ctx)
        ident = keep("ident", [P, P])
        epsc = keep("epsc", [P, 1])
        yt = keep("yt", [P, NTOK])
        alr = yt[0:LOWRANK]
        gates = keep("gates", [P, NT, 2])
        lgt = keep("lgt", [P, NT, GROUPS + NE])
        tidx = keep("tidx", [BR, NBLK], I32)
        yrow = keep("yrow", [P, 2, NT], I32)
        eovf = keep("eovf", [1, NOVF + 1], I32)

        ph = ExitStack()
        sb = sbuf(ph)
        XH = sb("XH", [P, KD, NPAD], F32R)
        XL = sb("XL", [P, KD, NPAD], F32R)
        RAW = [sb(f"RAW{i}", [P, KD, CW]) for i in range(2)]
        WH = [sb(f"WH{i}", [P, KD, CW], F32R) for i in range(2)]
        WL = [sb(f"WL{i}", [P, KD, CW], F32R) for i in range(2)]
        OF = [sb(f"OF{i}", [P, 2, NTOK]) for i in range(2)]
        ph1 = ExitStack()
        sb = sbuf(ph1)
        OT = [sb(f"OT{i}", [P, NT, CW]) for i in range(2)]
        g1b = sb("g1b", [P, D])
        X = [sb(f"X{i}", [P, D]) for i in range(2)]
        XN = [sb(f"XN{i}", [P, D]) for i in range(2)]
        ssq = [sb(f"ssq{i}", [P, 1]) for i in range(2)]
        rtt = [sb(f"rtt{i}", [P, 1]) for i in range(2)]
        rst = [sb(f"rst{i}", [P, 1]) for i in range(2)]
        junk = sb("junk", [P, D])
        ph1.close()
        ph1 = ExitStack()
        sb = sbuf(ph1)
        cbuf = sb("cbuf", [P, 5, NTOK])
        cH, cG, cB, cout, uT = (cbuf[:, i, :] for i in range(5))
        vsq = cbuf[:].rearrange("p a n -> p (a n)")[:, 0:NT * CONV_CH].rearrange("p (t c) -> p t c", t=NT)
        cwt = sb("cwt", [P, 3])
        cpp = sb("cpp", [P, 2 + SEQ])
        cps = sb("cps", [P, DEC_B, 2 + DEC_T])
        vvt = sb("vvt", [P, NT, CONV_CH])
        vss = sb("vss", [P, NT * NCH])
        vrs = sb("vrs", [P, NT * NCH])
        cmg = sb("cmg", [P, CONV_CH])
        wsn = sb("wsn", [P, NCH, P])
        wsd = sb("wsd", [NDEC, NCH, P])
        wsT = sb("wsT", [P, NCH, P])
        wsdT = sb("wsdT", [NDEC, NCH, NDEC])
        cmb = sb("cmb", [P, NCH, P])
        zc = sb("zc", [P, NTOK])
        smz = sb("smz", [P, NCH, NDEC])
        ph1.close()
        ph.close()

        ph = ExitStack()
        sb = sbuf(ph)
        a2h = sb("a2h", [LOWRANK, P])
        abh = sb("abh", [P, 1])
        qT = sb("qT", [P, NTOK])
        kT = sb("kT", [P, NTOK])
        vt = [sb(f"vt{i}", [P, NT, DV]) for i in range(2)]
        rt = [sb(f"rt{i}", [P, NT, DV]) for i in range(2)]
        rg = sb("rg", [P, DV])
        seg = sb("seg", [P, NTOK])
        zz = sb("zz", [P, NTOK])
        t1 = sb("t1", [P, NTOK])
        cs = sb("cs", [P, NTOK])
        eb = [sb(f"eb{i}", [P, NTOK]) for i in range(2)]
        qt = [sb(f"qt{i}", [P, NTOK]) for i in range(2)]
        kt = [sb(f"kt{i}", [P, NTOK]) for i in range(2)]
        ke = [sb(f"ke{i}", [P, NTOK]) for i in range(2)]
        qz = [sb(f"qz{i}", [P, DEC_B, NDEC]) for i in range(2)]
        ket = [sb(f"ket{i}", [P, P]) for i in range(3)]
        kz = sb("kz", [NDEC, DEC_B, P])
        rmask = sb("rmask", [NDEC, DEC_B])
        attm = [sb(f"attm{i}", [P, P]) for i in range(2)]
        attd = sb("attd", [NDEC, NDEC])
        mp = sb("mp", [P, P], I32)
        md = sb("md", [NDEC, NDEC], I32)
        mdf = sb("mdf", [NDEC, NDEC])
        mf = sb("mf", [P, P])
        S = sb("S", [P, NCHUNK + 1, DV])
        Sd = [sb(f"Sd{i}", [P, DEC_B, DV]) for i in range(2)]
        Sn = sb("Sn", [P, DEC_B, DV])
        osq = [sb(f"osq{i}", [P, DV]) for i in range(2)]
        og = [sb(f"og{i}", [P, DV]) for i in range(2)]
        oss = [sb(f"oss{i}", [P, 1]) for i in range(2)]
        ors = [sb(f"ors{i}", [P, 1]) for i in range(2)]
        orc = [sb(f"orc{i}", [P, 1]) for i in range(2)]
        zb = [sb(f"zb{i}", [P, 2, NTOK]) for i in range(2)]
        ph.close()

        ph = ExitStack()
        sb = sbuf(ph)
        ZH = sb("ZH", [P, 16, NTOK], F32R)
        ZL = sb("ZL", [P, 16, NTOK], F32R)
        PR = sb("PR", [P, 16, P])
        PH = [sb(f"PH{i}", [P, 16, P], F32R) for i in range(2)]
        PL = [sb(f"PL{i}", [P, 16, P], F32R) for i in range(2)]
        sg = sb("sg", [P, 3, NTOK])
        ymixs = sb("ymixs", [P, 2, NTOK])
        ymix = [ymixs[:, 0, :], ymixs[:, 1, :]]
        zr = [sg[:, 0, :], sg[:, 1, :], sg[:, 2, :]] + ymix
        NZ = len(zr)
        ph.close()

        ph = ExitStack()
        sb = sbuf(ph)
        WOR = sb("WOR", [P, KD, D])
        WOH = sb("WOH", [P, KD, D], F32R)
        WOL = sb("WOL", [P, KD, D], F32R)
        MR = [sb(f"MR{i}", [P, KD, P]) for i in range(2)]
        MH = [sb(f"MH{i}", [P, KD, P], F32R) for i in range(2)]
        ML = [sb(f"ML{i}", [P, KD, P], F32R) for i in range(2)]
        X4 = [sb(f"X4{i}", [P, D]) for i in range(2)]
        X2 = [sb(f"X2{i}", [P, D]) for i in range(2)]
        N2 = [sb(f"N2{i}", [P, D]) for i in range(2)]
        NTt = sb("NTt", [P, KD, P])
        g2b = sb("g2b", [P, D])
        wr = sb("wr", [P, KD, GROUPS + NE])
        rb = sb("rb", [P, GROUPS + NE])
        ss4 = sb("ss4", [P, 1])
        rt4 = sb("rt4", [P, 1])
        rs4 = sb("rs4", [P, 1])
        sq4 = sb("sq4", [P, D])
        ph.close()

        ph = ExitStack()
        sb = sbuf(ph)
        gmx = sb("gmx", [P, NT, 1])
        gsm = sb("gsm", [P, NT, 1])
        gmn = sb("gmn", [P, NT, 1])
        gex = sb("gex", [P, NT, GROUPS])
        gva = sb("gva", [P, NT, GROUPS])
        gtm = sb("gtm", [P, NT, GROUPS])
        ohg = sb("ohg", [P, NT, GROUPS])
        le = sb("le", [P, NT, NE])
        ev = sb("ev", [P, NT, NE])
        v12 = [sb(f"v{i}", [P, NT, 1]) for i in range(2)]
        gd = sb("gd", [P, NT, 1])
        gr = sb("gr", [P, NT, 1])
        oh = [sb(f"oh{i}", [P, NT, NE]) for i in range(2)]
        msk = sb("msk", [P, NT, NE])
        cum = sb("cum", [P, NT, NE])
        rank = sb("rank", [P, NT, NE])
        hib = sb("hib", [P, NT, NE])
        tE = sb("tE", [P, NT, NE])
        tot = sb("tot", [P, NE])
        cnt = sb("cnt", [P, NE])
        ovf = sb("ovf", [P, NE])
        ove = sb("ove", [P, NE])
        stw = sb("stw", [P, NE])
        dst = sb("dst", [P, 2, NT])
        ranki = sb("ranki", [P, NT, NE], I32)
        cnti = sb("cnti", [P, NE], I32)
        dsty = sb("dsty", [P, 2, NT])
        dsti = sb("dsti", [P, 2, NT], I32)
        ovx = sb("ovx", [1, NOVF, NE])
        iV = sb("iV", [1, NOVF, NE], I32)
        ioV = sb("ioV", [1, NOVF, NE])
        ovn = sb("ovn", [1, NOVF + 1])
        ph.close()

        ph = ExitStack()
        sb = sbuf(ph)
        E1H, E1L, E2H, E2L = ([None, sb(f"{n}1", shape, F32R)] for n, shape in
                              (("E1H", [P, 2, KD, DE]), ("E1L", [P, 2, KD, DE]), ("E2H", [P, 2, D]), ("E2L", [P, 2, D])))
        YS = [sb(f"YS{i}", [BR, D]) for i in range(2)]
        E1H[0] = sb("E1H0", [P, 2, KD, DE], F32R)
        E1L[0] = sb("E1L0", [P, 2, KD, DE], F32R)
        E2H[0] = sb("E2H0", [P, 2, D], F32R)
        E2L[0] = sb("E2L0", [P, 2, D], F32R)
        XG = [sb(f"XG{i}", [BR, D]) for i in range(2)]
        XTH = [sb(f"XTH{i}", [P, KD, P], F32R) for i in range(2)]
        XTL = [sb(f"XTL{i}", [P, KD, P], F32R) for i in range(2)]
        sil = sb("sil", [BR, DE])
        hid = sb("hid", [BR, DE])
        HTH = sb("HTH", [P, 2, P], F32R)
        HTL = sb("HTL", [P, 2, P], F32R)
        gix = [sb(f"gix{i}", [BR, 1], I32) for i in range(2)]
        E1 = [sb(f"E1{i}", [P, 2, KD, DE]) for i in range(2)]
        E2 = [sb(f"E2{i}", [P, 2, D]) for i in range(2)]
        iE = sb("iE", [P, NT, NE], I32)
        ioE = sb("ioE", [P, NT, NE])
        one64 = sb("one64", [P, NE])
        slot = sb("slot", [P, NT], I32)
        ltri = sb("ltri", [P, P])
        onesm = sb("onesm", [P, P])
        emp = sb("emp", [BR, NBLK], I32)
        FX = [sb(f"FX{i}", [P, D]) for i in range(2)]
        gfb = sb("gfb", [P, D])
        ph.close()

        ph = ExitStack()
        sb = sbuf(ph)
        FY = [sb(f"FY{i}", [P, 2, D]) for i in range(2)]
        FS = [sb(f"FS{i}", [P, D]) for i in range(2)]
        FO = [sb(f"FO{i}", [P, D]) for i in range(2)]
        jf = sb("jf", [P, D])
        gt6 = [sb(f"gt6{i}", [P, 2]) for i in range(2)]
        cix = [sb(f"cix{i}", [P, 2], I32) for i in range(2)]
        ss6 = sb("ss6", [P, 1])
        rt6 = sb("rt6", [P, 1])
        rs6 = sb("rs6", [P, 1])
        ph.close()

        ps = ctx.enter_context(nc.psum_tensor("ps", [P, 8, 512], F32))

        s_bar = sem("phase_done")
        s_const = sem("constants_ready")
        s_alone = {e.engine: sem(f"alone_{n}") for n, e in
                   (("sp", nc.sync), ("pool", nc.gpsimd), ("dve", nc.vector), ("pe", nc.tensor))}

        def barrier(eng, k):
            eng.drain().then_inc(s_bar, 1)
            eng.wait_ge(s_bar, 5 * k)

        def wait_alone(eng, sem_, value):
            eng.wait_ge(sem_, value)
            eng.sem_inc(s_alone[eng.engine], 1)

        def wait_if_any(eng, sem_, value):
            if not (isinstance(value, int) and value <= 0):
                eng.wait_ge(sem_, value)

        def turn_of(st, j, buffers=2):
            return (st.s * NT + j) % buffers

        def xpos(s):
            return ps[:, 4 + 2 * s:6 + 2 * s, :].rearrange("p b (k t) -> p (b k) t", k=4)

        yz_ready, yz_st = sem("zeros_ready"), sem("zeros_stored")
        x_in, g1_in = sem2("x_in"), sem("norm1_gain_in")
        rms_ready, xn_ready, xt_done = sem("rms_ready"), sem("xn_ready"), sem("xn_transposed")
        xh_ready, xl_ready = sem("xh_ready"), sem("xl_ready")
        w_in_s = sem2("w_chunk_in")
        wh_ready, wl_ready, w_used = sem("wh_ready"), sem("wl_ready"), sem("w_used")
        t_mm, t_ev, t_st = sem("tok_product"), sem("tok_evacuated"), sem2("tok_stored")
        f_mm, f_ev, f_st = sem("feat_product"), sem("feat_evacuated"), sem2("feat_stored")
        a_in, a_mm = (sem(f"lowrank_{n}") for n in ("in", "product"))
        cv_in, cv_st, cv_z = sem("conv_in"), sem("conv_stored"), sem("conv_done")
        cm_in, cm_wd0, cm_w, cm_wt, cm_wc = (sem(f"mlp_{n}") for n in ("in", "zeroed_and_masked", "diag_in", "w_transposed", "w_copied"))
        cm_sq, cm_rt, cm_v, cm_mm, cm_z, cm_st, cm_u, cm_vc = (
            sem(f"mlp_{n}") for n in ("v_squares", "v_rms", "v_normed", "mixed", "done", "stored", "u_in", "v_copied"))
        g_in, g_din, g_pin, g_r = sem2("gla_in"), sem("gla_decay_in"), sem("gla_qk_in"), sem("gla_gain_in")
        g_c, g_a, g_zc, g_z, g_b, g_e, g_q = (
            sem(f"gla_{n}") for n in ("consts", "decay_product", "decay_copied", "decay_ln", "decay_sum", "decay_exp", "qk"))
        g_kp, g_kc, g_u, g_s = (sem(f"gla_{n}") for n in ("k_transposed", "k_copied", "update", "state"))
        g_ap, g_am, g_o = (sem(f"gla_{n}") for n in ("scores", "scores_masked", "out"))
        g_kz = sem("gla_k_masked")
        g_rg, g_rt, g_n, g_tp, g_tc = (sem(f"gla_{n}") for n in ("r_gain", "out_rms", "out_normed", "out_transposed", "done"))
        g_st, g_sv = sem2("gla_stored"), sem("gla_states_stored")
        z_in, z_hi, z_lo = [sem(f"z_in{i}") for i in range(NZ)], sem("z_hi"), sem("z_lo")
        p_in, p_hi, p_lo, p_mm, p_ev = (sem(f"proj_{n}") for n in ("in", "hi", "lo", "product", "gated"))
        sg_in, mix_ready, mix_st = sem("gate_in"), sem("mix_ready"), sem("mix_stored")
        wo_in, wo_hi, wo_lo, m_in, m_hi, m_lo = [sem(f"wo_in{i}") for i in range(4)], sem("wo_hi"), sem("wo_lo"), sem2("mix_in"), sem("mix_hi"), sem("mix_lo")
        r4_in, o_mm, x2_ready, x2_rms, n2_ready, n2_tp, n2_tc, l_mm, l_ready = (
            sem(n) for n in ("router_in", "out_product", "x2_ready", "x2_rms", "xn2_ready", "xn2_transposed", "xn2_copied", "logit_product", "logits_ready"))
        n2_st = sem2("xn2_stored")
        r_c, r_df, r_ex, r_msk, r_mm, r_dst, r_tab, r_sc = (
            sem(f"route_{n}") for n in ("consts", "differences", "exponentials", "mask", "ranks", "rows", "table", "table_filled"))
        e_in = [sem2(f"expert_w{w}_in") for w in (1, 3, 2)]
        xg_in, y_st, i_gx = sem2("x_gathered"), sem2("y_stored"), sem("gather_index")
        e1_hi, e1_lo, e2_hi, e2_lo = sem("e1_hi"), sem("e1_lo"), sem("e2_hi"), sem("e2_lo")
        xg_tp, xth, xtl, h_mm, h_sig, h_ready, h_tp, hth, htl, y_mm, y_ready = (
            sem(f"e_{n}") for n in ("x_transposed", "x_hi", "x_lo", "h_product", "h_silu", "h_ready", "h_transposed", "h_hi", "h_lo", "y_product", "y_ready"))
        cy_in, c_ix = sem2("c_y_in"), sem("c_index")
        c_in, c_g, c_sum, c_rms, c_out, c_st = sem2("c_in"), sem("c_gain"), sem("c_sum"), sem("c_rms"), sem("c_out"), sem2("c_stored")

        class Step:
            def __init__(self, turn, slot):
                self.t, self.s, self.n = turn, slot, turn * 2 + slot
                self.static = isinstance(turn, int)
                self.first = self.static and turn == 0

            def ahead(self, d):
                return Step(self.t + (self.s + d) // 2, (self.s + d) % 2)

            def within(self, n):
                return not self.static or 0 <= self.n < n

        def steps(eng, body, n, ends=False):
            body(Step(0, 0))
            body(Step(0, 1))
            last = n // 2 - ends
            if last > 1:
                with eng.Fori(1, last) as t:
                    body(Step(t, 0))
                    body(Step(t, 1))
            if ends:
                body(Step(last, 0))
                body(Step(last, 1))
            if n % 2:
                body(Step(n // 2, 0))

        class More(Step):
            def __init__(self, j):
                self.t, self.s, self.n = j + NE // 2, 0, j + NE
                self.static = self.first = False

        def token_tiles(eng, body):
            steps(eng, lambda st: body(st, P), NFULL)
            body(Step(NFULL // 2, 0), NDEC)

        T_TURNS = [(C_V, 2), (C_R, 2), (C_VV, 1)]
        F_TURNS = [(C_H, 4), (C_K, 1), (C_U, 1), (C_G, 6)]
        NTC = 2 * sum(n for _, n in T_TURNS)
        NFC = 2 * sum(n for _, n in F_TURNS)

        F0 = NTC // 2
        GATES0 = F0 + 6

        def chunks(eng, all_turns, base, body, base0=None):
            base0 = base if base0 is None else base0
            for col, n in all_turns:
                lo = 0
                if base == base0 or n == 1:
                    for s in range(2):
                        body(col, Step(0, s), Step(base, s), Step(base - base0, s))
                    lo = 1
                if n > lo:
                    with eng.Fori(lo, n) as t:
                        for s in range(2):
                            body(col, Step(t, s), Step(t + base, s), Step(t + (base - base0), s))
                base += n

        def gate_chunks(eng, body, before, middle, after, n=6):
            def turn(t, work):
                if work:
                    before(t)
                body(C_G, Step(t, 0), Step(t + GATES0, 0), Step(t + (GATES0 - F0), 0))
                if work:
                    middle(t)
                body(C_G, Step(t, 1), Step(t + GATES0, 1), Step(t + (GATES0 - F0), 1))
                if work:
                    after(t)
            turn(0, True)
            with eng.Fori(1, NCH) as t:
                turn(t, True)
            with eng.Fori(NCH, n) as t:
                turn(t, False)

        def nothing(c):
            pass

        def but_chunk0(body):
            def go(col, st, all_, here):
                if not (all_.first and all_.s == 0):
                    body(col, st, all_, here)
            return go

        def tok(t, rows=P):
            return slice(SEQ, NTOK) if rows < P else bass.ds(t * P, P)

        block = ctx.enter_context(nc.Block())
        ctx.enter_context(nc.allow_non_contiguous_dma(reason="short columns of weights and states"))

        @block.sync
        def _(sp):
            sp.dma_start(g1b[:], norm1_g[0:1, :].to_broadcast([P, D])).then_inc(g1_in, 16)

            def load_x(st, rows):
                if not st.first:
                    sp.wait_ge(xn_ready, st.n - 1)
                src = xs[:, :] if rows < P else xp[tok(st.n), :]
                sp.dma_start(X[st.s][0:rows], src).then_inc(x_in[st.s], 16)
            def load_w(col, st, all_, here):
                if not all_.first:
                    sp.wait_ge(wl_ready, all_.n - 1)
                sp.dma_start(RAW[st.s][:], w_in_v[:, :, bass.ds(st.n * CW + col, CW)]).then_inc(w_in_s[st.s], 16)
            load_x(Step(0, 0), P)
            load_x(Step(0, 1), P)
            load_w(C_V, Step(0, 0), Step(0, 0), Step(0, 0))
            for n in range(2, NT):
                load_x(Step(n // 2, n % 2), rows_of(n))
            chunks(sp, T_TURNS, 0, but_chunk0(load_w))
            chunks(sp, F_TURNS[:1], F0, load_w)
            for s in range(2):
                sp.wait_ge(t_st[s], 32 * F0)
            sp.wait_ge(cm_wd0, 2)
            sp.dma_start(vvt[:, 0:NFULL, :], tokd[0:SEQ, 2048:2560].rearrange("(t p) c -> p t c", p=P)).then_inc(cm_in, 16)
            sp.dma_start(vvt[0:NDEC, NFULL, :], tokd[SEQ:NTOK, 2048:2560]).then_inc(cm_in, 16)
            sp.dma_start(cmg[:], cm_norm_g[0:1].rearrange("a g c -> a (g c)").to_broadcast([P, CONV_CH])).then_inc(cm_in, 16)
            sp.dma_start(cmb[:].rearrange("p g t -> p (g t)"),
                         cm_b[0:1].rearrange("a g t -> a (g t)").to_broadcast([P, NCH * P])).then_inc(cm_in, 16)
            sp.dma_start(wsn[:], cm_ws[0].rearrange("g t s -> t g s")).then_inc(cm_w, 16)
            for q in range(DEC_B):
                sp.dma_start(wsd[q * DEC_T:(q + 1) * DEC_T, :, q * DEC_T:(q + 1) * DEC_T],
                             cm_ws[0][:, 0:DEC_T, 0:DEC_T].rearrange("g t s -> t g s")).then_inc(cm_w, 16)
            chunks(sp, F_TURNS[1:3], F0 + 4, load_w, F0)

            def conv_load(c):
                for to, base in ((cH, C_H), (cG, C_CG), (cB, C_BG)):
                    sp.dma_start(to, feat[bass.ds(c * P + base, P), :]).then_inc(cv_in, 16)
                sp.dma_start(cwt[:], conv_w[0][:, bass.ds(c * P, P)].rearrange("k p -> p k")).then_inc(cv_in, 16)
                for b in range(2):
                    sp.dma_start(cps[:, :, b], state_conv[0][:, b, bass.ds(c * P, P)].rearrange("s p -> p s")).then_inc(cv_in, 16)

            def conv_store(c):
                sp.wait_ge(cv_z, c + 1)
                sp.dma_start(zT[bass.ds(c * P, P), :], cout).then_inc(cv_st, 16)
                sp.dma_start(conv_p[0, 0][:, bass.ds(c * P, P)].rearrange("k p -> p k"), cpp[:, SEQ:SEQ + 2]).then_inc(cv_st, 16)
                for b in range(2):
                    sp.dma_start(conv_s[0][:, b, bass.ds(c * P, P)].rearrange("s p -> p s"),
                                 cps[:, :, DEC_T + b]).then_inc(cv_st, 16)

            def mlp_load(c):
                sp.dma_start(uT, feat[bass.ds(c * P + C_U, P), :]).then_inc(cm_u, 16)

            def mlp_store(c):
                sp.wait_ge(cm_z, c + 1)
                sp.dma_start(zT[bass.ds(c * P + 12 * P, P), :], zc[:]).then_inc(cm_st, 16)

            def branches(c):
                if isinstance(c, int):
                    for s in range(2):
                        sp.wait_ge(f_st[s], 16 * 3)
                    sp.wait_ge(cm_v, 1)
                    conv_load(c)
                    sp.dma_start(chunk_v[0].rearrange("b t c -> (b t) c"), vvt[0:NDEC, NFULL, :]).then_inc(cm_st, 16)
                    for s in range(2):
                        sp.wait_ge(f_st[s], 16 * 6)
                    mlp_load(c)
                else:
                    conv_store(c - 1)
                    wait_alone(sp, cv_st, c * 64)
                    conv_load(c)
                    mlp_store(c - 1)
                    mlp_load(c)
            gate_chunks(sp, load_w, nothing, nothing, branches)
            conv_store(NCH - 1)
            mlp_store(NCH - 1)
            sp.wait_ge(wl_ready, NTC + NFC - 1)
            sp.dma_start(RAW[0][:, :, 0:P], w_in_v[:, :, C_A:C_A + P]).then_inc(a_in, 16)
            sp.wait_ge(cv_st, 64 * NCH)
            sp.wait_ge(cm_st, 16 * (1 + NCH))
            barrier(sp, 1)


            def load_qk(st):
                h = st.n
                wait_if_any(sp, g_q, h * 2)
                sp.dma_start(a2h[:], gla_a2[0][:, bass.ds(h * P, P)]).then_inc(g_din, 16)
                sp.dma_start(abh[:], gla_a_b[0:1, bass.ds(h * P, P)].rearrange("a p -> p a")).then_inc(g_din, 16)
                sp.dma_start(qT[:], feat[bass.ds(h * P + C_Q, P), :]).then_inc(g_pin, 16)
                sp.dma_start(kT[:], feat[bass.ds(h * P + C_K, P), :]).then_inc(g_pin, 16)

            def load_head(st):
                h, s = st.n, st.s
                for to, base in ((vt[s], 0), (rt[s], 1024)):
                    sp.dma_start(to[:, 0:NFULL, :], tokd[0:SEQ, bass.ds(h * DV + base, DV)]
                                 .rearrange("(t p) c -> p t c", p=P)).then_inc(g_in[s], 16)
                    sp.dma_start(to[0:NDEC, NFULL, :], tokd[SEQ:NTOK, bass.ds(h * DV + base, DV)]).then_inc(g_in[s], 16)
                sp.dma_start(Sd[s][:], state_gla[0][:, bass.ds(h, 1)].rearrange("s a d e -> d (s a) e")).then_inc(g_in[s], 16)

            load_qk(Step(0, 0))
            sp.dma_start(rg[:], gla_norm_g[0:1, :].to_broadcast([P, DV])).then_inc(g_r, 16)
            sp.wait_ge(g_c, 1)
            load_head(Step(0, 0))
            load_qk(Step(0, 1))

            def gla(st):
                h, s = st.n, st.s
                if st.ahead(1).within(HEADS):
                    load_head(st.ahead(1))
                if st.ahead(2).within(HEADS):
                    load_qk(st.ahead(2))
                out = zT[bass.ds(h * DV + 4 * P, DV), :].rearrange("(a p) n -> p a n", p=P)
                sp.wait_ge(g_tc, h * NT + NFULL)
                sp.dma_start(out[:, :, 0:SEQ], zb[s][:, :, 0:SEQ]).then_inc(g_st[s], 16)
                sp.wait_ge(g_s, h * (NCHUNK + DEC_B) + NCHUNK + DEC_B)
                sp.dma_start(gla_p[0, 0][bass.ds(h, 1)].rearrange("a d e -> (a d) e"), S[:, NCHUNK, :]).then_inc(g_sv, 16)
                sp.dma_start(gla_s[0][:, bass.ds(h, 1)].rearrange("s a d e -> d (s a) e"), Sn[:]).then_inc(g_sv, 16)
                sp.wait_ge(g_tc, h * NT + NT)
                sp.dma_start(out[:, :, SEQ:NTOK], zb[s][:, :, SEQ:NTOK]).then_inc(g_st[s], 16)
            steps(sp, gla, HEADS, ends=True)
            sp.wait_ge(g_sv, 32 * HEADS)
            for s in range(2):
                sp.wait_ge(g_st[s], 32 * (HEADS // 2))
            barrier(sp, 2)

            def load_weights(st):
                if not (st.first and st.s == 0):
                    sp.wait_ge(p_lo, st.n)
                for k0, kn, w in ((0, 4, proj_a), (4, 8, proj_b), (12, 4, proj_c)):
                    sp.dma_start(PR[:, k0:k0 + kn, :], w[0].rearrange("(k p) c -> p k c", p=P)[:, :, bass.ds(st.n * P, P)]).then_inc(p_in, 16)

            load_weights(Step(0, 0))
            for n in range(16):
                if n >= NZ:
                    sp.wait_ge(z_lo, n - NZ + 1)
                sp.dma_start(zr[n % NZ], zT[n * P:(n + 1) * P, :]).then_inc(z_in[n % NZ], 16)
            sp.wait_ge(z_lo, 16)

            def load_proj(st):
                n = st.n
                again = not (st.first and st.s == 0)
                if again:
                    load_weights(st)
                    sp.wait_ge(mix_ready, n)
                    sp.dma_start(mixT[bass.ds((n - 1) * P, P), :], ymix[1 - st.s]).then_inc(mix_st, 16)
                for b in range(3):
                    sp.dma_start(sg[:, b, :], feat[bass.ds(n * P + C_G + b * D, P), :]).then_inc(sg_in, 16)
                if again:
                    wait_alone(sp, mix_st, n * 16)
            steps(sp, load_proj, KD)
            sp.wait_ge(mix_ready, KD)
            sp.dma_start(mixT[(KD - 1) * P:KD * P, :], ymix[1]).then_inc(mix_st, 16)
            sp.wait_ge(mix_st, 16 * KD)
            barrier(sp, 3)

            def load_wo(i):
                sp.dma_start(WOR[:, 2 * i:2 * i + 2, :], w_out[0].rearrange("(k p) c -> p k c", p=P)[:, 2 * i:2 * i + 2, :]).then_inc(wo_in[i], 16)
            load_wo(0)
            def load_r4():
                sp.dma_start(g2b[:], norm2_g[0:1, :].to_broadcast([P, D])).then_inc(r4_in, 16)
                sp.dma_start(wr[:, :, 0:GROUPS], rg_w[0].rearrange("(k p) c -> p k c", p=P)).then_inc(r4_in, 16)
                sp.dma_start(wr[:, :, GROUPS:], re_w[0].rearrange("(k p) c -> p k c", p=P)).then_inc(r4_in, 16)
                sp.dma_start(rb[:, 0:GROUPS], rg_b[0:1, :].to_broadcast([P, GROUPS])).then_inc(r4_in, 16)
                sp.dma_start(rb[:, GROUPS:], re_b[0:1, :].to_broadcast([P, NE])).then_inc(r4_in, 16)

            def load_m(st, rows):
                if not st.first:
                    sp.wait_ge(m_lo, st.n - 1)
                    sp.wait_ge(x2_ready, st.n - 1)
                mv = mixT.rearrange("(k p) n -> p k n", p=P)
                sp.dma_start(MR[st.s][:, :, 0:rows], mv[:, :, tok(st.n, rows)]).then_inc(m_in[st.s], 16)
                src = xs[:, :] if rows < P else xp[tok(st.n), :]
                sp.dma_start(X4[st.s][0:rows], src).then_inc(m_in[st.s], 16)
            load_m(Step(0, 0), P)
            for i in range(1, 4):
                load_wo(i)
            load_m(Step(0, 1), P)
            load_r4()
            with sp.Fori(1, NFULL // 2) as t:
                load_m(Step(t, 0), P)
                load_m(Step(t, 1), P)
            load_m(Step(NFULL // 2, 0), NDEC)
            barrier(sp, 4)

            def load_expert(e, s, wait):
                for i, w in enumerate((exp_w1, exp_w3)):
                    wait(i)
                    sp.dma_start(E1[s][:, i, :, :], w[0][bass.ds(e, 1)].rearrange("a (p k) c -> p (a k) c", k=KD)).then_inc(e_in[i][s], 16)
                wait(2)
                sp.dma_start(E2[s][:], exp_w2[0][bass.ds(e, 1)].rearrange("a (p k) c -> p (a k) c", k=2)).then_inc(e_in[2][s], 16)

            def expert(st):
                def wait(i):
                    if not st.first:
                        if i < 2:
                            sp.wait_ge(e1_lo, st.n * 2 - 3 + i)
                        else:
                            sp.wait_ge(e2_lo, st.n - 1)
                load_expert(st.n, st.s, wait)
            expert(Step(0, 0))
            expert(Step(0, 1))

            sp.wait_ge(r_c, 1)
            sp.dma_start(table.rearrange("(p b) a -> p (b a)", p=BR), emp[:]).then_inc(r_tab, 16)
            expert(Step(1, 0))
            sp.wait_ge(r_sc, 16 * 2 * NT)
            sp.dma_start(tidx[:], table.rearrange("(p b) a -> p (b a)", p=BR)).then_inc(r_tab, 16)
            sp.wait_ge(r_tab, 32)
            barrier(sp, 5)

            expert(Step(1, 1))
            with sp.Fori(2, NE // 2) as t:
                expert(Step(t, 0))
                expert(Step(t, 1))

            def load_c(st, rows):
                if not st.first:
                    sp.wait_ge(c_sum, st.n - 1)
                r0 = SEQ if rows < P else st.n * P
                sp.dma_start(FX[st.s][0:rows], x2d[bass.ds(r0, rows), :]).then_inc(c_in[st.s], 16)
            sp.dma_start(gfb[:], final_g.rearrange("(a n) -> a n", a=1).to_broadcast([P, D])).then_inc(c_g, 16)
            load_c(Step(0, 0), P)
            load_c(Step(0, 1), P)
            barrier(sp, 6)
            n_more = sp.value_load(eovf[0:1, NOVF:NOVF + 1], min_val=0, max_val=NOVF)
            with sp.If(n_more > 0):
                with sp.Fori(0, n_more) as j:
                    e = sp.value_load(eovf[0:1, bass.ds(j, 1)], min_val=0, max_val=NE - 1)
                    sp.wait_ge(y_ready, j + NE)
                    load_expert(e, 0, lambda i: None)
            barrier(sp, 7)

            with sp.Fori(1, NFULL // 2) as t:
                load_c(Step(t, 0), P)
                load_c(Step(t, 1), P)
            load_c(Step(NFULL // 2, 0), NDEC)
            barrier(sp, 8)

        @block.gpsimd
        def _(pool):
            pool.memset(ident[:], 0.0)
            pool.memset(epsc[:], EPS)
            pool.memset(lgt[:, NFULL, :], 0.0)
            pool.drain()
            pool.affine_select(out=ident[:], in_=ident[:], compare_op=ALU.not_equal, fill=1.0, base=0,
                               pattern=[[-1, P]], channel_multiplier=1).then_inc(s_const, 1)

            pool.memset(yt[:], 0.0).then_inc(yz_ready, 1)

            def store_zeros(part):
                pool.wait_ge(yz_ready, 1)
                b0, n = NE + part * (NOVF // 3), NOVF // 3 if part < 2 else NOVF - 2 * (NOVF // 3)
                pool.dma_start(yb[b0 * BR:(b0 + n) * BR, :].rearrange("(b p) c -> p b c", p=BR),
                               yt[0:BR, 0:D].rearrange("p (a c) -> p a c", a=1).to_broadcast([BR, n, D])).then_inc(yz_st, 16)

            def store_t(col, st, all_, here):
                base = {C_V: 0, C_R: 1024, C_VV: 2048}[col]
                pool.wait_ge(t_ev, all_.n * NT + NT)
                cols = bass.ds(st.n * CW + base, CW)
                pool.dma_start(tokd[0:SEQ, cols].rearrange("(t p) c -> p t c", p=P), OT[st.s][:, 0:NFULL, :]).then_inc(t_st[st.s], 16)
                pool.dma_start(tokd[SEQ:NTOK, cols], OT[st.s][0:NDEC, NFULL, :]).then_inc(t_st[st.s], 16)
            chunks(pool, T_TURNS, 0, store_t)

            def store_f(col, st, all_, here):
                pool.wait_ge(f_ev, here.n * 2 + 2)
                pool.dma_start(feat[bass.ds(st.n * CW + col, CW), :].rearrange("(a p) n -> p a n", p=P), OF[st.s][:]).then_inc(f_st[st.s], 16)
            for s in range(2):
                pool.wait_ge(t_st[s], 32 * F0)
            pool.memset(wsd[:], 0.0).then_inc(cm_wd0, 1)
            pool.memset(vvt[:, NFULL, :], 0.0).then_inc(cm_wd0, 1)
            store_zeros(0)
            chunks(pool, F_TURNS[:1], F0, store_f)
            store_zeros(1)
            pool.wait_ge(cm_w, 16 * (1 + DEC_B))
            pool.affine_select(out=wsn[:], in_=wsn[:], compare_op=ALU.is_ge, fill=0.0, base=0,
                               pattern=[[0, NCH], [-1, P]], channel_multiplier=1).then_inc(cm_wd0, 1)
            pool.affine_select(out=wsd[:], in_=wsd[:], compare_op=ALU.is_ge, fill=0.0, base=0,
                               pattern=[[0, NCH], [-1, P]], channel_multiplier=1).then_inc(cm_wd0, 1)
            chunks(pool, F_TURNS[1:3], F0 + 4, store_f, F0)
            store_zeros(2)
            gate_chunks(pool, store_f, nothing, nothing, nothing)
            for s in range(2):
                pool.wait_ge(t_st[s], 32 * (NTC // 2))
                pool.wait_ge(f_st[s], 16 * (NFC // 2))
            pool.wait_ge(yz_st, 48)
            barrier(pool, 1)

            pool.memset(mf[:], 1.0)
            pool.memset(mdf[:], 1.0)
            pool.memset(rmask[:], 1.0)
            pool.memset(seg[:], 1.0)
            pool.memset(S[:, 0, :], 0.0)
            for s in range(2):
                pool.memset(qz[s][:], 0.0)
                pool.memset(rt[s][:, NFULL, :], 0.0)
            for b in attm:
                pool.memset(b[:], 0.0)
            pool.memset(attd[:], 0.0)
            pool.drain()
            pool.memset(seg[:, 0:SEQ].rearrange("p (c t) -> p c t", t=CHUNK)[:, :, 0:1], 0.0)
            pool.memset(seg[:, SEQ:NTOK].rearrange("p (c t) -> p c t", t=DEC_T)[:, :, 0:1], 0.0)
            pool.affine_select(out=mf[:], in_=mf[:], compare_op=ALU.is_ge, fill=0.0, base=0,
                               pattern=[[1, P]], channel_multiplier=-1)
            pool.affine_select(out=mdf[:], in_=mdf[:], compare_op=ALU.is_ge, fill=0.0, base=0,
                               pattern=[[1, NDEC]], channel_multiplier=-1)
            pool.affine_select(out=rmask[:], in_=rmask[:], compare_op=ALU.is_ge, fill=0.0, base=0,
                               pattern=[[-DEC_T, DEC_B]], channel_multiplier=1)
            pool.drain()
            pool.memset(mf[0:CHUNK, CHUNK:P], 0.0)
            pool.affine_select(out=mdf[:], in_=mdf[:], compare_op=ALU.is_ge, fill=0.0, base=0,
                               pattern=[[-DEC_T, DEC_B], [0, DEC_T]], channel_multiplier=1)
            pool.affine_select(out=rmask[:], in_=rmask[:], compare_op=ALU.is_ge, fill=0.0, base=DEC_T - 1,
                               pattern=[[DEC_T, DEC_B]], channel_multiplier=-1)
            pool.drain()
            pool.tensor_copy(mp[:], mf[:])
            pool.tensor_copy(md[:], mdf[:])
            pool.drain().then_inc(g_c, 1)
            pool.wait_ge(g_r, 16)

            def r_gain(st):
                pool.wait_ge(g_in[st.s], st.t * 80 + 80)
                pool.tensor_tensor(rt[st.s][:], rt[st.s][:], rg[:].rearrange("p (a c) -> p a c", a=1).to_broadcast([P, NT, DV]),
                                   ALU.mult).then_inc(g_rg, 1)
            def decayed_k(st):
                pool.wait_ge(g_pin, st.n * 32 + 32)
                pool.wait_ge(g_e, st.n + 1)
                pool.tensor_tensor(kt[st.s][:], kT[:], t1[:], ALU.mult)
                pool.tensor_tensor(ke[st.s][:], kT[:], zz[:], ALU.mult)
                pool.drain().then_inc(g_q, 1)

            def gla(st):
                r_gain(st)
                if st.ahead(1).within(HEADS):
                    decayed_k(st.ahead(1))
            decayed_k(Step(0, 0))
            steps(pool, gla, HEADS, ends=True)
            barrier(pool, 2)
            barrier(pool, 3)

            pool.memset(emp[:], EMPTY)
            pool.memset(onesm[:], 1.0)
            pool.memset(ltri[:], 1.0)
            pool.memset(one64[:], 1.0)
            pool.iota(iE[:], pattern=[[0, NT], [1, NE]], base=0, channel_multiplier=0)
            pool.iota(slot[:], pattern=[[P, NT]], base=0, channel_multiplier=1)
            pool.drain()
            pool.affine_select(out=ltri[:], in_=ltri[:], compare_op=ALU.is_gt, fill=0.0, base=0,
                               pattern=[[1, P]], channel_multiplier=-1)
            pool.tensor_copy(ioE[:], iE[:])
            pool.drain().then_inc(r_c, 1)

            def store_n2(st, rows):
                pool.wait_ge(n2_ready, st.n + 1)
                pool.dma_start(x2d[tok(st.n, rows), :], X2[st.s][0:rows]).then_inc(n2_st[st.s], 16)
                pool.dma_start(xn2d[tok(st.n, rows), :], N2[st.s][0:rows]).then_inc(n2_st[st.s], 16)
            token_tiles(pool, store_n2)
            pool.wait_ge(n2_st[0], 32 * (NFULL // 2 + 1))
            pool.wait_ge(n2_st[1], 32 * (NFULL // 2))
            barrier(pool, 4)

            pool.iota(iV[:], pattern=[[1, NOVF], [0, NE]], base=0, channel_multiplier=0)
            pool.drain()
            pool.tensor_copy(ioV[:], iV[:])
            pool.drain().then_inc(r_c, 1)
            pool.memset(XG[0][:], 0.0)
            pool.memset(XG[1][:], 0.0)
            pool.drain()
            pool.wait_ge(r_tab, 16)
            pool.wait_ge(r_dst, 1)
            for t in range(NT):
                for k in range(2):
                    pool.indirect_dma_start(out=table[:, :], out_offset=bass.IndirectOffsetOnAxis(ap=dsti[:, k, t:t + 1], axis=0),
                                            in_=slot[:, t:t + 1], in_offset=None,
                                            bounds_check=BR * NBLK - 1, oob_is_err=False).then_inc(r_sc, 16)
            pool.wait_ge(r_sc, 16 * 2 * NT)
            barrier(pool, 5)


            def gather(st, lag=2):
                n, s = st.n, st.s
                if lag == 1 or not st.first:
                    pool.wait_ge(xg_tp, n + 1 - lag)
                    pool.wait_ge(xg_in[s], st.t * 16)
                pool.tensor_copy(gix[s][:], tidx[:, bass.ds(n, 1)]).then_inc(i_gx, 1)
                wait_alone(pool, i_gx, n + 1)
                pool.indirect_dma_start(out=XG[s][:], out_offset=None, in_=xn2d[:, :],
                                        in_offset=bass.IndirectOffsetOnAxis(ap=gix[s][:, 0:1], axis=0),
                                        bounds_check=NTOK - 1, oob_is_err=False).then_inc(xg_in[s], 16)

            gather(Step(0, 0))
            gather(Step(0, 1))
            with pool.Fori(1, NE // 2) as t:
                gather(Step(t, 0))
                gather(Step(t, 1))
            barrier(pool, 6)
            n_more = pool.value_load(eovf[0:1, NOVF:NOVF + 1], min_val=0, max_val=NOVF)
            with pool.If(n_more > 0):
                with pool.Fori(0, n_more) as j:
                    gather(More(j), lag=1)
            barrier(pool, 7)

            def gather_c(st, rows):
                n, s = st.n, st.s
                if not st.first:
                    pool.wait_ge(c_sum, n - 1)
                pool.tensor_copy(cix[s][:], yrow[:, :, bass.ds(n, 1)].rearrange("p k a -> p (k a)")).then_inc(c_ix, 1)
                wait_alone(pool, c_ix, n + 1)
                for k in range(2):
                    pool.indirect_dma_start(out=FY[s][0:rows, k, :], out_offset=None, in_=yb[:, :],
                                            in_offset=bass.IndirectOffsetOnAxis(ap=cix[s][0:rows, k:k + 1], axis=0),
                                            bounds_check=NBLK * BR - 1, oob_is_err=False).then_inc(cy_in[s], 16)
            gather_c(Step(0, 0), P)
            gather_c(Step(0, 1), P)

            def store_c(st, rows):
                pool.wait_ge(c_out, st.n + 1)
                out = y_sample.rearrange("a b n -> (a b) n") if rows < P else y_prompt[0][tok(st.n), :]
                pool.dma_start(out, FO[st.s][0:rows]).then_inc(c_st[st.s], 16)

            def move_c(st):
                gather_c(st.ahead(2), P)
                store_c(st, P)
            steps(pool, move_c, NFULL - 2)
            gather_c(Step(NFULL // 2, 0), NDEC)
            store_c(Step(NFULL // 2 - 1, 0), P)
            store_c(Step(NFULL // 2 - 1, 1), P)
            store_c(Step(NFULL // 2, 0), NDEC)
            pool.wait_ge(c_st[0], 16 * (NFULL // 2 + 1))
            pool.wait_ge(c_st[1], 16 * (NFULL // 2))
            barrier(pool, 8)

        @block.scalar
        def _(act):
            act.wait_ge(s_const, 1)

            def squares(n):
                s, rows = n % 2, rows_of(n)
                act.wait_ge(x_in[s], n // 2 * 16 + 16)
                act.activation(junk[0:rows], X[s][0:rows], ACT.Square, accum_out=ssq[s][0:rows])
                act.drain()
                act.activation(rtt[s][0:rows], ssq[s][0:rows], ACT.Sqrt, bias=epsc[0:rows], scale=1.0 / D).then_inc(rms_ready, 1)

            def x_high(n):
                s, rows = n % 2, rows_of(n)
                act.wait_ge(xt_done, n + 1)
                act.activation(XH[:, :, tok(n, rows)], xpos(s)[:, :, 0:rows], ACT.Copy).then_inc(xh_ready, 1)

            def split_w(all_):
                n, s = all_.n, all_.s
                act.wait_ge(w_in_s[s], all_.t * 16 + 16)
                if not all_.first:
                    act.wait_ge(w_used, n - 1)
                act.activation(WH[s][:], RAW[s][:], ACT.Copy).then_inc(wh_ready, 1)

            def evacuate(col, all_, tile):
                s, rows = all_.s, rows_of(tile)
                act.wait_ge(t_mm, all_.n * NT + tile + 1)
                if tile == 0 and not all_.first:
                    act.wait_ge(t_st[s], all_.t * 32)
                func = {C_V: ACT.Copy, C_R: ACT.Silu, C_VV: ACT.Gelu_apprx_tanh}[col]
                act.activation(OT[s][0:rows, tile, :], ps[0:rows, tile % 3, 0:CW], func).then_inc(t_ev, 1)

            squares(0)
            squares(1)
            split_w(Step(0, 0))
            for n in range(NT):
                x_high(n)
                if n + 2 < NT:
                    squares(n + 2)
                if n:
                    evacuate(C_V, Step(0, 0), n - 1)
            split_w(Step(0, 1))
            evacuate(C_V, Step(0, 0), NT - 1)

            def t_chunk(col, st, all_, here):
                split_w(all_.ahead(1))
                for tile in range(NT):
                    evacuate(col, all_, tile)
            chunks(act, T_TURNS, 0, but_chunk0(t_chunk))

            def f_chunk(func, last=None):
                def go(col, st, all_, here):
                    s = st.s
                    if not (last and st.static and s == 1):
                        split_w(all_.ahead(1))
                    for f in range(2):
                        act.wait_ge(f_mm, here.n * 2 + (f + 1))
                        if f == 0 and not here.first:
                            act.wait_ge(f_st[s], here.t * 16)
                        act.activation(OF[s][:, f, 0:768].rearrange("p (g n) -> p g n", g=2), ps[:, 3 * f:3 * f + 2, 0:384], func)
                        act.activation(OF[s][:, f, 768:NTOK], ps[:, 3 * f + 2, 0:320], func).then_inc(f_ev, 1)
                return go
            b = F0
            for s in range(2):
                f_chunk(ACT.Copy)(C_H, Step(0, s), Step(b, s), Step(0, s))
            with act.Fori(1, 4) as t:
                for s in range(2):
                    f_chunk(ACT.Copy)(C_H, Step(t, s), Step(t + b, s), Step(t, s))
            act.wait_ge(cm_in, 64)
            act.activation(vsq, vvt[:], ACT.Square).then_inc(cm_sq, 1)
            act.wait_ge(cm_wt, 1)
            act.activation(wsT[:], ps[:, 6, :].rearrange("p (g t) -> p g t", g=NCH), ACT.Copy).then_inc(cm_wc, 1)
            act.activation(wsdT[:], ps[0:NDEC, 7, 0:NCH * NDEC].rearrange("p (g t) -> p g t", g=NCH), ACT.Copy).then_inc(cm_wc, 1)
            f_chunk(ACT.Copy)(C_K, Step(0, 0), Step(b + 4, 0), Step(4, 0))
            act.wait_ge(cm_rt, 1)
            act.activation(vrs[:], vss[:], ACT.Sqrt, bias=epsc[:], scale=1.0 / P).then_inc(cm_rt, 1)
            f_chunk(ACT.Copy)(C_K, Step(0, 1), Step(b + 4, 1), Step(4, 1))
            for s in range(2):
                f_chunk(ACT.Gelu_apprx_tanh)(C_U, Step(0, s), Step(b + 5, s), Step(5, s))
            act.wait_ge(cm_wt, 2)
            act.activation(smz[:], ps[:, 6, 0:NCH * NDEC].rearrange("p (g t) -> p g t", g=NCH), ACT.Copy).then_inc(cm_wc, 1)
            with act.Fori(0, 5) as t:
                for s in range(2):
                    f_chunk(ACT.Sigmoid)(C_G, Step(t, s), Step(t + (b + 6), s), Step(t + 6, s))
            for s in range(2):
                f_chunk(ACT.Sigmoid, last=True)(C_G, Step(5, s), Step(b + 11, s), Step(11, s))
            act.wait_ge(a_in, 16)
            act.wait_ge(w_used, NTC + NFC)
            act.activation(WH[0][:, :, 0:P], RAW[0][:, :, 0:P], ACT.Copy).then_inc(wh_ready, 1)
            act.wait_ge(a_mm, 1)
            act.wait_ge(yz_st, 48)
            act.activation(alr[:, 0:768].rearrange("p (g n) -> p g n", g=2), ps[0:LOWRANK, 0:2, 0:384], ACT.Copy)
            act.activation(alr[:, 768:NTOK], ps[0:LOWRANK, 2, 0:320], ACT.Copy)
            barrier(act, 1)

            def decay_copy(st, g):
                n, (t0, tn) = st.n, TG[g]
                if g == 0:
                    act.wait_ge(g_din, n * 32 + 32)
                    wait_if_any(act, g_q, n * 2)
                act.wait_ge(g_a, n * 3 + g + 1)
                act.activation(zz[:, t0:t0 + tn], ps[:, 2, 0:tn], ACT.Identity, bias=abh[:]).then_inc(g_zc, 1)

            def decay_abs(st):
                act.drain()
                act.activation(t1[:], zz[:], ACT.Abs)
                act.drain()
                act.activation(t1[:], t1[:], ACT.Exp, scale=-1.0)
                act.drain()

            def decay_ln(st):
                act.activation(t1[:], t1[:], ACT.Ln, bias=1.0).then_inc(g_z, 1)

            def decay_exp(st):
                act.wait_ge(g_b, st.n * 2 + 1)
                act.activation(eb[st.s][:], cs[:], ACT.Exp, scale=1.0 / TAU)
                act.activation(t1[:], cs[:], ACT.Exp, scale=-1.0 / TAU)

            def decay_exp_end(st):
                act.wait_ge(g_b, st.n * 2 + 2)
                act.activation(zz[:], zz[:], ACT.Exp, scale=1.0 / TAU).then_inc(g_e, 1)

            def k_copy(st, j):
                rows, b = rows_of(j), turn_of(st, j, 3)
                act.wait_ge(g_kp, st.n * NT + (j + 1))
                act.activation(ket[b][0:rows], ps[0:rows, 3, 0:P], ACT.Copy).then_inc(g_kc, 1)

            def out_rms(st, j):
                rows, b = rows_of(j), turn_of(st, j)
                act.wait_ge(g_o, st.n * NT + (j + 1))
                wait_if_any(act, g_n, st.n * NT + (j - 1))
                act.activation(osq[b][0:rows], ps[0:rows, b, 0:DV], ACT.Square, accum_out=oss[b][0:rows])
                act.drain()
                act.activation(ors[b][0:rows], oss[b][0:rows], ACT.Sqrt, bias=epsc[0:rows], scale=1.0 / DV).then_inc(g_rt, 1)

            def out_copy(st, j):
                rows = rows_of(j)
                act.wait_ge(g_tp, st.n * NT + (j + 1))
                if j == 0:
                    wait_if_any(act, g_st[st.s], st.t * 32)
                act.activation(zb[st.s][:, :, j * P:j * P + rows], ps[:, 4, 0:DV].rearrange("p (a t) -> p a t", a=2)[:, :, 0:rows],
                               ACT.Copy).then_inc(g_tc, 1)

            for g in range(3):
                decay_copy(Step(0, 0), g)
            decay_abs(Step(0, 0))
            decay_ln(Step(0, 0))
            decay_exp(Step(0, 0))
            decay_exp_end(Step(0, 0))

            def gla(st):
                nxt = st.ahead(1)
                more = nxt.within(HEADS)
                k_copy(st, 0)
                k_copy(st, 1)
                for j in range(NT):
                    if j + 2 < NT:
                        k_copy(st, j + 2)
                    if more and 1 <= j < 4:
                        decay_copy(nxt, j - 1)
                    if j:
                        out_copy(st, j - 1)
                    out_rms(st, j)
                    if more and 3 <= j < 7:
                        (decay_abs, decay_ln, decay_exp, decay_exp_end)[j - 3](nxt)
                out_copy(st, NT - 1)
            steps(act, gla, HEADS, ends=True)
            barrier(act, 2)

            def hi_z(n):
                act.wait_ge(z_in[n % NZ], n // NZ * 16 + 16)
                act.activation(ZH[:, n, :], zr[n % NZ], ACT.Copy).then_inc(z_hi, 1)

            def hi_p(st):
                act.wait_ge(p_in, st.n * 48 + 48)
                if not st.first:
                    act.wait_ge(p_mm, st.n * 3 - 3)
                act.activation(PH[st.s][:], PR[:], ACT.Copy).then_inc(p_hi, 1)
            hi_p(Step(0, 0))
            for n in range(16):
                hi_z(n)
            hi_p(Step(0, 1))
            with act.Fori(1, KD // 2) as t:
                hi_p(Step(t, 0))
                hi_p(Step(t, 1))
            barrier(act, 3)

            def hi_wo(i):
                act.wait_ge(wo_in[i], 16)
                act.activation(WOH[:, 2 * i:2 * i + 2, :], WOR[:, 2 * i:2 * i + 2, :], ACT.Copy).then_inc(wo_hi, 1)

            def hi_m(st, rows):
                act.wait_ge(m_in[st.s], st.t * 32 + 32)
                if not st.first:
                    act.wait_ge(o_mm, st.n - 1)
                act.activation(MH[st.s][:, :, 0:rows], MR[st.s][:, :, 0:rows], ACT.Copy).then_inc(m_hi, 1)

            def norm2(st, rows, meanwhile):
                act.wait_ge(x2_ready, st.n + 1)
                act.activation(sq4[0:rows], X2[st.s][0:rows], ACT.Square, accum_out=ss4[0:rows])
                act.drain()
                act.activation(rt4[0:rows], ss4[0:rows], ACT.Sqrt, bias=epsc[0:rows], scale=1.0 / D).then_inc(x2_rms, 1)
                meanwhile()
                act.wait_ge(n2_tp, st.n + 1)
                if not (st.first and st.s == 0):
                    act.wait_ge(l_mm, st.n)
                act.activation(NTt[:, :, 0:rows], ps[:, 4:6, :].rearrange("p b (k t) -> p (b k) t", k=4)[:, :, 0:rows], ACT.Copy).then_inc(n2_tc, 1)
            hi_wo(0)
            hi_m(Step(0, 0), P)
            for i in range(1, 4):
                hi_wo(i)
            hi_m(Step(0, 1), P)
            steps(act, lambda st: norm2(st, P, lambda: hi_m(st.ahead(2), P)), NFULL - 2)
            norm2(Step(NFULL // 2 - 1, 0), P, lambda: hi_m(Step(NFULL // 2, 0), NDEC))
            norm2(Step(NFULL // 2 - 1, 1), P, lambda: None)
            norm2(Step(NFULL // 2, 0), NDEC, lambda: None)
            barrier(act, 4)

            act.wait_ge(r_df, 1)
            act.activation(gex[:], gva[:], ACT.Exp).then_inc(r_ex, 1)
            act.wait_ge(r_df, 2)
            act.activation(gd[:], gd[:], ACT.Exp).then_inc(r_ex, 1)

            def split1(st, i, lag=2):
                act.wait_ge(e_in[i][st.s], st.t * 16 + 16)
                if i == 0 and (lag == 1 or not st.first):
                    act.wait_ge(h_mm, st.n + 1 - lag)
                act.activation(E1H[st.s][:, i], E1[st.s][:, i], ACT.Copy).then_inc(e1_hi, 1)

            def split2(st, lag=2):
                act.wait_ge(e_in[2][st.s], st.t * 16 + 16)
                if lag == 1 or not st.first:
                    act.wait_ge(y_mm, st.n + 1 - lag)
                act.activation(E2H[st.s][:], E2[st.s][:], ACT.Copy).then_inc(e2_hi, 1)

            split1(Step(0, 0), 0)
            split1(Step(0, 0), 1)
            split2(Step(0, 0))
            barrier(act, 5)

            def x_hi(st):
                act.wait_ge(xg_tp, st.n + 1)
                act.activation(XTH[st.s][:, :, 0:BR], ps[:, 0, :].rearrange("p (k t) -> p k t", k=KD), ACT.Copy).then_inc(xth, 1)

            def silu(st):
                act.wait_ge(h_mm, st.n + 1)
                if not (st.first and st.s == 0):
                    act.wait_ge(h_ready, st.n)
                act.activation(sil[:], ps[0:BR, 2 + st.s, 0:DE], ACT.Silu).then_inc(h_sig, 1)

            def y_out(st):
                act.wait_ge(y_mm, st.n + 1)
                if not st.first:
                    act.wait_ge(y_st[st.s], st.t * 16)
                act.activation(YS[st.s][:], ps[0:BR, 5:7, :].rearrange("p b n -> p (b n)"), ACT.Copy).then_inc(y_ready, 1)
                act.wait_ge(y_ready, st.n + 1)
                act.dma_start(yb[bass.ds(st.n * BR, BR), :], YS[st.s][:]).then_inc(y_st[st.s], 16)

            def h_hi(st):
                act.wait_ge(h_tp, st.n + 1)
                act.activation(HTH[:, :, 0:BR], ps[:, 4, 0:2 * BR].rearrange("p (a t) -> p a t", a=2), ACT.Copy).then_inc(hth, 1)

            x_hi(Step(0, 0))

            def expert(st):
                nxt, prev, before = st.ahead(1), st.ahead(-1), st.ahead(-2)
                more = nxt.within(NE)
                if more:
                    split1(nxt, 0)
                if prev.within(NE):
                    h_hi(prev)
                if more:
                    split1(nxt, 1)
                if before.within(NE):
                    y_out(before)
                silu(st)
                if more:
                    x_hi(nxt)
                if not (st.first and st.s == 0):
                    split2(st)
            steps(act, expert, NE, ends=True)
            h_hi(Step(NE // 2 - 1, 1))
            y_out(Step(NE // 2 - 1, 0))
            y_out(Step(NE // 2 - 1, 1))
            for s in range(2):
                act.wait_ge(y_st[s], 16 * (NE // 2))
            barrier(act, 6)
            n_more = act.value_load(eovf[0:1, NOVF:NOVF + 1], min_val=0, max_val=NOVF)
            with act.If(n_more > 0):
                with act.Fori(0, n_more) as j:
                    st = More(j)
                    split1(st, 0, lag=1)
                    split1(st, 1, lag=1)
                    split2(st, lag=1)
                    x_hi(st)
                    silu(st)
                    h_hi(st)
                    y_out(st)
                    act.wait_ge(y_st[0], (j + (1 + NE // 2)) * 16)
            barrier(act, 7)

            def norm_f(st, rows):
                act.wait_ge(c_sum, st.n + 1)
                act.activation(jf[0:rows], FS[st.s][0:rows], ACT.Square, accum_out=ss6[0:rows])
                act.drain()
                act.activation(rt6[0:rows], ss6[0:rows], ACT.Sqrt, bias=epsc[0:rows], scale=1.0 / D).then_inc(c_rms, 1)
            token_tiles(act, norm_f)
            barrier(act, 8)

        @block.vector
        def _(dve):
            dve.memset(XH[:, :, NTOK:].bitcast(F32), 0.0)
            dve.memset(XL[:, :, NTOK:].bitcast(F32), 0.0)
            dve.wait_ge(g1_in, 16)

            def normalise(n):
                s, rows = n % 2, rows_of(n)
                dve.wait_ge(rms_ready, n + 1)
                dve.reciprocal(rst[s][0:rows], rtt[s][0:rows])
                dve.drain()
                if n >= 2:
                    dve.wait_ge(xt_done, n - 1)
                dve.scalar_tensor_tensor(out=XN[s][0:rows], in0=X[s][0:rows], scalar=rst[s][0:rows], in1=g1b[0:rows],
                                         op0=ALU.mult, op1=ALU.mult).then_inc(xn_ready, 1)

            def x_low(n):
                s, rows = n % 2, rows_of(n)
                dve.wait_ge(xh_ready, n + 1)
                dve.tensor_tensor(XL[:, :, tok(n, rows)], xpos(s)[:, :, 0:rows], XH[:, :, tok(n, rows)].bitcast(F32),
                                  ALU.subtract).then_inc(xl_ready, 1)

            def low_w(col, st, all_, here):
                dve.wait_ge(wh_ready, all_.n + 1)
                dve.tensor_tensor(WL[st.s][:], RAW[st.s][:], WH[st.s][:].bitcast(F32), ALU.subtract).then_inc(wl_ready, 1)
            normalise(0)
            normalise(1)
            low_w(C_V, Step(0, 0), Step(0, 0), Step(0, 0))
            for n in range(NT):
                x_low(n)
                if n + 2 < NT:
                    normalise(n + 2)
            chunks(dve, T_TURNS, 0, but_chunk0(low_w))
            chunks(dve, F_TURNS[:1], F0, low_w)
            chunks(dve, F_TURNS[1:2], F0 + 4, low_w, F0)
            dve.wait_ge(cm_sq, 1)
            dve.tensor_reduce(vss[:], vsq.rearrange("p t (g c) -> p (t g) c", g=NCH), AX.X, ALU.add).then_inc(cm_rt, 1)
            dve.wait_ge(cm_rt, 2)
            dve.reciprocal(vss[:], vrs[:])
            dve.drain()
            v3 = vvt[:].rearrange("p t (g c) -> p (t g) c", g=NCH)
            dve.tensor_tensor(v3, v3, vss[:].rearrange("p (a b) -> p a b", b=1).to_broadcast([P, NT * NCH, P]), ALU.mult)
            dve.drain()
            dve.tensor_tensor(vvt[:], vvt[:], cmg[:].rearrange("p (a c) -> p a c", a=1).to_broadcast([P, NT, CONV_CH]), ALU.mult).then_inc(cm_v, 1)
            chunks(dve, F_TURNS[2:3], F0 + 5, low_w, F0)

            def conv(c):
                dve.wait_ge(cv_in, c * 96 + 96)
                dve.tensor_tensor(cpp[:, 2:2 + SEQ], cG[:, 0:SEQ], cH[:, 0:SEQ], ALU.mult)
                dve.tensor_tensor(cps[:, :, 2:2 + DEC_T], cG[:, SEQ:NTOK].rearrange("p (s t) -> p s t", s=DEC_B),
                                  cH[:, SEQ:NTOK].rearrange("p (s t) -> p s t", s=DEC_B), ALU.mult)
                dve.drain()
                co, cz = cout[:, SEQ:NTOK].rearrange("p (s t) -> p s t", s=DEC_B), cout[:, 0:SEQ]
                dve.tensor_scalar(cz, cpp[:, 0:SEQ], cwt[:, 0:1], None, ALU.mult)
                dve.tensor_scalar(co, cps[:, :, 0:DEC_T], cwt[:, 0:1], None, ALU.mult)
                for k in (1, 2):
                    dve.drain()
                    dve.scalar_tensor_tensor(out=cz, in0=cpp[:, k:k + SEQ], scalar=cwt[:, k:k + 1], in1=cz, op0=ALU.mult, op1=ALU.add)
                    dve.scalar_tensor_tensor(out=co, in0=cps[:, :, k:k + DEC_T], scalar=cwt[:, k:k + 1], in1=co, op0=ALU.mult, op1=ALU.add)
                dve.drain()
                dve.tensor_tensor(cout, cB, cout, ALU.mult).then_inc(cv_z, 1)

            def mlp(c):
                one = bass.ds(c, 1)
                if isinstance(c, int):
                    dve.wait_ge(cm_wc, 3)
                dve.wait_ge(cm_mm, c + 1)
                dve.tensor_tensor(zc[:, 0:SEQ].rearrange("p (n t) -> p n t", t=P), ps[:, 6:8, :].rearrange("p b (n t) -> p (b n) t", t=P),
                                  cmb[:, one, :].to_broadcast([P, NFULL, P]), ALU.add)
                dve.tensor_tensor(zc[:, SEQ:NTOK].rearrange("p (n t) -> p n t", t=DEC_T), smz[:, one, :].rearrange("p a (n t) -> p (a n) t", t=DEC_T),
                                  cmb[:, one, 0:DEC_T].to_broadcast([P, DEC_B, DEC_T]), ALU.add)
                dve.drain()
                dve.wait_ge(cm_u, c * 16 + 16)
                dve.tensor_tensor(zc[:], zc[:], uT, ALU.mult).then_inc(cm_z, 1)

            def conv_and_copy(c):
                if isinstance(c, int):
                    dve.wait_ge(cm_v, 1)
                    dve.memset(cpp[:, 0:2], 0.0)
                    dve.drain()
                conv(c)
                if not isinstance(c, int):
                    dve.wait_ge(cm_st, c * 16 + 16)
                dve.tensor_copy(zc[:, 0:SEQ].rearrange("p (n t) -> p n t", t=P), vvt[:, 0:NFULL, bass.ds(c * P, P)]).then_inc(cm_vc, 1)
            gate_chunks(dve, low_w, nothing, conv_and_copy, mlp)
            dve.wait_ge(wh_ready, NTC + NFC + 1)
            dve.tensor_tensor(WL[0][:, :, 0:P], RAW[0][:, :, 0:P], WH[0][:, :, 0:P].bitcast(F32), ALU.subtract).then_inc(wl_ready, 1)
            barrier(dve, 1)

            dve.wait_ge(g_c, 1)
            csp = cs[:, 0:SEQ].rearrange("p (c t) -> p c t", t=CHUNK)
            csd = cs[:, SEQ:NTOK].rearrange("p (c t) -> p c t", t=DEC_T)
            per = NCHUNK + DEC_B

            def decay_sums(st):
                dve.wait_ge(g_z, st.n + 1)
                dve.scalar_tensor_tensor(out=zz[:], in0=zz[:], scalar=0.0, in1=t1[:], op0=ALU.min, op1=ALU.subtract)
                dve.drain()
                dve.tensor_tensor_scan(cs[:], seg[:], zz[:], 0.0, ALU.mult, ALU.add)
                dve.drain().then_inc(g_b, 1)
                dve.tensor_tensor(zz[:, 0:SEQ].rearrange("p (c t) -> p c t", t=CHUNK), csp[:, :, CHUNK - 1:CHUNK].to_broadcast([P, NCHUNK, CHUNK]), csp, ALU.subtract)
                dve.tensor_tensor(zz[:, SEQ:NTOK].rearrange("p (c t) -> p c t", t=DEC_T), csd[:, :, DEC_T - 1:DEC_T].to_broadcast([P, DEC_B, DEC_T]), csd, ALU.subtract)
                dve.drain().then_inc(g_b, 1)

            def decayed_q(st):
                dve.wait_ge(g_pin, st.n * 32 + 32)
                dve.wait_ge(g_e, st.n + 1)
                dve.scalar_tensor_tensor(out=qt[st.s][:], in0=qT[:], scalar=float(DK) ** -0.5, in1=eb[st.s][:], op0=ALU.mult, op1=ALU.mult)
                dve.drain()

            def sample_queries(st):
                s = st.s
                for q in range(DEC_B):
                    dve.tensor_copy(qz[s][:, q, q * DEC_T:(q + 1) * DEC_T], qt[s][:, SEQ + q * DEC_T:SEQ + (q + 1) * DEC_T])
                dve.drain().then_inc(g_q, 1)

            def mask(st, j):
                b = turn_of(st, j)
                wait_alone(dve, g_ap, st.n * NT + (j + 1))
                if j < NFULL:
                    dve.copy_predicated(attm[b][:], mp[:], ps[:, 7, 0:P]).then_inc(g_am, 1)
                else:
                    dve.copy_predicated(attd[:], md[:], ps[0:NDEC, 7, 0:NDEC]).then_inc(g_am, 1)

            def state(st, c):
                dve.wait_ge(g_u, st.n * per + (c + 1))
                if c == NCHUNK - 1:
                    wait_if_any(dve, g_sv, st.n * 32)
                last = c * CHUNK + CHUNK - 1
                dve.scalar_tensor_tensor(out=S[:, c + 1, :], in0=S[:, c, :], scalar=eb[st.s][:, last:last + 1], in1=ps[:, 5 + c % 2, 0:DV],
                                         op0=ALU.mult, op1=ALU.add).then_inc(g_s, 1)
                dve.drain()

            def end_keys(st):
                dve.wait_ge(g_kc, st.n * NT + NT)
                for q in range(DEC_B):
                    dve.tensor_scalar(kz[:, q, :], ket[turn_of(st, NFULL, 3)][0:NDEC], rmask[:, q:q + 1], None, ALU.mult)
                dve.drain().then_inc(g_kz, 1)

            def state_d(st, q):
                dve.wait_ge(g_u, st.n * per + (NCHUNK + q + 1))
                last = SEQ + q * DEC_T + DEC_T - 1
                dve.scalar_tensor_tensor(out=Sn[:, q, :], in0=Sd[st.s][:, q, :], scalar=eb[st.s][:, last:last + 1], in1=ps[:, 5 + q % 2, 0:DV],
                                         op0=ALU.mult, op1=ALU.add).then_inc(g_s, 1)

            def out_norm(st, j):
                rows, b = rows_of(j), turn_of(st, j)
                dve.wait_ge(g_rt, st.n * NT + (j + 1))
                dve.reciprocal(orc[b][0:rows], ors[b][0:rows])
                dve.drain()
                if j == 0:
                    dve.wait_ge(g_rg, st.n + 1)
                wait_if_any(dve, g_tp, st.n * NT + (j - 1))
                dve.scalar_tensor_tensor(out=og[b][0:rows], in0=ps[0:rows, b, 0:DV], scalar=orc[b][0:rows], in1=rt[st.s][0:rows, j, :],
                                         op0=ALU.mult, op1=ALU.mult).then_inc(g_n, 1)

            decay_sums(Step(0, 0))
            decayed_q(Step(0, 0))
            sample_queries(Step(0, 0))

            def gla(st):
                nxt = st.ahead(1)
                more = nxt.within(HEADS)
                mask(st, 0)
                dve.wait_ge(g_in[st.s], st.t * 80 + 80)
                state(st, 0)
                state(st, 1)
                for j in range(NT):
                    if j + 1 < NT:
                        mask(st, j + 1)
                    if j + 1 < NFULL:
                        state(st, 2 * j + 2)
                        state(st, 2 * j + 3)
                    if j == NFULL - 1:
                        end_keys(st)
                    out_norm(st, j)
                    if more and j == 4:
                        decay_sums(nxt)
                    if more and j == 7:
                        decayed_q(nxt)
                        sample_queries(nxt)
                for q in range(DEC_B):
                    state_d(st, q)
            steps(dve, gla, HEADS, ends=True)
            barrier(dve, 2)

            def low_z(n):
                dve.wait_ge(z_hi, n + 1)
                dve.tensor_tensor(ZL[:, n, :], zr[n % NZ], ZH[:, n, :].bitcast(F32), ALU.subtract).then_inc(z_lo, 1)

            def low_p(st):
                dve.wait_ge(p_hi, st.n + 1)
                dve.tensor_tensor(PL[st.s][:], PR[:], PH[st.s][:].bitcast(F32), ALU.subtract).then_inc(p_lo, 1)
            low_p(Step(0, 0))
            for n in range(16):
                low_z(n)

            def gate(st):
                s, n = st.s, st.n
                wait_alone(dve, sg_in, n * 48 + 48)
                for b in range(3):
                    bank = 3 * ((s * 3 + b) % 2)
                    dve.drain()
                    dve.wait_ge(p_mm, n * 3 + (b + 1))
                    for to, frm in ((slice(0, 768), None), (slice(768, NTOK), 2)):
                        src = ps[:, bank:bank + 2, 0:384] if frm is None else ps[:, bank + 2, 0:320]
                        g = sg[:, b, to] if frm else sg[:, b, to].rearrange("p (g n) -> p g n", g=2)
                        out = ymix[s] if b == 0 else yt
                        out = out[:, to] if frm else out[:, to].rearrange("p (g n) -> p g n", g=2)
                        last = dve.tensor_tensor(out, src, g, ALU.mult)
                    last.then_inc(p_ev, 1)
                    dve.drain()
                    if b:
                        last = dve.tensor_tensor(ymix[s], ymix[s], yt[:], ALU.add)
                    if b == 0 and st.ahead(1).within(KD):
                        low_p(st.ahead(1))
                last.then_inc(mix_ready, 1)
            steps(dve, gate, KD, ends=True)
            barrier(dve, 3)

            def low_wo(i):
                k = slice(2 * i, 2 * i + 2)
                dve.wait_ge(wo_hi, i + 1)
                dve.tensor_tensor(WOL[:, k, :], WOR[:, k, :], WOH[:, k, :].bitcast(F32), ALU.subtract).then_inc(wo_lo, 1)

            def low_m(st, rows):
                dve.wait_ge(m_hi, st.n + 1)
                dve.tensor_tensor(ML[st.s][:, :, 0:rows], MR[st.s][:, :, 0:rows], MH[st.s][:, :, 0:rows].bitcast(F32), ALU.subtract).then_inc(m_lo, 1)
            low_wo(0)
            low_m(Step(0, 0), P)
            for i in range(1, 4):
                low_wo(i)
            low_m(Step(0, 1), P)
            dve.wait_ge(r4_in, 80)

            def resid(st, rows, meanwhile):
                n, s = st.n, st.s
                dve.wait_ge(o_mm, n + 1)
                if not st.first:
                    dve.wait_ge(n2_st[s], st.t * 32)
                dve.tensor_tensor(X2[s][0:rows], ps[0:rows, 2 * s:2 * s + 2, :].rearrange("p b n -> p (b n)"), X4[s][0:rows], ALU.add).then_inc(x2_ready, 1)
                dve.wait_ge(x2_rms, n + 1)
                dve.reciprocal(rs4[0:rows], rt4[0:rows])
                dve.drain()
                dve.scalar_tensor_tensor(out=N2[s][0:rows], in0=X2[s][0:rows], scalar=rs4[0:rows], in1=g2b[0:rows], op0=ALU.mult, op1=ALU.mult).then_inc(n2_ready, 1)
                meanwhile()
                if not (st.first and s == 0):
                    logit_bias(st.ahead(-1), P)

            def logit_bias(st, rows):
                n = st.n
                dve.wait_ge(l_mm, n + 1)
                dve.tensor_tensor(lgt[0:rows, bass.ds(n, 1), :].rearrange("p a c -> p (a c)"), ps[0:rows, 6, 0:GROUPS + NE], rb[0:rows], ALU.add).then_inc(l_ready, 1)

            steps(dve, lambda st: resid(st, P, lambda: low_m(st.ahead(2), P)), NFULL - 2)
            resid(Step(NFULL // 2 - 1, 0), P, lambda: low_m(Step(NFULL // 2, 0), NDEC))
            resid(Step(NFULL // 2 - 1, 1), P, lambda: None)
            resid(Step(NFULL // 2, 0), NDEC, lambda: None)
            logit_bias(Step(NFULL // 2, 0), NDEC)
            barrier(dve, 4)

            lg, lx = lgt[:, :, 0:GROUPS], lgt[:, :, GROUPS:]
            wide = [P, NT, GROUPS]
            dve.wait_ge(r_c, 1)

            def onehot(out, vals, mx, tmp, n):
                dve.tensor_tensor(tmp[:], vals, mx[:].to_broadcast([P, NT, n]), ALU.is_equal)
                dve.drain()
                dve.scalar_tensor_tensor(out=tmp[:], in0=tmp[:], scalar=-1000.0, in1=ioE[:, :, 0:n], op0=ALU.mult, op1=ALU.add)
                dve.drain()
                dve.tensor_reduce(gmn[:], tmp[:], AX.X, ALU.min)
                dve.drain()
                dve.tensor_tensor(out[:], tmp[:], gmn[:].to_broadcast([P, NT, n]), ALU.is_equal)
                dve.drain()

            dve.tensor_reduce(gmx[:], lg, AX.X, ALU.max)
            dve.drain()
            dve.tensor_tensor(gva[:], lg, gmx[:].to_broadcast(wide), ALU.subtract).then_inc(r_df, 1)
            onehot(ohg, lg, gmx, gtm, GROUPS)
            dve.tensor_scalar(gtm[:], ohg[:], -1.0, 1e30, ALU.add, ALU.mult)
            dve.drain()
            for g in range(GROUPS):
                dve.tensor_tensor(le[:, :, g * EPG:(g + 1) * EPG], lx[:, :, g * EPG:(g + 1) * EPG],
                                  gtm[:, :, g:g + 1].to_broadcast([P, NT, EPG]), ALU.add)
            dve.drain()
            for k in range(2):
                dve.tensor_reduce(v12[k][:], le[:], AX.X, ALU.max)
                dve.drain()
                onehot(oh[k], le[:], v12[k], ev, NE)
                if k == 0:
                    dve.scalar_tensor_tensor(out=le[:], in0=oh[0][:], scalar=-2e30, in1=le[:], op0=ALU.mult, op1=ALU.add)
                    dve.drain()
            dve.tensor_tensor(gd[:], v12[1][:], v12[0][:], ALU.subtract).then_inc(r_df, 1)
            dve.wait_ge(r_ex, 1)
            dve.tensor_reduce(gsm[:], gex[:], AX.X, ALU.add)
            dve.wait_ge(r_ex, 2)
            dve.tensor_scalar(gr[:], gd[:], 1.0, None, ALU.add)
            dve.drain()
            dve.tensor_tensor(gr[:], gr[:], gsm[:], ALU.mult)
            dve.drain()
            dve.reciprocal(gsm[:], gr[:])
            dve.drain()
            dve.tensor_copy(gates[:, :, 0:1], gsm[:])
            dve.tensor_tensor(gates[:, :, 1:2], gsm[:], gd[:], ALU.mult)
            dve.tensor_tensor(msk[:], oh[0][:], oh[1][:], ALU.add)
            dve.memset(cum[:, 0, :], 0.0)
            dve.drain()
            dve.memset(msk[NDEC:P, NFULL, :], 0.0)
            dve.drain()
            for t in range(1, NT):
                dve.tensor_tensor(cum[:, t, :], cum[:, t - 1, :], msk[:, t - 1, :], ALU.add)
                dve.drain()
            dve.tensor_tensor(tot[:], cum[:, NFULL, :], msk[:, NFULL, :], ALU.add)
            dve.drain().then_inc(r_msk, 1)
            dve.wait_ge(r_mm, 1)
            half = NT * NE // 2
            rf = rank[:].rearrange("p t e -> p (t e)")
            dve.tensor_copy(rf[:, 0:half], ps[:, 0, 0:half])
            dve.tensor_copy(rf[:, half:], ps[:, 1, 0:half])
            dve.tensor_copy(cnt[:], ps[:, 2, 0:NE])
            dve.drain()
            dve.tensor_copy(ranki[:], rank[:])
            dve.tensor_scalar(cnt[:], cnt[:], 1.0, -1.0, ALU.max, ALU.add)
            dve.drain()
            dve.tensor_copy(cnti[:], cnt[:])
            dve.tensor_scalar(ranki[:], ranki[:], BR_BITS, None, ALU.arith_shift_right)
            dve.drain()
            dve.tensor_scalar(cnti[:], cnti[:], BR_BITS, None, ALU.arith_shift_right)
            dve.tensor_copy(hib[:], ranki[:])
            dve.drain()
            dve.tensor_copy(ovf[:], cnti[:])
            dve.drain()
            dve.tensor_tensor_scan(ove[:], one64[:], ovf[:], 0.0, ALU.mult, ALU.add)
            dve.drain()
            dve.tensor_tensor(stw[:], ove[:], ovf[:], ALU.subtract)
            dve.drain()
            dve.tensor_tensor(stw[:], stw[:], ioE[:, 0, :], ALU.subtract)
            dve.drain()
            dve.tensor_scalar(stw[:], stw[:], float(NE - 1), None, ALU.add)
            dve.tensor_scalar(tE[:], hib[:], 0.0, None, ALU.is_gt)
            dve.drain()
            dve.tensor_tensor(tE[:], tE[:], stw[:].rearrange("p (a e) -> p a e", a=1).to_broadcast([P, NT, NE]), ALU.mult)
            dve.drain()
            dve.tensor_tensor(tE[:], tE[:], hib[:], ALU.add)
            dve.scalar_tensor_tensor(out=rank[:], in0=hib[:], scalar=-float(BR), in1=rank[:], op0=ALU.mult, op1=ALU.add)
            dve.drain()
            dve.tensor_tensor(tE[:], tE[:], ioE[:], ALU.add)
            dve.drain()
            dve.scalar_tensor_tensor(out=cum[:], in0=tE[:], scalar=float(BR), in1=rank[:], op0=ALU.mult, op1=ALU.add)
            dve.scalar_tensor_tensor(out=hib[:], in0=rank[:], scalar=float(NBLK), in1=tE[:], op0=ALU.mult, op1=ALU.add)
            dve.drain()
            for k in range(2):
                for rows, to in ((cum, dsty), (hib, dst)):
                    dve.tensor_tensor(tE[:], oh[k][:], rows[:], ALU.mult)
                    dve.drain()
                    dve.tensor_reduce(to[:, k, :], tE[:], AX.X, ALU.add)
                    dve.drain()
            dve.tensor_copy(yrow[:], dsty[:])
            for k in range(2):
                dve.memset(dst[NDEC:P, k, NFULL:NT], float(NOWHERE))
            dve.drain()
            dve.tensor_copy(dsti[:], dst[:])
            dve.drain().then_inc(r_dst, 1)
            dve.wait_ge(r_c, 2)
            dve.tensor_tensor(ovx[:], ove[0:1, :].rearrange("p (a e) -> p a e", a=1).to_broadcast([1, NOVF, NE]), ioV[:], ALU.is_le)
            dve.drain()
            dve.tensor_reduce(ovn[:, 0:NOVF], ovx[:], AX.X, ALU.add)
            dve.tensor_copy(ovn[:, NOVF:NOVF + 1], ove[0:1, NE - 1:NE])
            dve.drain()
            dve.tensor_scalar(ovn[:, 0:NOVF], ovn[:, 0:NOVF], float(NE - 1), None, ALU.min)
            dve.drain()
            dve.tensor_copy(eovf[:], ovn[:])

            def low1(st, i):
                dve.wait_ge(e1_hi, st.n * 2 + (i + 1))
                dve.tensor_tensor(E1L[st.s][:, i], E1[st.s][:, i], E1H[st.s][:, i].bitcast(F32), ALU.subtract).then_inc(e1_lo, 1)

            def low2(st):
                dve.wait_ge(e2_hi, st.n + 1)
                dve.tensor_tensor(E2L[st.s][:], E2[st.s][:], E2H[st.s][:].bitcast(F32), ALU.subtract).then_inc(e2_lo, 1)

            for b in XTH + XTL + [HTH, HTL]:
                dve.memset(b[:, :, BR:].bitcast(F32), 0.0)
            low1(Step(0, 0), 0)
            low1(Step(0, 0), 1)
            low2(Step(0, 0))
            barrier(dve, 5)

            def x_lo(st):
                dve.wait_ge(xth, st.n + 1)
                dve.tensor_tensor(XTL[st.s][:, :, 0:BR], ps[:, 0, :].rearrange("p (k t) -> p k t", k=KD), XTH[st.s][:, :, 0:BR].bitcast(F32), ALU.subtract).then_inc(xtl, 1)

            def hidden(st):
                dve.wait_ge(h_sig, st.n + 1)
                if not (st.first and st.s == 0):
                    dve.wait_ge(h_tp, st.n)
                dve.tensor_tensor(hid[:], ps[0:BR, 2 + st.s, DE:2 * DE], sil[:], ALU.mult).then_inc(h_ready, 1)

            def h_lo(st):
                dve.wait_ge(hth, st.n + 1)
                dve.tensor_tensor(HTL[:, :, 0:BR], ps[:, 4, 0:2 * BR].rearrange("p (a t) -> p a t", a=2), HTH[:, :, 0:BR].bitcast(F32), ALU.subtract).then_inc(htl, 1)
            x_lo(Step(0, 0))

            def expert(st):
                nxt, prev = st.ahead(1), st.ahead(-1)
                more = nxt.within(NE)
                if prev.within(NE) and not (prev.first and prev.s == 0):
                    low2(prev)
                if more:
                    low1(nxt, 0)
                if prev.within(NE):
                    h_lo(prev)
                if more:
                    low1(nxt, 1)
                hidden(st)
                if more:
                    x_lo(nxt)
            steps(dve, expert, NE, ends=True)
            low2(Step(NE // 2 - 1, 1))
            h_lo(Step(NE // 2 - 1, 1))
            barrier(dve, 6)
            n_more = dve.value_load(eovf[0:1, NOVF:NOVF + 1], min_val=0, max_val=NOVF)
            with dve.If(n_more > 0):
                with dve.Fori(0, n_more) as j:
                    st = More(j)
                    low1(st, 0)
                    low1(st, 1)
                    low2(st)
                    x_lo(st)
                    hidden(st)
                    h_lo(st)
            barrier(dve, 7)

            dve.wait_ge(c_g, 16)

            def combine(st, rows):
                n, s = st.n, st.s
                dve.wait_ge(c_in[s], st.t * 16 + 16)
                dve.wait_ge(cy_in[s], st.t * 32 + 32)
                dve.tensor_copy(gt6[s][:], gates[:, bass.ds(n, 1), :].rearrange("p a k -> p (a k)"))
                dve.drain()
                if not st.first:
                    dve.wait_ge(c_out, n - 1)
                dve.scalar_tensor_tensor(out=FS[s][0:rows], in0=FY[s][0:rows, 0, :], scalar=gt6[s][0:rows, 0:1], in1=FX[s][0:rows], op0=ALU.mult, op1=ALU.add)
                dve.drain()
                dve.scalar_tensor_tensor(out=FS[s][0:rows], in0=FY[s][0:rows, 1, :], scalar=gt6[s][0:rows, 1:2], in1=FS[s][0:rows], op0=ALU.mult, op1=ALU.add)
                dve.drain().then_inc(c_sum, 1)
                dve.wait_ge(c_rms, n + 1)
                dve.reciprocal(rs6[0:rows], rt6[0:rows])
                dve.drain()
                if not st.first:
                    dve.wait_ge(c_st[s], st.t * 16)
                dve.scalar_tensor_tensor(out=FO[s][0:rows], in0=FS[s][0:rows], scalar=rs6[0:rows], in1=gfb[0:rows], op0=ALU.mult, op1=ALU.mult).then_inc(c_out, 1)
            token_tiles(dve, combine)
            barrier(dve, 8)

        @block.tensor
        def _(pe):
            pe.wait_ge(s_const, 1)

            def x_transpose(n):
                s, rows = n % 2, rows_of(n)
                pe.wait_ge(xn_ready, n + 1)
                for k in range(KD):
                    last = pe.transpose(xpos(s)[:, k, 0:rows], XN[s][0:rows, k * P:(k + 1) * P], ident[0:rows, 0:rows])
                last.then_inc(xt_done, 1)

            def three(out, hi, lo, mhi, mlo, start, stop):
                pe.matmul(out, hi, mhi, start=start, stop=False)
                pe.matmul(out, hi, mlo, start=False, stop=False)
                return pe.matmul(out, lo, mhi, start=False, stop=stop)

            def t_product(all_, tile):
                s = all_.s
                if not (all_.first and s * NT + tile < 3):
                    pe.wait_ge(t_ev, all_.n * NT + tile - 2)
                cols = slice(tile * P, tile * P + P)
                for k in range(KD):
                    last = three(ps[:, tile % 3, 0:CW], XH[:, k, cols], XL[:, k, cols], WH[s][:, k, :], WL[s][:, k, :],
                                 k == 0, k == KD - 1)
                last.then_inc(t_mm, 1)

            def t_chunk(col, st, all_, here):
                pe.wait_ge(wl_ready, all_.n + 1)
                for tile in range(NT):
                    t_product(all_, tile)
                pe.drain().then_inc(w_used, 1)

            x_transpose(0)
            x_transpose(1)
            pe.wait_ge(wl_ready, 1)
            for n in range(NT):
                pe.wait_ge(xl_ready, n + 1)
                if n + 2 < NT:
                    x_transpose(n + 2)
                t_product(Step(0, 0), n)
            pe.drain().then_inc(w_used, 1)
            chunks(pe, T_TURNS, 0, but_chunk0(t_chunk))

            def feature(f, wh, wl, nk, xh, xl):
                for k in range(nk):
                    for i, (w, x) in enumerate(((wh, xh), (wh, xl), (wl, xh))):
                        for g, (t0, tn) in enumerate(TG):
                            last = pe.matmul(ps[:, 3 * f + g, 0:tn], w[:, k, :], x[:, k, t0:t0 + tn],
                                             start=(k == 0 and i == 0), stop=(k == nk - 1 and i == 2))
                return last

            def f_chunk(col, st, all_, here):
                s = st.s
                pe.wait_ge(wl_ready, all_.n + 1)
                for f in range(2):
                    if here.first and here.s == 0:
                        pe.wait_ge(t_ev, NTC * NT)
                    else:
                        pe.wait_ge(f_ev, here.n * 2 + (f - 1))
                    last = feature(f, WH[s][:, :, f * P:(f + 1) * P], WL[s][:, :, f * P:(f + 1) * P], KD, XH, XL)
                    last.then_inc(f_mm, 1)
                pe.drain().then_inc(w_used, 1)
            chunks(pe, F_TURNS[:1], F0, f_chunk)
            pe.wait_ge(cm_wd0, 4)
            for g in range(NCH):
                pe.transpose(ps[:, 6, g * P:(g + 1) * P], wsn[:, g, :], ident[:])
            for g in range(NCH):
                last = pe.transpose(ps[:, 7, g * NDEC:(g + 1) * NDEC], wsd[:, g, :], ident[0:NDEC, 0:NDEC])
            last.then_inc(cm_wt, 1)
            chunks(pe, F_TURNS[1:3], F0 + 4, f_chunk, F0)
            pe.wait_ge(cm_v, 1)
            pe.wait_ge(cm_wc, 2)
            for g in range(NCH):
                last = pe.matmul(ps[:, 6, g * NDEC:(g + 1) * NDEC], vvt[0:NDEC, NFULL, g * P:(g + 1) * P], wsdT[:, g, :], start=True, stop=True)
            last.then_inc(cm_wt, 1)
            pe.wait_ge(cm_wc, 3)

            def mix(c):
                pe.wait_ge(cm_vc, c + 1)
                for t in range(NFULL):
                    last = pe.matmul(ps[:, 6 + t // 4, (t % 4) * P:(t % 4 + 1) * P], zc[:, t * P:(t + 1) * P],
                                     wsT[:, bass.ds(c, 1), :].rearrange("p a t -> p (a t)"), start=True, stop=True)
                last.then_inc(cm_mm, 1)
            gate_chunks(pe, f_chunk, mix, nothing, nothing)
            pe.wait_ge(wl_ready, NTC + NFC + 1)
            pe.wait_ge(f_ev, 2 * NFC - 1)
            feature(0, WH[0][:, :, 0:P], WL[0][:, :, 0:P], KD, XH, XL).then_inc(a_mm, 1)
            barrier(pe, 1)

            per = NCHUNK + DEC_B

            def decay_mm(st, g):
                n, (t0, tn) = st.n, TG[g]
                pe.wait_ge(g_din, n * 32 + 32)
                wait_if_any(pe, g_zc, n * 3 + g)
                pe.matmul(ps[:, 2, 0:tn], a2h[:], alr[:, t0:t0 + tn], start=True, stop=True).then_inc(g_a, 1)

            def k_transpose(st, j):
                rows = rows_of(j)
                if st.n or j:
                    wait_alone(pe, g_kc, st.n * NT + j)
                pe.transpose(ps[0:rows, 3, 0:P], ke[st.s][:, j * P:j * P + rows], ident[:]).then_inc(g_kp, 1)

            def scores(st, j):
                rows = rows_of(j)
                wait_if_any(pe, g_am, st.n * NT + j)
                cols = slice(j * P, j * P + rows)
                pe.matmul(ps[0:rows, 7, 0:rows], kt[st.s][:, cols], qt[st.s][:, cols], start=True, stop=True).then_inc(g_ap, 1)

            def update(st, j):
                b = turn_of(st, j, 3)
                pe.wait_ge(g_kc, st.n * NT + (j + 1))
                for c in (2 * j, 2 * j + 1):
                    lo = (c % 2) * CHUNK
                    wait_if_any(pe, g_s, st.n * per + (c - 1))
                    pe.matmul(ps[:, 5 + c % 2, 0:DV], ket[b][lo:lo + CHUNK, :], vt[st.s][lo:lo + CHUNK, j, :], start=True, stop=True).then_inc(g_u, 1)

            def out_mm_b(st, j):
                s, b = st.s, turn_of(st, j)
                wait_if_any(pe, g_n, st.n * NT + (j - 1))
                wait_alone(pe, g_am, st.n * NT + (j + 1))
                if j < NFULL:
                    pe.wait_ge(g_s, st.n * per + (2 * j + 1))
                    pe.matmul(ps[:, b, 0:DV], attm[b][:], vt[s][:, j, :], start=True, stop=False)
                    pe.matmul(ps[0:CHUNK, b, 0:DV], qt[s][:, j * P:j * P + CHUNK], S[:, 2 * j, :], start=False, stop=True)
                    pe.matmul(ps[CHUNK:P, b, 0:DV], qt[s][:, j * P + CHUNK:(j + 1) * P], S[:, 2 * j + 1, :], start=False, stop=True).then_inc(g_o, 1)
                else:
                    pe.matmul(ps[0:NDEC, b, 0:DV], attd[:], vt[s][0:NDEC, j, :], start=True, stop=False)
                    for q in range(DEC_B):
                        last = pe.matmul(ps[0:NDEC, b, 0:DV], qz[s][:, q, :], Sd[s][:, q, :], start=False, stop=(q == DEC_B - 1))
                    last.then_inc(g_o, 1)

            def update_d(st):
                pe.wait_ge(g_kz, st.n + 1)
                for q in range(DEC_B):
                    pe.wait_ge(g_s, st.n * per + (NCHUNK + q - 1))
                    pe.matmul(ps[:, 5 + q % 2, 0:DV], kz[:, q, :], vt[st.s][0:NDEC, NFULL, :], start=True, stop=True).then_inc(g_u, 1)

            def out_transpose(st, j):
                rows, b = rows_of(j), turn_of(st, j)
                wait_if_any(pe, g_tc, st.n * NT + j)
                wait_alone(pe, g_n, st.n * NT + (j + 1))
                for a in range(2):
                    last = pe.transpose(ps[:, 4, a * P:a * P + rows], og[b][0:rows, a * P:(a + 1) * P], ident[0:rows, 0:rows])
                last.then_inc(g_tp, 1)

            for g in range(3):
                decay_mm(Step(0, 0), g)

            def gla(st):
                nxt = st.ahead(1)
                more = nxt.within(HEADS)
                pe.wait_ge(g_q, st.n * 2 + 2)
                k_transpose(st, 0)
                scores(st, 0)
                k_transpose(st, 1)
                pe.wait_ge(g_in[st.s], st.t * 80 + 80)
                update(st, 0)
                for j in range(NT):
                    if j + 2 < NT:
                        k_transpose(st, j + 2)
                    if j + 1 < NT:
                        scores(st, j + 1)
                    if more and 1 <= j < 4:
                        decay_mm(nxt, j - 1)
                    if j + 1 < NFULL:
                        update(st, j + 1)
                    out_mm_b(st, j)
                    if j:
                        out_transpose(st, j - 1)
                update_d(st)
                out_transpose(st, NT - 1)
            steps(pe, gla, HEADS, ends=True)
            barrier(pe, 2)

            def project(st):
                s, n = st.s, st.n
                pe.wait_ge(p_lo, n + 1)
                for b, (k0, kn) in enumerate(((0, 4), (4, 8), (12, 4))):
                    if st.first and s == 0:
                        pe.wait_ge(z_lo, k0 + kn)
                    if not (st.first and s == 0 and b < 2):
                        pe.wait_ge(p_ev, n * 3 + (b - 1))
                    f = (s * 3 + b) % 2
                    feature(f, PH[s][:, k0:k0 + kn, :], PL[s][:, k0:k0 + kn, :], kn, ZH[:, k0:k0 + kn, :], ZL[:, k0:k0 + kn, :]).then_inc(p_mm, 1)
            steps(pe, project, KD)
            barrier(pe, 3)

            def out_mm(st, rows):
                n, s = st.n, st.s
                pe.wait_ge(m_lo, n + 1)
                if not st.first:
                    pe.wait_ge(x2_ready, n - 1)
                for b in range(2):
                    for k in range(KD):
                        c = slice(b * 512, (b + 1) * 512)
                        if st.first and s == 0 and b == 0 and k % 2 == 0:
                            pe.wait_ge(wo_lo, k // 2 + 1)
                        last = three(ps[:, 2 * s + b, :], MH[s][:, k, :], ML[s][:, k, :], WOH[:, k, c], WOL[:, k, c], k == 0, k == KD - 1)
                last.then_inc(o_mm, 1)

            def router(st, rows):
                n, s = st.n, st.s
                pe.wait_ge(n2_ready, n + 1)
                if not (st.first and s == 0):
                    pe.wait_ge(n2_tc, n)
                tp = ps[:, 4:6, :].rearrange("p b (k t) -> p (b k) t", k=4)
                for k in range(KD):
                    last = pe.transpose(tp[:, k, 0:rows], N2[s][0:rows, k * P:(k + 1) * P], ident[0:rows, 0:rows])
                last.then_inc(n2_tp, 1)

            def logits(st, rows):
                n, s = st.n, st.s
                pe.wait_ge(n2_tc, n + 1)
                if not (st.first and s == 0):
                    pe.wait_ge(l_ready, n)
                for k in range(KD):
                    last = pe.matmul(ps[0:rows, 6, 0:GROUPS + NE], NTt[:, k, 0:rows], wr[:, k, :], start=(k == 0), stop=(k == KD - 1))
                last.then_inc(l_mm, 1)
            out_mm(Step(0, 0), P)
            pe.wait_ge(r4_in, 80)

            def out_tile(st):
                out_mm(st.ahead(1), P)
                if not (st.first and st.s == 0):
                    logits(st.ahead(-1), P)
                router(st, P)
            steps(pe, out_tile, NFULL - 2)
            last4 = Step(NFULL // 2 - 1, 0)
            out_tile(last4)
            out_mm(Step(NFULL // 2, 0), NDEC)
            logits(last4, P)
            router(last4.ahead(1), P)
            logits(last4.ahead(1), P)
            router(Step(NFULL // 2, 0), NDEC)
            logits(Step(NFULL // 2, 0), NDEC)
            barrier(pe, 4)

            pe.wait_ge(r_c, 1)
            pe.wait_ge(r_msk, 1)
            half = NT * NE // 2
            mflat, cflat = msk[:].rearrange("p t e -> p (t e)"), cum[:].rearrange("p t e -> p (t e)")
            for b in range(2):
                c = slice(b * half, (b + 1) * half)
                pe.matmul(ps[:, b, 0:half], ltri[:], mflat[:, c], start=True, stop=False)
                pe.matmul(ps[:, b, 0:half], onesm[:], cflat[:, c], start=False, stop=True)
            pe.matmul(ps[:, 2, 0:NE], onesm[:], tot[:], start=True, stop=True).then_inc(r_mm, 1)
            barrier(pe, 5)

            xgp = ps[:, 0, :].rearrange("p (k t) -> p k t", k=KD)

            def x_t(st):
                n, s = st.n, st.s
                if not (st.first and s == 0):
                    pe.wait_ge(xtl, n)
                wait_alone(pe, xg_in[s], st.t * 16 + 16)
                xg = XG[s][:].rearrange("p (q k) -> p k q", k=KD)
                for k in range(KD):
                    last = pe.transpose(xgp[:, k, :], xg[:, k, :], ident[0:BR, 0:BR])
                last.then_inc(xg_tp, 1)

            def h_mul(st):
                n, s = st.n, st.s
                pe.wait_ge(xtl, n + 1)
                pe.wait_ge(e1_lo, n * 2 + 2)
                if not st.first:
                    pe.wait_ge(h_ready, n - 1)
                for k in range(KD):
                    last = three(ps[:, 2 + s, :], XTH[s][:, k, :], XTL[s][:, k, :], E1H[s][:, :, k, :], E1L[s][:, :, k, :], k == 0, k == KD - 1)
                last.then_inc(h_mm, 1)

            def h_t(st):
                n = st.n
                if not (st.first and st.s == 0):
                    pe.wait_ge(htl, n)
                wait_alone(pe, h_ready, n + 1)
                hv = hid[:].rearrange("p (q k) -> p k q", k=2)
                for k in range(2):
                    last = pe.transpose(ps[:, 4, k * BR:(k + 1) * BR], hv[:, k, :], ident[0:BR, 0:BR])
                last.then_inc(h_tp, 1)

            def y_mul(st):
                n, s = st.n, st.s
                pe.wait_ge(htl, n + 1)
                pe.wait_ge(e2_lo, n + 1)
                if not (st.first and s == 0):
                    pe.wait_ge(y_ready, n)
                for b in range(2):
                    for k in range(2):
                        c = slice(b * 512, (b + 1) * 512)
                        last = three(ps[:, 5 + b, :], HTH[:, k, :], HTL[:, k, :], E2H[s][:, k, c], E2L[s][:, k, c], k == 0, k == 1)
                last.then_inc(y_mm, 1)
            x_t(Step(0, 0))

            def expert(st):
                h_mul(st)
                if st.ahead(1).within(NE):
                    x_t(st.ahead(1))
                if st.ahead(-1).within(NE):
                    y_mul(st.ahead(-1))
                h_t(st)
            steps(pe, expert, NE, ends=True)
            y_mul(Step(NE // 2 - 1, 1))
            barrier(pe, 6)
            n_more = pe.value_load(eovf[0:1, NOVF:NOVF + 1], min_val=0, max_val=NOVF)
            with pe.If(n_more > 0):
                with pe.Fori(0, n_more) as j:
                    st = More(j)
                    x_t(st)
                    h_mul(st)
                    h_t(st)
                    y_mul(st)
            barrier(pe, 7)
            barrier(pe, 8)


_INS = ['x_prompt', 'x_sample', 'state_conv', 'state_gla', 'norm1_g', 'w_in', 'conv_w', 'gla_a2', 'gla_a_b',
        'gla_norm_g', 'cm_norm_g', 'cm_ws', 'cm_b', 'proj_a', 'proj_b', 'proj_c', 'w_out', 'norm2_g',
        'router_group_w', 'router_group_b', 'router_expert_w', 'router_expert_b',
        'exp_w1', 'exp_w3', 'exp_w2', 'final_norm_g']
_OUTS = [(1, SEQ, D), (DEC_B, DEC_T, D), (1, 1, 2, CONV_CH), (1, 1, HEADS, DK, DV),
         (1, DEC_B, 2, CONV_CH), (1, DEC_B, HEADS, DK, DV), (1, DEC_B, DEC_T, CONV_CH)]


def kernel(**inputs):
    import numpy as _np
    import concourse.bacc as _bacc
    from concourse import mybir as _mybir
    from concourse.bass_utils import run_bass_kernel_spmd as _run

    nc = _bacc.Bacc("TRN2", target_bir_lowering=False, num_devices=1)
    arrays, args = {}, []
    for name in _INS:
        a = _np.ascontiguousarray(inputs[name])
        arrays[f"in_{name}_dram"] = a
        args.append(nc.dram_tensor(f"in_{name}_dram", a.shape, _mybir.dt.from_np(a.dtype), kind="ExternalInput").ap())
    for i, shape in enumerate(_OUTS):
        args.append(nc.dram_tensor(f"out_{i}_dram", shape, _mybir.dt.float32, kind="ExternalOutput").ap())
    trunk(nc, *args)
    r = _run(nc, [arrays], core_ids=[0])
    return tuple(r.results[0][f"out_{i}_dram"] for i in range(len(_OUTS)))
```
